# Optimizing a Trainium2 kernel written in Bass

```python
import jax, jax.numpy as jnp
from jax import lax
import numpy as np

D_MODEL = 1024
BATCH = 1
SEQ = 512
DEPTH = 2

PLE_DIM = 256
FOX_HEADS = 8
FOX_HEAD_DIM = 64
FOX_WIDTH = FOX_HEADS * FOX_HEAD_DIM
HG_HEADS = 4
HG_KEY_DIM = 128
HG_VAL_DIM = 128
HG_WIDTH = HG_HEADS * HG_VAL_DIM
MIX_WIDTH = FOX_WIDTH + HG_WIDTH
IN_COLS = 3 * FOX_WIDTH + FOX_HEADS + 4 * HG_WIDTH
QUERY_BLOCK = 128
HG_CHUNK = 32
PEER_HEADS = 8
PEER_N_KEYS = 128
PEER_N_EXPERTS = PEER_N_KEYS * PEER_N_KEYS
PEER_QUERY_DIM = 256
PEER_HALF_DIM = PEER_QUERY_DIM // 2
PEER_TOPK = 16
PEER_TOKEN_BLOCK = 128
DEEPNORM_ALPHA = (2 * DEPTH) ** 0.25
DEEPNORM_BETA = (8 * DEPTH) ** -0.25
LN_EPS = 1e-5
RMS_EPS = 1e-6
MASK_VALUE = -1e30
LB_FLOOR = 1e-30

kernel_name = 'hybrid_fox_hgrn2_peer_deepnorm'

def layer_norm(x, g, b):
    xf = x.astype(jnp.float32)
    mu = xf.mean(-1, keepdims=True)
    var = jnp.square(xf - mu).mean(-1, keepdims=True)
    return ((xf - mu) * lax.rsqrt(var + LN_EPS) * g + b).astype(x.dtype)

def rms_norm(x, g):
    xf = x.astype(jnp.float32)
    return (xf * lax.rsqrt(jnp.square(xf).mean(-1, keepdims=True) + RMS_EPS) * g).astype(x.dtype)

def fox_attention(q, k, v, log_f):
    T = q.shape[1]
    c = jnp.cumsum(log_f, axis=1).transpose(0, 2, 1)
    scale = FOX_HEAD_DIM ** -0.5
    outs = []
    for blk in range(T // QUERY_BLOCK):
        q0 = blk * QUERY_BLOCK
        q1 = q0 + QUERY_BLOCK
        s = jnp.einsum('bqhd,bkhd->bhqk', q[:, q0:q1], k[:, :q1]).astype(jnp.float32) * scale
        s = s + c[:, :, q0:q1, None] - c[:, :, None, :q1]
        mask = jnp.arange(q1)[None, :] <= jnp.arange(q0, q1)[:, None]
        pr = jax.nn.softmax(jnp.where(mask, s, MASK_VALUE), axis=-1)
        outs.append(jnp.einsum('bhqk,bkhd->bqhd', pr.astype(v.dtype), v[:, :q1]))
    return jnp.concatenate(outs, axis=1)

def hgrn2_chunkwise(q, k, log_f, v):
    B, T, H, dk = q.shape
    dv = v.shape[-1]
    n_chunks = T // HG_CHUNK

    def to_chunks(a):
        return a.reshape(B, n_chunks, HG_CHUNK, H, a.shape[-1]).transpose(1, 0, 3, 2, 4)

    causal = jnp.tril(jnp.ones((HG_CHUNK, HG_CHUNK), dtype=bool))

    def step(S, inp):
        qc, kc, lfc, vc = inp
        b = jnp.cumsum(lfc, axis=2)
        o_inter = jnp.einsum('bhtk,bhkv->bhtv', qc * jnp.exp(b), S)
        diff = b[:, :, :, None, :] - b[:, :, None, :, :]
        decay = jnp.exp(jnp.where(causal[:, :, None], diff, MASK_VALUE))
        A = jnp.einsum('bhtk,bhsk,bhtsk->bhts', qc, kc, decay)
        o_intra = jnp.einsum('bhts,bhsv->bhtv', A, vc)
        b_last = b[:, :, -1:, :]
        S_new = jnp.exp(b_last[:, :, 0, :, None]) * S + jnp.einsum('bhsk,bhsv->bhkv', kc * jnp.exp(b_last - b), vc)
        return S_new, o_inter + o_intra

    S0 = jnp.zeros((B, H, dk, dv), jnp.float32)
    _, o = lax.scan(step, S0, (to_chunks(q), to_chunks(k), to_chunks(log_f), to_chunks(v)))
    return o.transpose(1, 0, 3, 2, 4).reshape(B, T, H, dv)

def hybrid_mixer(h, w_in, fox_fb, fox_norm_g, lower_bound, hg_norm_g, w_out):
    B, T, _ = h.shape
    proj = h @ w_in
    split_at = [int(s) for s in np.cumsum([FOX_WIDTH, FOX_WIDTH, FOX_WIDTH, FOX_HEADS, HG_WIDTH, HG_WIDTH, HG_WIDTH])]
    fq, fk, fv, ff, hq, hf, hi, hg = jnp.split(proj, split_at, axis=-1)
    fq = fq.reshape(B, T, FOX_HEADS, FOX_HEAD_DIM)
    fk = fk.reshape(B, T, FOX_HEADS, FOX_HEAD_DIM)
    fv = fv.reshape(B, T, FOX_HEADS, FOX_HEAD_DIM)
    log_f_fox = jax.nn.log_sigmoid((ff + fox_fb).astype(jnp.float32))
    fox_o = fox_attention(fq, fk, fv, log_f_fox).reshape(B, T, FOX_WIDTH)
    fox_o = rms_norm(fox_o, fox_norm_g)
    z = hf.astype(jnp.float32).reshape(B, T, HG_HEADS, HG_KEY_DIM)
    lb = lower_bound.reshape(HG_HEADS, HG_KEY_DIM)
    log_f_hg = jnp.logaddexp(jnp.log(jnp.maximum(lb, LB_FLOOR)), jnp.log1p(-lb) + jax.nn.log_sigmoid(z))
    k_hg = (1.0 - lb) * jax.nn.sigmoid(-z)
    o_hg = hgrn2_chunkwise(hq.astype(jnp.float32).reshape(B, T, HG_HEADS, HG_KEY_DIM), k_hg, log_f_hg,
                           hi.astype(jnp.float32).reshape(B, T, HG_HEADS, HG_VAL_DIM))
    o_hg = rms_norm(o_hg, hg_norm_g.reshape(HG_HEADS, HG_VAL_DIM)).reshape(B, T, HG_WIDTH)
    o_hg = (o_hg * jax.nn.silu(hg.astype(jnp.float32))).astype(h.dtype)
    return jnp.concatenate([fox_o, o_hg], axis=-1) @ w_out

def peer_ffn(h, wq, keys, u, v):
    B, T, D = h.shape
    xt = h.reshape(-1, PEER_TOKEN_BLOCK, D)

    def block(xb):
        q = (xb @ wq).reshape(PEER_TOKEN_BLOCK, PEER_HEADS, 2, PEER_HALF_DIM)
        s = jnp.einsum('thpd,hpnd->thpn', q, keys).astype(jnp.float32)
        s1, i1 = lax.top_k(s[:, :, 0], PEER_TOPK)
        s2, i2 = lax.top_k(s[:, :, 1], PEER_TOPK)
        cand_s = (s1[..., :, None] + s2[..., None, :]).reshape(PEER_TOKEN_BLOCK, PEER_HEADS, PEER_TOPK * PEER_TOPK)
        cand_i = (i1[..., :, None] * PEER_N_KEYS + i2[..., None, :]).reshape(PEER_TOKEN_BLOCK, PEER_HEADS, PEER_TOPK * PEER_TOPK)
        top_s, pos = lax.top_k(cand_s, PEER_TOPK)
        idx = jnp.take_along_axis(cand_i, pos, axis=-1)
        gate = jax.nn.softmax(top_s, axis=-1)
        act = jax.nn.gelu(jnp.einsum('thkd,td->thk', u[idx], xb).astype(jnp.float32), approximate=False)
        return jnp.einsum('thk,thkd->td', (gate * act).astype(xb.dtype), v[idx])

    return lax.map(block, xt).reshape(B, T, D)

def setup_inputs(seed: int = 0) -> dict:
    key = jax.random.key(seed)
    ks = jax.random.split(key, 24)

    def nrm(k, shape, std):
        return std * jax.random.normal(k, shape, jnp.float32)

    beta = DEEPNORM_BETA
    col_scale = jnp.concatenate([
        jnp.ones((2 * FOX_WIDTH,), jnp.float32),
        jnp.full((FOX_WIDTH,), beta, jnp.float32),
        jnp.ones((FOX_HEADS + 2 * HG_WIDTH,), jnp.float32),
        jnp.full((HG_WIDTH,), beta, jnp.float32),
        jnp.ones((HG_WIDTH,), jnp.float32)])
    return {
        'x': nrm(ks[0], (BATCH, SEQ, D_MODEL), 1.0),
        'p': nrm(ks[1], (DEPTH, BATCH, SEQ, PLE_DIM), 1.0),
        'emb_ln_g': 1.0 + nrm(ks[2], (D_MODEL,), 0.02),
        'emb_ln_b': nrm(ks[3], (D_MODEL,), 0.02),
        'w_in': nrm(ks[4], (DEPTH, D_MODEL, IN_COLS), D_MODEL ** -0.5) * col_scale,
        'fox_fb': 1.0 + nrm(ks[5], (DEPTH, FOX_HEADS), 0.5),
        'fox_norm_g': 1.0 + nrm(ks[6], (DEPTH, FOX_WIDTH), 0.02),
        'hg_lb_logits': nrm(ks[7], (DEPTH, HG_HEADS * HG_KEY_DIM), 0.5),
        'hg_norm_g': 1.0 + nrm(ks[8], (DEPTH, HG_WIDTH), 0.02),
        'w_out': nrm(ks[9], (DEPTH, MIX_WIDTH, D_MODEL), beta * MIX_WIDTH ** -0.5),
        'ln1_g': 1.0 + nrm(ks[10], (DEPTH, D_MODEL), 0.02),
        'ln1_b': nrm(ks[11], (DEPTH, D_MODEL), 0.02),
        'peer_wq': nrm(ks[12], (DEPTH, D_MODEL, PEER_HEADS * PEER_QUERY_DIM), D_MODEL ** -0.5),
        'peer_keys': nrm(ks[13], (DEPTH, PEER_HEADS, 2, PEER_N_KEYS, PEER_HALF_DIM), PEER_HALF_DIM ** -0.5),
        'peer_u': nrm(ks[14], (DEPTH, PEER_N_EXPERTS, D_MODEL), D_MODEL ** -0.5),
        'peer_v': nrm(ks[15], (DEPTH, PEER_N_EXPERTS, D_MODEL), beta * PEER_HEADS ** -0.5),
        'ple_gate_w': nrm(ks[16], (DEPTH, D_MODEL, D_MODEL), D_MODEL ** -0.5),
        'ple_w': nrm(ks[17], (DEPTH, PLE_DIM, D_MODEL), beta * PLE_DIM ** -0.5),
        'ln2_g': 1.0 + nrm(ks[18], (DEPTH, D_MODEL), 0.02),
        'ln2_b': nrm(ks[19], (DEPTH, D_MODEL), 0.02),
    }

def reference(x, p, emb_ln_g, emb_ln_b, w_in, fox_fb, fox_norm_g, hg_lb_logits, hg_norm_g, w_out,
              ln1_g, ln1_b, peer_wq, peer_keys, peer_u, peer_v, ple_gate_w, ple_w, ln2_g, ln2_b):
    lb_probs = jax.nn.softmax(hg_lb_logits.astype(jnp.float32), axis=0)
    lower_bounds = jnp.cumsum(lb_probs, axis=0) - lb_probs[:1]
    h = layer_norm(x, emb_ln_g, emb_ln_b)
    for i in range(DEPTH):
        mix = hybrid_mixer(h, w_in[i], fox_fb[i], fox_norm_g[i], lower_bounds[i], hg_norm_g[i], w_out[i])
        h = layer_norm(DEEPNORM_ALPHA * h + mix, ln1_g[i], ln1_b[i])
        ffn = peer_ffn(h, peer_wq[i], peer_keys[i], peer_u[i], peer_v[i])
        ple = jax.nn.sigmoid(h @ ple_gate_w[i]) * (p[i] @ ple_w[i])
        h = layer_norm(DEEPNORM_ALPHA * h + ffn + ple, ln2_g[i], ln2_b[i])
    return h


_drawn_inputs = setup_inputs


def setup_inputs(seed=0):
    import zlib

    import numpy as np

    out = dict(_drawn_inputs(seed))
    spreads = {}
    factors = {'fox_norm_g': 5.213, 'hg_norm_g': 7.826}
    for name, (base, spread) in spreads.items():
        noise = np.random.default_rng([zlib.crc32(name.encode()), seed]).standard_normal(out[name].shape)
        drawn = base * np.exp(spread * noise) if base else spread * noise
        out[name] = __import__('jax').numpy.asarray(drawn.astype(out[name].dtype))
    for name, factor in factors.items():
        out[name] = (out[name] * factor).astype(out[name].dtype)
    return out
```

```python
from contextlib import ExitStack

import concourse.bass as bass
from concourse import mybir

P = 128
T = 512
D = 1024
NT = T // P
NC = D // P
FH, FD = 8, 64
FW = FH * FD
HH, HD = 4, 128
HW = HH * HD
IN_COLS = 3 * FW + FH + 4 * HW
PH, NK, TOPK = 8, 128, 16
NE = NK * NK
SLOTS = PH * TOPK
PLE = 256
BANKS = 8
PANEL = 512
RING = 8
LEVELS = 8
STAIR = [TOPK // (a + 1) for a in range(TOPK)]
CAND = sum(STAIR)
LN_EPS, RMS_EPS, LB_FLOOR, MASK = 1e-5, 1e-6, 1e-30, -1e30
LN_SPLIT = 2.0 ** 60

ALU = mybir.AluOpType
ACT = mybir.ActivationFunctionType
F32 = mybir.dt.float32
BF16 = mybir.dt.bfloat16
U32 = mybir.dt.uint32
AX_X = mybir.AxisListType.X


class Signal:

    def __init__(self, sem, per_layer, before=0):
        self.sem, self.per_layer, self.before, self.made = sem, per_layer, before, 0


def build(nc, x, pT, emb_g, emb_b, w_in, fox_fb, fox_g, lbl, hg_g, w_out, ln1_g, ln1_b,
          wq, keysT, u, v, gate_w, ple_w, ln2_g, ln2_b, consts, out):
    DEPTH = w_in.shape[0]
    ALPHA = (2 * DEPTH) ** 0.25
    SCALE = FD ** -0.5
    u_rows = u.rearrange("l e d -> (l e) d")
    v_rows = v.rearrange("l e d -> (l e) d")

    c0 = 3 * FW + FH
    PANELS = [(w_in, c0 + HW), (w_in, c0), (w_in, 0), (w_in, FW), (w_in, 2 * FW),
              (w_in, c0 + 2 * HW), (w_in, c0 + 3 * HW),
              (w_out, 0), (w_out, PANEL)] + [(wq, PANEL * j) for j in range(4)] + \
             [(gate_w, 0), (gate_w, PANEL), (ple_w, None)]

    with ExitStack() as ctx:
        def sb(name, shape, dt=F32):
            return ctx.enter_context(nc.sbuf_tensor(name, shape, dt))

        names = []

        def sig(name, per_layer, before=0):
            s = Signal(ctx.enter_context(nc.semaphore(name)), per_layer, before)
            names.append((name, s))
            return s

        ps = ctx.enter_context(nc.psum_tensor("ps", [P, BANKS, 512], F32))

        h = sb("h", [P, NT, D])
        hT = sb("hT", [P, NC, T])
        panel = sb("panel", [P, 2, NC, PANEL])
        wff = sb("wff", [P, NC, FH])
        lng = sb("lng", [P, 2, D])
        ng = sb("ng", [P, 2, 512])
        pTs = sb("pTs", [P, 2, T])
        cst = sb("cst", [P, consts.shape[1]])
        cb = sb("cb", [P, 2 * P], BF16)
        arena = sb("arena", [P, 25600])
        work = sb("work", [P, 2048])
        negc = sb("negc", [FH, T])
        ff_bias = sb("ff_bias", [FH, 1])
        stat = sb("stat", [P, NT, 12])
        mv = sb("mv", [P, NT, 2])
        rstd = sb("rstd", [P, NT])

        ident = cst[:, 0:128]
        cmask = cst[:, 128:256]
        iota = cst[:, 256:320]
        level_mask = cst[:, 320:320 + LEVELS * P]
        reset = cst[:, 1344:1344 + T]
        ident_b, cmask_b = cb[:, 0:128], cb[:, 128:256]

        def part(at, *shape):
            n = 1
            for s in shape:
                n *= s
            ap = arena[:, at:at + n]
            if len(shape) == 2:
                return ap.rearrange("p (a b) -> p a b", b=shape[1])
            if len(shape) == 3:
                return ap.rearrange("p (a b c) -> p a b c", b=shape[1], c=shape[2])
            return ap

        fqT = part(0, 4, T)
        fkT = part(2048, 4, T)
        fv = part(4096, NT, FW)
        QE = part(0, LEVELS - 1, T)
        KE = part(3584, LEVELS - 1, T)
        gt = [part(2048 * j, HH, T) for j in range(3)]
        hqT = part(7168, HH, T)
        kT = part(9216, HH, T)
        b = part(11264, HH, T)
        hi = part(13312, NT, HW)
        silu = part(15360, NT, HW)
        qe = part(17408, HH, T)
        kd = part(19456, HH, T)
        mix = part(21504, NT, D)
        pqT = part(0, 2 * PH, T)
        score = part(8192, 2 * PH, NK)
        keys_s = part(10240, 2 * PH, NK)
        acc = part(12288, NT, D)
        rows = part(16384, RING, D)
        acc2 = part(24576, D)
        cand_s = work[:, 0:PH * CAND].rearrange("p (h c) -> p h c", c=CAND)
        cand_i = work[:, 400:400 + PH * CAND].rearrange("p (h c) -> p h c", c=CAND)
        pick = work[:, 800:800 + TOPK * CAND].rearrange("p (k c) -> p k c", c=CAND)
        probs = work[:, 0:1024].rearrange("p (a n) -> p a n", a=2)
        probsT = work[:, 1024:2048].rearrange("p (a n) -> p a n", a=2)
        AT = work[:, 0:2048].rearrange("p (a l n) -> p a l n", a=2, n=P)

        ffw = work[0:FH, 0:3 * T].rearrange("p (a t) -> p a t", a=3)

        nmax = sb("nmax", [P, 2])
        psum_p = sb("psum_p", [P, 4])
        rinv = sb("rinv", [P, 2])
        state = sb("state", [P, HH, HD])
        kdT = sb("kdT", [P, 2, P])
        eblast = sb("eblast", [P, HH * NT])
        ssq = sb("ssq", [P, 16])
        lb_in = sb("lb_in", [P, DEPTH, HH])
        lb_all = sb("lb_all", [P, DEPTH, HH])
        lb_t = sb("lb_t", [P, 2, HH])
        lb = sb("lb", [P, 2, HH])
        top = hT[:, 0, 0:256].rearrange("p (a k) -> p a k", k=TOPK)
        top_i = hT[:, 0, 256:512].rearrange("p (a k) -> p a k", k=TOPK)
        top_u = hT[:, 1, 0:256].bitcast(U32).rearrange("p (a k) -> p a k", k=TOPK)
        sel_s = sb("sel_s", [P, PH, TOPK])
        sel_u = sb("sel_u", [P, PH, TOPK], U32)
        sel_p = sb("sel_p", [P, PH, TOPK])
        expert = sb("expert", [P, SLOTS])
        h_tile = hT[:, 3:5, :].rearrange("p a t -> p (a t)")
        expert_u = hT[:, 2, :].bitcast(U32).rearrange("p (i k) -> p i k", k=SLOTS)
        gate = sb("gate", [P, PH, TOPK])
        gsum = sb("gsum", [P, 2, PH])
        dot = sb("dot", [P, SLOTS])
        dots = sb("dots", [P, RING])
        act_g = sb("act_g", [P, SLOTS])
        wgt = sb("wgt", [P, SLOTS])
        row_base = sb("row_base", [P, 1])
        idx_col = sb("idx_col", [P, 2, RING], U32)

        dve_passed = sig("dve_passed", 0)
        pool_passed = sig("pool_passed", 0)
        const_in = sig("const_in", 0, 16)
        x_in = sig("x_in", 0, 16)
        emb_in = sig("emb_in", 0, 32)
        lb_loaded = sig("lb_loaded", 0, 16)
        ff_in = sig("ff_in", 32)
        gains_in = sig("gains_in", 32)
        ln1_in = sig("ln1_in", 32)
        ln2_in = sig("ln2_in", 32)
        pT_in = sig("pT_in", 16)
        keys_in = sig("keys_in", 16)
        panel_in = [sig(f"panel_in{s}", 16 * len(PANELS) // 2) for s in range(2)]
        h_ready = sig("h_ready", 2 * NT, NT)
        lb_shift = sig("lb_shift", 0, 1)
        lb_exp = sig("lb_exp", 0, 1)
        var_ready = sig("var_ready", 4, 1)
        root_ready = sig("root_ready", 4, 1)
        casts = sig("casts", 0, 2)
        dve_step = sig("dve_step", 270, 15)
        act_step = sig("act_step", 1)
        pool_step = sig("pool_step", 0)
        turned = sig("turned", 3 * NC)
        hT_act = sig("hT_act", 3 * NC // 2)
        hT_dve = sig("hT_dve", 3 * NC // 2)
        projected = sig("projected", 29)
        ff_z = sig("ff_z", 1)
        ff_e = sig("ff_e", 1)
        negc_ready = sig("negc_ready", 1)
        hf_ready = sig("hf_ready", HH)
        hf_exp = sig("hf_exp", HH)
        f_ready = sig("f_ready", 1)
        f_log = sig("f_log", 1)
        b_ready = sig("b_ready", 1)
        b_exp = sig("b_exp", 1)
        d_exp = sig("d_exp", 1)
        hdec_ready = sig("hdec_ready", 1)
        qk_ready = sig("qk_ready", 12)
        v_ready = sig("v_ready", 8)
        hg_sig = sig("hg_sig", NT)
        silu_ready = sig("silu_ready", NT)
        NS = FH * NT
        scored = sig("scored", NS)
        nmax_ready = sig("nmax_ready", NS)
        probs_ready = sig("probs_ready", NS)
        probs_turned = sig("probs_turned", NS)
        probsT_ready = sig("probsT_ready", NS)
        pv_done = sig("pv_done", NS)
        fox_out = sig("fox_out", NS)
        lev_ready = sig("lev_ready", HH)
        lev_exp = sig("lev_exp", HH)
        lev_mul = sig("lev_mul", HH)
        a_done = sig("a_done", 2 * HH * NT)
        at_ready = sig("at_ready", 2 * HH * NT)
        o_done = sig("o_done", HH * NT)
        o_out = sig("o_out", HH * NT)
        kd_turned = sig("kd_turned", HH * (NT - 1))
        kdT_ready = sig("kdT_ready", HH * (NT - 1))
        u_done = sig("u_done", HH * (NT - 1))
        state_ready = sig("state_ready", HH * (NT - 1))
        mix_ready = sig("mix_ready", 2)
        outed = sig("outed", 8)
        pre1 = sig("pre1", 8)
        queried = sig("queried", 16)
        pq_act = sig("pq_act", 8)
        pq_dve = sig("pq_dve", 8)
        key_scored = sig("key_scored", 16)
        score_sb = sig("score_sb", 16)
        gated = sig("gated", 8)
        gate_sig = sig("gate_sig", 8)
        pled = sig("pled", 8, 1)
        ple_mul = sig("ple_mul", 8)
        acc_init = sig("acc_init", 8)
        routed = sig("routed", NT)
        sel_shift = sig("sel_shift", NT)
        sel_exp = sig("sel_exp", NT)
        experts_ready = sig("experts_ready", NT)
        row_in = [sig(f"row_in{r}", NT * 2 * SLOTS // RING * 16) for r in range(RING)]
        row_used = sig("row_used", NT * 2 * SLOTS)
        dots_kept = sig("dots_kept", NT * SLOTS // RING)
        dots_done = sig("dots_done", NT)
        gelu_done = sig("gelu_done", NT)
        out_sent = sig("out_sent", 0, 16)

        block = ctx.enter_context(nc.Block())

        def settle(eng, passed):
            eng.sem_inc(passed.sem, 1)

        class Program:

            def __init__(self, eng, layer):
                self.eng, self.layer = eng, layer

            def need(self, s, n):
                self.eng.wait_ge(s.sem, self.layer * s.per_layer + (s.before + n))

            def mark(self, ins, s, n=1):
                ins.then_inc(s.sem, n)
                s.made += n
                return s.made

            def link(self, ins, s):
                self.need(s, self.mark(ins, s))

        G_T1 = 0
        G_PROJ = G_T1 + NC
        G_FOX = G_PROJ + 29
        G_HG = G_FOX + 3 * NS
        G_T2 = G_HG + 4 * HH * NT + 2 * HH * (NT - 1) - HH * NT
        G_OUT = G_T2 + NC
        G_T3 = G_OUT + 8
        G_Q = G_T3 + NC
        G_S0 = G_Q + 16
        G_PLE = G_S0 + 4
        G_S1 = G_PLE + 16

        def bank(g):
            return ps[:, g % BANKS, :]

        def fox_group(kind, s):
            g = G_FOX
            for st in range(NS + 2):
                for k in range(3):
                    q = st - k
                    if 0 <= q < NS:
                        if (k, q) == (kind, s):
                            return g
                        g += 1

        def hg_group(kind, j):
            g = G_HG
            for jj in range(HH * NT):
                for k in (0, 1, 3, 2, 4):
                    if k >= 3 and jj % NT == NT - 1:
                        continue
                    if (k, jj) == (kind, j):
                        return g
                    g += 1

        def score_group(i, q):
            return (G_S0 if i == 0 else G_S1 + 4 * (i - 1)) + q

        @block.sync
        def _(sp):
            sp.dma_start(cst[:], consts).then_inc(const_in.sem, 16)
            sp.dma_start(h[:], x.rearrange("(i p) d -> p i d", p=P)).then_inc(x_in.sem, 16)
            sp.dma_start(lb_in[:], lbl).then_inc(lb_loaded.sem, 16)
            for k, a in enumerate((emb_g, emb_b)):
                sp.dma_start(lng[:, k, :], a.partition_broadcast(P)).then_inc(emb_in.sem, 16)
            with sp.Fori(0, DEPTH) as layer:
                pr = Program(sp, layer)
                at = bass.ds(layer, 1)

                def load_panel(k):
                    w, col = PANELS[k]
                    if col is None:
                        src = w[at].rearrange("l (c p) n -> p (l c) n", p=P)
                        dst = panel[:, k % 2, 0:2 * PLE // P, :].rearrange("p (c a) n -> p c (a n)", c=PLE // P)
                    else:
                        src = w[at, :, col:col + PANEL].rearrange("l (c p) n -> p (l c) n", p=P)
                        dst = panel[:, k % 2]
                    pr.mark(sp.dma_start(dst, src), panel_in[k % 2], 16)

                def row(a):
                    return a[at].rearrange("l d -> (l d)").partition_broadcast(P)

                pr.need(pled, 0)
                load_panel(0)
                pr.mark(sp.dma_start(wff[:], w_in[at, :, 3 * FW:3 * FW + FH].rearrange("l (c p) n -> p (l c) n", p=P)),
                        ff_in, 16)
                pr.mark(sp.dma_start(ff_bias[:], fox_fb[at].rearrange("l h -> h l")), ff_in, 16)
                load_panel(1)
                for k, a in enumerate((fox_g, hg_g)):
                    pr.mark(sp.dma_start(ng[:, k, :], row(a)), gains_in, 16)
                pr.mark(sp.dma_start(pTs[:], pT[at].rearrange("l (c p) t -> p (l c) t", p=P)), pT_in, 16)
                pr.need(h_ready, 0)
                for k, a in enumerate((ln1_g, ln1_b)):
                    pr.mark(sp.dma_start(lng[:, k, :], row(a)), ln1_in, 16)
                for k in range(2, 9):
                    pr.need(projected, 1 + 4 * (k - 1))
                    load_panel(k)
                for k in range(9, 11):
                    pr.need(outed, 4 * (k - 8))
                    load_panel(k)
                pr.need(h_ready, NT)
                for k, a in enumerate((ln2_g, ln2_b)):
                    pr.mark(sp.dma_start(lng[:, k, :], row(a)), ln2_in, 16)
                pr.mark(sp.dma_start(keys_s, keysT[at].rearrange("l d a n -> d (l a) n")), keys_in, 16)
                for k in range(11, 15):
                    pr.need(queried, 4 * (k - 10))
                    load_panel(k)
                pr.need(gated, 4)
                load_panel(15)

        @block.gpsimd
        def _(pool):
            with pool.Fori(0, DEPTH) as layer:
                with pool.Fori(0, NT) as i:
                    tile = layer * NT + i
                    pool.wait_ge(experts_ready.sem, tile + 1)
                    settle(pool, pool_passed)
                    for half, table in enumerate((u_rows, v_rows)):
                        with pool.Fori(0, SLOTS // (2 * RING)) as j:
                            for par in range(2):
                                slot = (tile * 2 + half) * SLOTS + j * 2 * RING + par * RING
                                pool.wait_ge(row_used.sem, slot + RING - RING + 1)
                                nc.gpsimd.tensor_copy(
                                    idx_col[:, par, :],
                                    expert_u[:, bass.ds(i, 1), bass.ds(j * 2 * RING + par * RING, RING)]
                                    .rearrange("p a n -> p (a n)")).then_inc(pool_step.sem, 1)
                                pool.wait_ge(pool_step.sem, ((tile * 2 + half) * (SLOTS // (2 * RING)) + j) * 2 + par + 1)
                                for r in range(RING):
                                    pool.wait_ge(row_used.sem, slot + r + 1)
                                    settle(pool, pool_passed)
                                    pool.indirect_dma_start(
                                        out=rows[:, r, :], out_offset=None, in_=table,
                                        in_offset=bass.IndirectOffsetOnAxis(ap=idx_col[:, par, r:r + 1], axis=0)
                                    ).then_inc(row_in[r].sem, 16)

        @block.tensor
        def _(pe):
            pe.wait_ge(const_in.sem, 16)
            pe.wait_ge(casts.sem, 2)
            pe.sem_inc(pled.sem, 1)
            with pe.Fori(0, DEPTH) as layer:
                pr = Program(pe, layer)
                freed = []

                def take(g, release):
                    assert g == len(freed), (g, len(freed))
                    if g >= BANKS:
                        pr.need(*freed[g - BANKS])
                    freed.append(release)
                    return bank(g)

                def turn(src, g0, n):
                    for c in range(NC):
                        o = take(g0 + c, ((hT_act, hT_dve)[c % 2], (n * NC + c) // 2 + 1))
                        for i in range(NT):
                            mm = nc.tensor.transpose(o[:, i * P:(i + 1) * P], src[:, i, c * P:(c + 1) * P], ident)
                        pr.mark(mm, turned)
                    pr.need(hT_act, (n + 1) * NC // 2)
                    pr.need(hT_dve, (n + 1) * NC // 2)

                def columns(o, w, m):
                    for c in range(NC):
                        mm = nc.tensor.matmul(o, w[:, c, m * P:(m + 1) * P], hT[:, c, :],
                                              start=(c == 0), stop=(c == NC - 1))
                    return mm

                def tokens(o, w, i):
                    for c in range(NC):
                        mm = nc.tensor.matmul(o, hT[:, c, i * P:(i + 1) * P], w[:, c, :],
                                              start=(c == 0), stop=(c == NC - 1))
                    return mm

                def loaded(k):
                    pr.need(panel_in[k % 2], 16 * (k // 2 + 1))
                    return panel[:, k % 2]

                pr.need(h_ready, 0)
                turn(h, G_T1, 0)
                pr.need(ff_in, 32)
                g = G_PROJ
                o = take(g, (ff_z, 1))
                for c in range(NC):
                    mm = nc.tensor.matmul(o[0:FH, :], wff[:, c, :], hT[:, c, :], start=(c == 0), stop=(c == NC - 1))
                pr.mark(mm, projected)
                for k in range(7):
                    w = loaded(k)
                    for m in range(4):
                        g += 1
                        release = [(hf_ready, m + 1), (qk_ready, m + 1), (qk_ready, 5 + m), (qk_ready, 9 + m),
                                   (v_ready, m + 1), (v_ready, 5 + m), (silu_ready, m + 1)][k]
                        o = take(g, release)
                        pr.mark(columns(o, w, m) if k < 4 else tokens(o, w, m), projected)

                pr.need(negc_ready, 1)
                pr.need(qk_ready, 12)
                pr.need(v_ready, 4)
                for st in range(NS + 2):
                    if st < NS:
                        hd, i = st // NT, st % NT
                        n = (i + 1) * P
                        o = take(fox_group(0, st), (probs_ready, st + 1))
                        rows_ = slice(FD * (hd % 2), FD * (hd % 2) + FD)
                        nc.tensor.matmul(o[:, 0:n], fqT[rows_, hd // 2, i * P:(i + 1) * P], fkT[rows_, hd // 2, 0:n],
                                         start=True, stop=False)
                        nc.tensor.matmul(o[:, 0:n], ident[0:FH, hd:hd + 1].to_broadcast([FH, P]), negc[:, 0:n],
                                         start=False, stop=False)
                        pr.mark(nc.tensor.matmul(o[:, n - P:n], ident_b, cmask_b, start=False, stop=True), scored)
                    if 0 <= st - 1 < NS:
                        s = st - 1
                        i = s % NT
                        o = take(fox_group(1, s), (probsT_ready, s + 1))
                        pr.need(probs_ready, s + 1)
                        for j in range(i + 1):
                            mm = nc.tensor.transpose(o[:, j * P:(j + 1) * P], probs[:, s % 2, j * P:(j + 1) * P], ident)
                        pr.mark(mm, probs_turned)
                    if 0 <= st - 2:
                        s = st - 2
                        hd, i = s // NT, s % NT
                        o = take(fox_group(2, s), (fox_out, s + 1))
                        pr.need(probsT_ready, s + 1)
                        for j in range(i + 1):
                            mm = nc.tensor.matmul(o[:, 0:FD], probsT[:, s % 2, j * P:(j + 1) * P],
                                                  fv[:, j, hd * FD:(hd + 1) * FD], start=(j == 0), stop=(j == i))
                        pr.mark(mm, pv_done)

                pr.need(hdec_ready, 1)
                pr.need(v_ready, 8)
                for j in range(HH * NT):
                    hd, i = j // NT, j % NT
                    toks = slice(i * P, (i + 1) * P)
                    if i == 0:
                        pr.need(lev_mul, hd + 1)
                    for half in range(2):
                        o = take(hg_group(half, j), (at_ready, 2 * j + half + 1))
                        for k in range(4):
                            lev = 4 * half + k
                            kk = kT[:, hd, toks] if lev == 0 else KE[:, lev - 1, toks]
                            qq = hqT[:, hd, toks] if lev == 0 else QE[:, lev - 1, toks]
                            mm = nc.tensor.matmul(o[:, k * P:(k + 1) * P], kk, qq, start=True, stop=True)
                        pr.mark(mm, a_done)
                    up = hd * (NT - 1) + i
                    if i < NT - 1:
                        o = take(hg_group(3, j), (kdT_ready, up + 1))
                        pr.mark(nc.tensor.transpose(o[:, 0:P], kd[:, hd, toks], ident), kd_turned)
                    o = take(hg_group(2, j), (o_out, j + 1))
                    vv = hi[:, i, hd * HD:(hd + 1) * HD]
                    if i > 0:
                        pr.need(state_ready, up)
                        nc.tensor.matmul(o[:, 0:HD], qe[:, hd, toks], state[:, hd, :], start=True, stop=False)
                    pr.need(at_ready, 2 * j + 2)
                    for lev in range(LEVELS):
                        mm = nc.tensor.matmul(o[:, 0:HD], AT[:, j % 2, lev, :], vv,
                                              start=(lev == 0 and i == 0), stop=(lev == LEVELS - 1))
                    pr.mark(mm, o_done)
                    if i < NT - 1:
                        o = take(hg_group(4, j), (state_ready, up + 1))
                        pr.need(kdT_ready, up + 1)
                        pr.mark(nc.tensor.matmul(o[:, 0:HD], kdT[:, up % 2, :], vv, start=True, stop=True), u_done)

                pr.need(mix_ready, 2)
                turn(mix, G_T2, 1)
                for half in range(2):
                    w = loaded(7 + half)
                    for i in range(NT):
                        o = take(G_OUT + 4 * half + i, (pre1, 4 * half + i + 1))
                        pr.mark(tokens(o, w, i), outed)

                pr.need(h_ready, NT)
                turn(h, G_T3, 2)
                for k in range(4):
                    w = loaded(9 + k)
                    for m in range(4):
                        g = 4 * k + m
                        o = take(G_Q + g, ((pq_act, pq_dve)[g % 2], g // 2 + 1))
                        pr.mark(columns(o, w, m), queried)

                def scores(i):
                    for q in range(4):
                        o = take(score_group(i, q), (score_sb, 4 * i + q + 1))
                        for a in range(4):
                            mm = nc.tensor.matmul(o[:, a * NK:(a + 1) * NK], pqT[:, 4 * q + a, i * P:(i + 1) * P],
                                                  keys_s[:, 4 * q + a, :], start=True, stop=True)
                        pr.mark(mm, key_scored)

                pr.need(keys_in, 16)
                pr.need(pq_act, 8)
                pr.need(pq_dve, 8)
                scores(0)
                pr.need(pT_in, 16)
                for half in range(2):
                    w = loaded(13 + half)
                    if half == 0:
                        wp = None
                    for i in range(NT):
                        o = take(G_PLE + 4 * half + i, (gate_sig, 4 * half + i + 1))
                        pr.mark(tokens(o, w, i), gated)
                loaded(15)
                wp = panel[:, 1, 0:4, :].rearrange("p (c a) n -> p c (a n)", c=2)
                for half in range(2):
                    for i in range(NT):
                        o = take(G_PLE + 8 + 4 * half + i, (ple_mul, 4 * half + i + 1))
                        for c in range(2):
                            mm = nc.tensor.matmul(o, pTs[:, c, i * P:(i + 1) * P],
                                                  wp[:, c, half * 512:(half + 1) * 512], start=(c == 0), stop=(c == 1))
                        pr.mark(mm, pled)
                for i in range(1, NT):
                    scores(i)

        @block.scalar
        def _(act):
            act.wait_ge(lb_shift.sem, 1)
            nc.scalar.activation(lb_in[:], lb_in[:], ACT.Exp).then_inc(lb_exp.sem, 1)
            act.wait_ge(var_ready.sem, 1)
            nc.scalar.activation(rstd[:], rstd[:], ACT.Sqrt).then_inc(root_ready.sem, 1)
            with act.Fori(0, DEPTH) as layer:
                pr = Program(act, layer)

                def turn(g0, n):
                    for c in range(0, NC, 2):
                        pr.need(turned, n * NC + c + 1)
                        pr.mark(nc.scalar.copy(hT[:, c, :], bank(g0 + c)), hT_act)

                def root(n, var):
                    pr.need(var_ready, n)
                    pr.mark(nc.scalar.activation(var, var, ACT.Sqrt), root_ready)

                turn(G_T1, 0)
                pr.need(ff_z, 1)
                pr.link(nc.scalar.activation(ffw[:, 2, :], ffw[:, 1, :], ACT.Exp), act_step)
                pr.mark(nc.scalar.activation(ffw[:, 1, :], ffw[:, 2, :], ACT.Ln, bias=1.0), ff_e)
                for m in range(HH):
                    pr.need(hf_ready, m + 1)
                    pr.mark(nc.scalar.activation(gt[0][:, m, :], gt[0][:, m, :], ACT.Exp), hf_exp)
                for m in range(4):
                    pr.need(projected, 6 + m)
                    pr.mark(nc.scalar.copy(hqT[:, m, :], bank(G_PROJ + 5 + m)), qk_ready)
                pr.need(f_ready, 1)
                nc.scalar.activation(gt[1], gt[1], ACT.Ln)
                pr.mark(nc.scalar.activation(gt[2], gt[2], ACT.Ln), f_log)
                pr.need(b_ready, 1)
                pr.mark(nc.scalar.activation(qe, b, ACT.Exp), b_exp)
                for hd in range(HH):
                    for i in range(NT):
                        last = nc.scalar.activation(kd[:, hd, i * P:(i + 1) * P], b[:, hd, i * P:(i + 1) * P], ACT.Exp,
                                                    scale=-1.0, bias=b[:, hd, (i + 1) * P - 1:(i + 1) * P])
                pr.mark(last, d_exp)
                pr.need(hdec_ready, 1)
                for k, dst in enumerate((fqT, fkT)):
                    for m in range(4):
                        pr.need(projected, 10 + 4 * k + m)
                        pr.mark(nc.scalar.copy(dst[:, m, :], bank(G_PROJ + 9 + 4 * k + m)), qk_ready)
                for i in range(NT):
                    pr.need(projected, 26 + i)
                    pr.mark(nc.scalar.activation(silu[:, i, :], bank(G_PROJ + 25 + i), ACT.Sigmoid), hg_sig)
                for s in range(NS):
                    n = (s % NT + 1) * P
                    pr.need(nmax_ready, s + 1)
                    if s >= 2:
                        pr.need(probs_turned, s - 1)
                        pr.need(fox_out, s - 1)
                    pr.mark(nc.scalar.activation(probs[:, s % 2, 0:n], bank(fox_group(0, s))[:, 0:n], ACT.Exp,
                                                 scale=SCALE, bias=nmax[:, s % 2:s % 2 + 1],
                                                 accum_out=psum_p[:, s % 2:s % 2 + 1]), probs_ready)
                root(1, ssq[:, 0:NT])
                for hd in range(HH):
                    pr.need(lev_ready, hd + 1)
                    pr.mark(nc.scalar.activation(KE, KE, ACT.Exp), lev_exp)
                    for i in range(NT - 1):
                        up = hd * (NT - 1) + i
                        pr.need(kd_turned, up + 1)
                        if up >= 2:
                            pr.need(u_done, up - 1)
                        pr.mark(nc.scalar.copy(kdT[:, up % 2, :], bank(hg_group(3, hd * NT + i))[:, 0:P]), kdT_ready)
                root(2, ssq[:])
                turn(G_T2, 1)
                root(3, rstd[:])
                turn(G_T3, 2)
                for g in range(0, 16, 2):
                    pr.need(queried, g + 1)
                    pr.mark(nc.scalar.copy(pqT[:, g, :], bank(G_Q + g)), pq_act)

                def scores(i):
                    if i > 0:
                        pr.need(routed, i)
                    for q in range(4):
                        pr.need(key_scored, 4 * i + q + 1)
                        pr.mark(nc.scalar.copy(score[:, 4 * q:4 * q + 4, :],
                                               bank(score_group(i, q)).rearrange("p (a n) -> p a n", n=NK)), score_sb)

                scores(0)
                for g in range(8):
                    half, i = g // 4, g % 4
                    pr.need(gated, g + 1)
                    pr.mark(nc.scalar.activation(acc[:, i, half * 512:(half + 1) * 512], bank(G_PLE + g),
                                                 ACT.Sigmoid), gate_sig)
                for i in range(NT):
                    pr.need(sel_shift, i + 1)
                    pr.mark(nc.scalar.activation(gate[:], gate[:], ACT.Exp), sel_exp)
                    if i < NT - 1:
                        scores(i + 1)
                    pr.need(dots_done, i + 1)
                    pr.mark(nc.scalar.activation(act_g[:], dot[:], ACT.Gelu), gelu_done)
                root(4, rstd[:])

        @block.vector
        def _(dve):
            before = [0]

            def first(ins):
                ins.then_inc(dve_step.sem, 1)
                before[0] += 1
                dve.wait_ge(dve_step.sem, before[0])

            def norm(step, root, signal):
                for i in range(NT):
                    for k in range(2):
                        last = nc.vector.bn_stats(stat[:, i, 6 * k:6 * k + 6], h[:, i, k * 512:(k + 1) * 512])
                step(last)
                for i in range(NT):
                    last = nc.vector.bn_aggr(mv[:, i, :], stat[:, i, :])
                step(last)
                root(nc.vector.tensor_scalar(rstd[:], mv[:, :, 1], LN_EPS, None, ALU.add))
                step(nc.vector.reciprocal(rstd[:], rstd[:]))
                for i in range(NT):
                    last = nc.vector.tensor_scalar(h[:, i, :], h[:, i, :], mv[:, i, 0:1], rstd[:, i:i + 1],
                                                   ALU.subtract, ALU.mult)
                step(last)
                for i in range(NT):
                    last = nc.vector.tensor_tensor(h[:, i, :], h[:, i, :], lng[:, 0, :], ALU.mult)
                step(last)
                for i in range(NT):
                    signal(nc.vector.tensor_tensor(h[:, i, :], h[:, i, :], lng[:, 1, :], ALU.add))

            nc.vector.memset(row_base[:], -float(NE)).then_inc(row_used.sem, RING)
            dve.wait_ge(row_used.sem, RING)
            dve.wait_ge(const_in.sem, 16)
            nc.vector.tensor_copy(ident_b, ident).then_inc(casts.sem, 1)
            nc.vector.tensor_copy(cmask_b, cmask).then_inc(casts.sem, 1)
            dve.wait_ge(lb_loaded.sem, 16)
            first(nc.vector.tensor_copy(lb_t[:, 0, :], lb_in[:, 0, :]))
            for k in range(1, DEPTH):
                first(nc.vector.tensor_tensor(lb_t[:, 0, :], lb_t[:, 0, :], lb_in[:, k, :], ALU.max))
            for k in range(DEPTH):
                last = nc.vector.tensor_tensor(lb_in[:, k, :], lb_in[:, k, :], lb_t[:, 0, :], ALU.subtract)
            last.then_inc(lb_shift.sem, 1)
            dve.wait_ge(lb_exp.sem, 1)
            first(nc.vector.tensor_copy(lb_t[:, 0, :], lb_in[:, 0, :]))
            for k in range(1, DEPTH):
                first(nc.vector.tensor_tensor(lb_t[:, 0, :], lb_t[:, 0, :], lb_in[:, k, :], ALU.add))
            first(nc.vector.reciprocal(lb_t[:, 1, :], lb_t[:, 0, :]))
            for k in range(DEPTH):
                last = nc.vector.tensor_tensor(lb_in[:, k, :], lb_in[:, k, :], lb_t[:, 1, :], ALU.mult)
            first(last)
            first(nc.vector.tensor_copy(lb_all[:, 0, :], lb_in[:, 0, :]))
            for k in range(1, DEPTH):
                first(nc.vector.tensor_tensor(lb_all[:, k, :], lb_all[:, k - 1, :], lb_in[:, k, :], ALU.add))
            first(nc.vector.tensor_copy(lb_t[:, 0, :], lb_in[:, 0, :]))
            for k in range(DEPTH):
                last = nc.vector.tensor_tensor(lb_all[:, k, :], lb_all[:, k, :], lb_t[:, 0, :], ALU.subtract)
            first(last)
            dve.wait_ge(x_in.sem, 16)
            dve.wait_ge(emb_in.sem, 32)
            def root0(ins):
                ins.then_inc(var_ready.sem, 1)
                dve.wait_ge(root_ready.sem, 1)

            norm(first, root0, lambda ins: ins.then_inc(h_ready.sem, 1))
            assert before[0] == dve_step.before, before[0]

            with dve.Fori(0, DEPTH) as layer:
                pr = Program(dve, layer)

                def step(ins):
                    n = pr.mark(ins, dve_step)
                    pr.need(dve_step, n)
                    settle(dve, dve_passed)

                def root(ins):
                    pr.need(root_ready, pr.mark(ins, var_ready))

                def turn(g0, n):
                    for c in range(1, NC, 2):
                        pr.need(turned, n * NC + c + 1)
                        pr.mark(nc.vector.tensor_copy(hT[:, c, :], bank(g0 + c)), hT_dve)

                step(nc.vector.tensor_scalar(row_base[:], row_base[:], float(NE), None, ALU.add))
                lb_now = lb_all[:, bass.ds(layer, 1), :].rearrange("p a h -> p (a h)")
                nc.vector.tensor_scalar(lb[:, 0, :], lb_now, LB_FLOOR, None, ALU.max)
                step(nc.vector.tensor_scalar(lb[:, 1, :], lb_now, -1.0, 1.0, ALU.mult, ALU.add))
                turn(G_T1, 0)
                pr.need(projected, 1)
                pr.need(ff_in, 32)
                step(nc.vector.tensor_scalar(ffw[:, 0, :], bank(G_PROJ)[0:FH, :], ff_bias[:], None, ALU.add))
                pr.mark(nc.vector.scalar_tensor_tensor(out=ffw[:, 1, :], in0=ffw[:, 0, :], scalar=-1.0, in1=ffw[:, 0, :],
                                                       op0=ALU.mult, op1=ALU.min), ff_z)
                for m in range(HH):
                    pr.need(projected, 2 + m)
                    pr.mark(nc.vector.tensor_scalar(gt[0][:, m, :], bank(G_PROJ + 1 + m), 80.0, None, ALU.min),
                            hf_ready)
                pr.need(ff_e, 1)
                step(nc.vector.scalar_tensor_tensor(out=ffw[:, 2, :], in0=ffw[:, 0, :], scalar=0.0, in1=ffw[:, 1, :],
                                                    op0=ALU.min, op1=ALU.subtract))
                step(nc.vector.memset(ffw[:, 1, :], 1.0))
                step(nc.vector.tensor_tensor_scan(out=ffw[:, 0, :], data0=ffw[:, 1, :], data1=ffw[:, 2, :],
                                                  initial=0.0, op0=ALU.mult, op1=ALU.add))
                pr.mark(nc.vector.tensor_scalar(negc[:], ffw[:, 0, :], -1.0 / SCALE, None, ALU.mult), negc_ready)
                pr.need(hf_exp, HH)
                step(nc.vector.tensor_scalar(kT, gt[0], 1.0, None, ALU.add))
                step(nc.vector.reciprocal(kT, kT))
                for m in range(HH):
                    last = nc.vector.tensor_scalar(kT[:, m, :], kT[:, m, :], lb[:, 1, m:m + 1], None, ALU.mult)
                step(last)
                step(nc.vector.tensor_tensor(gt[0], gt[0], kT, ALU.mult))
                for m in range(HH):
                    last = nc.vector.tensor_scalar(gt[0][:, m, :], gt[0][:, m, :], lb[:, 0, m:m + 1], None, ALU.add)
                step(last)
                nc.vector.tensor_scalar(gt[1], gt[0], 1.0 / LN_SPLIT, None, ALU.max)
                pr.mark(nc.vector.tensor_scalar(gt[2], gt[0], LN_SPLIT, 1.0, ALU.mult, ALU.min), f_ready)
                pr.need(f_log, 1)
                step(nc.vector.tensor_tensor(gt[1], gt[1], gt[2], ALU.add))
                for m in range(HH):
                    last = nc.vector.tensor_tensor_scan(out=b[:, m, :], data0=reset, data1=gt[1][:, m, :],
                                                        initial=0.0, op0=ALU.mult, op1=ALU.add)
                pr.mark(last, b_ready)
                pr.need(b_exp, 1)
                step(nc.vector.tensor_copy(eblast[:].rearrange("p (h i) -> p h i", h=HH),
                                           qe.rearrange("p h (i t) -> p h i t", t=P)[:, :, :, P - 1]))
                pr.need(qk_ready, 4)
                nc.vector.tensor_tensor(qe, qe, hqT, ALU.mult)
                pr.need(d_exp, 1)
                pr.mark(nc.vector.tensor_tensor(kd, kd, kT, ALU.mult), hdec_ready)
                pr.need(hdec_ready, 1)
                for k, dst in enumerate((fv, hi)):
                    for i in range(NT):
                        pr.need(projected, 18 + 4 * k + i)
                        pr.mark(nc.vector.tensor_copy(dst[:, i, :], bank(G_PROJ + 17 + 4 * k + i)), v_ready)
                for i in range(NT):
                    pr.need(hg_sig, i + 1)
                    pr.mark(nc.vector.tensor_tensor(silu[:, i, :], silu[:, i, :], bank(G_PROJ + 25 + i), ALU.mult),
                            silu_ready)

                for st in range(NS + 2):
                    if st < NS:
                        n = (st % NT + 1) * P
                        pr.need(scored, st + 1)
                        if st >= 2:
                            pr.need(probs_ready, st - 1)
                        if st >= 1:
                            pr.need(nmax_ready, st)
                        step(nc.vector.tensor_reduce(rinv[:, 1:2], bank(fox_group(0, st))[:, 0:n], AX_X, ALU.max))
                        pr.mark(nc.vector.tensor_scalar(nmax[:, st % 2:st % 2 + 1], rinv[:, 1:2], -SCALE, None,
                                                        ALU.mult), nmax_ready)
                    if 0 <= st - 1 < NS:
                        s = st - 1
                        n = (s % NT + 1) * P
                        pr.need(probs_turned, s + 1)
                        if s >= 2:
                            pr.need(pv_done, s - 1)
                        pr.mark(nc.vector.tensor_copy(probsT[:, s % 2, 0:n], bank(fox_group(1, s))[:, 0:n]),
                                probsT_ready)
                    if 0 <= st - 2:
                        s = st - 2
                        hd, i = s // NT, s % NT
                        pr.need(probs_ready, s + 1)
                        if s >= 1:
                            pr.need(fox_out, s)
                        step(nc.vector.reciprocal(rinv[:, 0:1], psum_p[:, s % 2:s % 2 + 1]))
                        pr.need(pv_done, s + 1)
                        pr.mark(nc.vector.tensor_scalar(mix[:, i, hd * FD:(hd + 1) * FD],
                                                        bank(fox_group(2, s))[:, 0:FD], rinv[:, 0:1], None, ALU.mult),
                                fox_out)

                sq = gt[0]
                pr.need(pv_done, NS)
                pr.need(fox_out, NS)
                step(nc.vector.tensor_tensor(sq, mix[:, :, 0:FW], mix[:, :, 0:FW], ALU.mult))
                step(nc.vector.tensor_reduce(ssq[:, 0:NT], sq, AX_X, ALU.add))
                root(nc.vector.tensor_scalar(ssq[:, 0:NT], ssq[:, 0:NT], 1.0 / FW, RMS_EPS, ALU.mult, ALU.add))
                step(nc.vector.reciprocal(ssq[:, 0:NT], ssq[:, 0:NT]))
                pr.need(gains_in, 32)
                for i in range(NT):
                    last = nc.vector.scalar_tensor_tensor(out=mix[:, i, 0:FW], in0=mix[:, i, 0:FW],
                                                          scalar=ssq[:, i:i + 1], in1=ng[:, 0, :],
                                                          op0=ALU.mult, op1=ALU.mult)
                pr.mark(last, mix_ready)

                for hd in range(HH):
                    if hd > 0:
                        pr.need(a_done, 2 * NT * hd)
                    for lev in range(1, LEVELS):
                        m = 2 ** (lev - 1)
                        bb = b[:, hd, :].rearrange("p (g a m) -> p g a m", a=2, m=m)
                        dd = KE[:, lev - 1, :].rearrange("p (g a m) -> p g a m", a=2, m=m)
                        mid = bb[:, :, 0, m - 1:m].to_broadcast([P, T // (2 * m), m])
                        nc.vector.tensor_tensor(dd[:, :, 0, :], mid, bb[:, :, 0, :], ALU.subtract)
                        last = nc.vector.tensor_tensor(dd[:, :, 1, :], bb[:, :, 1, :], mid, ALU.subtract)
                    pr.mark(last, lev_ready)
                    pr.need(lev_exp, hd + 1)

                    def over_levels(ap):
                        return ap.rearrange("p (o t) -> p o t", o=1).to_broadcast([P, LEVELS - 1, T])

                    step(nc.vector.tensor_tensor(QE, KE, over_levels(hqT[:, hd, :]), ALU.mult))
                    pr.mark(nc.vector.tensor_tensor(KE, KE, over_levels(kT[:, hd, :]), ALU.mult), lev_mul)
                    for i in range(NT):
                        j = hd * NT + i
                        if j >= 2:
                            pr.need(o_done, j - 1)
                        for half in range(2):
                            pr.need(a_done, 2 * j + half + 1)
                            pr.mark(nc.vector.tensor_tensor(
                                AT[:, j % 2, 4 * half:4 * half + 4, :].rearrange("p l n -> p (l n)"),
                                bank(hg_group(half, j)), level_mask[:, half * 512:(half + 1) * 512], ALU.mult),
                                at_ready)
                        pr.need(o_done, j + 1)
                        pr.mark(nc.vector.tensor_copy(mix[:, i, FW + hd * HD:FW + (hd + 1) * HD],
                                                      bank(hg_group(2, j))[:, 0:HD]), o_out)
                        if i < NT - 1:
                            up = hd * (NT - 1) + i
                            pr.need(u_done, up + 1)
                            upd = bank(hg_group(4, j))[:, 0:HD]
                            if i == 0:
                                ins = nc.vector.tensor_copy(state[:, hd, :], upd)
                            else:
                                pr.need(state_ready, up)
                                ins = nc.vector.scalar_tensor_tensor(out=state[:, hd, :], in0=state[:, hd, :],
                                                                     scalar=eblast[:, j:j + 1], in1=upd,
                                                                     op0=ALU.mult, op1=ALU.add)
                            pr.mark(ins, state_ready)
                pr.need(o_out, HH * NT)
                pr.need(mix_ready, 1)
                o_hg = mix[:, :, FW:2 * FW]
                step(nc.vector.tensor_tensor(sq, o_hg, o_hg, ALU.mult))
                step(nc.vector.tensor_reduce(ssq[:], sq.rearrange("p i (h n) -> p (i h) n", n=HD), AX_X, ALU.add))
                root(nc.vector.tensor_scalar(ssq[:], ssq[:], 1.0 / HD, RMS_EPS, ALU.mult, ALU.add))
                step(nc.vector.reciprocal(ssq[:], ssq[:]))
                for i in range(NT):
                    for hd in range(HH):
                        cols = slice(FW + hd * HD, FW + (hd + 1) * HD)
                        last = nc.vector.scalar_tensor_tensor(
                            out=mix[:, i, cols], in0=mix[:, i, cols], scalar=ssq[:, i * HH + hd:i * HH + hd + 1],
                            in1=ng[:, 1, hd * HD:(hd + 1) * HD], op0=ALU.mult, op1=ALU.mult)
                step(last)
                pr.mark(nc.vector.tensor_tensor(o_hg, o_hg, silu, ALU.mult), mix_ready)

                turn(G_T2, 1)
                for g in range(8):
                    half, i = g // 4, g % 4
                    pr.need(outed, g + 1)
                    hh = h[:, i, half * 512:(half + 1) * 512]
                    pr.mark(nc.vector.scalar_tensor_tensor(out=hh, in0=hh, scalar=ALPHA, in1=bank(G_OUT + g),
                                                           op0=ALU.mult, op1=ALU.add), pre1)
                pr.need(pre1, 8)
                pr.need(ln1_in, 32)
                norm(step, root, lambda ins: pr.mark(ins, h_ready))
                pr.need(h_ready, NT)

                turn(G_T3, 2)
                for g in range(1, 16, 2):
                    pr.need(queried, g + 1)
                    pr.mark(nc.vector.tensor_copy(pqT[:, g, :], bank(G_Q + g)), pq_dve)
                for g in range(8):
                    half, i = g // 4, g % 4
                    aa = acc[:, i, half * 512:(half + 1) * 512]
                    pr.need(gate_sig, g + 1)
                    pr.need(pled, g + 1)
                    pr.mark(nc.vector.tensor_tensor(aa, aa, bank(G_PLE + 8 + g), ALU.mult), ple_mul)
                    pr.need(ple_mul, g + 1)
                    pr.mark(nc.vector.scalar_tensor_tensor(out=aa, in0=h[:, i, half * 512:(half + 1) * 512],
                                                           scalar=ALPHA, in1=aa, op0=ALU.mult, op1=ALU.add), acc_init)
                pr.need(acc_init, 8)
                settle(dve, dve_passed)

                with dve.Fori(0, NT) as i:
                    tile = layer * NT + i
                    TILE_STEPS = 43
                    at_entry = dve_step.made
                    count = [0]

                    def tstep(ins):
                        ins.then_inc(dve_step.sem, 1)
                        count[0] += 1
                        dve.wait_ge(dve_step.sem, layer * dve_step.per_layer + i * TILE_STEPS +
                                    (dve_step.before + at_entry + count[0]))
                        settle(dve, dve_passed)

                    def top16(values, keep, keep_u, n):
                        for a in range(n):
                            last = nc.vector.max(keep[:, a, 0:8], values[:, a, :])
                        tstep(last)
                        for a in range(n):
                            last = nc.vector.max_index(keep_u[:, a, 0:8], keep[:, a, 0:8], values[:, a, :])
                        tstep(last)
                        for a in range(n):
                            last = nc.vector.match_replace(values[:, a, :], keep[:, a, 0:8], values[:, a, :], -3e38)
                        tstep(last)
                        for a in range(n):
                            last = nc.vector.max(keep[:, a, 8:16], values[:, a, :])
                        tstep(last)
                        for a in range(n):
                            last = nc.vector.max_index(keep_u[:, a, 8:16], keep[:, a, 8:16], values[:, a, :])
                        tstep(last)

                    dve.wait_ge(score_sb.sem, (tile + 1) * 4)
                    settle(dve, dve_passed)
                    top16(score, top, top_u, 2 * PH)
                    tstep(nc.vector.tensor_copy(top_i, top_u))
                    ti = top_i.rearrange("p (h a) k -> p h a k", a=2)
                    ts = top.rearrange("p (h a) k -> p h a k", a=2)
                    tstep(nc.vector.tensor_scalar(ti[:, :, 0, :], ti[:, :, 0, :], float(NK), None, ALU.mult))
                    off = 0
                    for a in range(8):
                        nb = STAIR[a]
                        for src, dst in ((ts, cand_s), (ti, cand_i)):
                            nc.vector.tensor_tensor(dst[:, :, off:off + nb], src[:, :, 1, 0:nb],
                                                    src[:, :, 0, a:a + 1].to_broadcast([P, PH, nb]), ALU.add)
                        off += nb
                    for src, dst in ((ts, cand_s), (ti, cand_i)):
                        last = nc.vector.tensor_tensor(dst[:, :, off:CAND], src[:, :, 0, 8:TOPK],
                                                       src[:, :, 1, 0:1].to_broadcast([P, PH, 8]), ALU.add)
                    tstep(last)
                    top16(cand_s, sel_s, sel_u, PH)
                    nc.vector.tensor_copy(sel_p[:], sel_u[:]).then_inc(routed.sem, 1)
                    dve.wait_ge(routed.sem, tile + 1)
                    nc.vector.tensor_tensor(gate[:], sel_s[:], sel_s[:, :, 0:1].to_broadcast([P, PH, TOPK]),
                                            ALU.subtract).then_inc(sel_shift.sem, 1)
                    for a in range(PH):
                        tstep(nc.vector.tensor_tensor(
                            pick, iota[:, 0:CAND].rearrange("p (o c) -> p o c", o=1).to_broadcast([P, TOPK, CAND]),
                            sel_p[:, a, :].rearrange("p (k o) -> p k o", o=1).to_broadcast([P, TOPK, CAND]),
                            ALU.is_equal))
                        tstep(nc.vector.tensor_tensor(
                            pick, pick, cand_i[:, a:a + 1, :].to_broadcast([P, TOPK, CAND]), ALU.mult))
                        tstep(nc.vector.tensor_reduce(expert[:, a * TOPK:(a + 1) * TOPK], pick, AX_X, ALU.add))
                    nc.vector.tensor_scalar(expert_u[:, bass.ds(i, 1), :].rearrange("p a n -> p (a n)"), expert[:],
                                            row_base[:, 0:1], None, ALU.add).then_inc(experts_ready.sem, 1)
                    dve.wait_ge(sel_exp.sem, tile + 1)
                    tstep(nc.vector.tensor_reduce(gsum[:, 0, :], gate[:], AX_X, ALU.add))
                    tstep(nc.vector.reciprocal(gsum[:, 1, :], gsum[:, 0, :]))
                    tstep(nc.vector.tensor_tensor(gate[:], gate[:],
                                                  gsum[:, 1, :].rearrange("p (h o) -> p h o", o=1)
                                                  .to_broadcast([P, PH, TOPK]), ALU.mult))
                    h_i = h[:, bass.ds(i, 1), :].rearrange("p a d -> p (a d)")
                    acc_i = acc[:, bass.ds(i, 1), :].rearrange("p a d -> p (a d)")
                    tstep(nc.vector.tensor_copy(h_tile, h_i))
                    with dve.Fori(0, SLOTS // RING) as j:
                        for r in range(RING):
                            dve.wait_ge(row_in[r].sem, ((tile * 2) * (SLOTS // RING) + j + 1) * 16)
                            nc.vector.tensor_tensor_reduce(
                                out=rows[:, r, :], in0=rows[:, r, :], in1=h_tile, scale=1.0, scalar=0.0, op0=ALU.mult,
                                op1=ALU.add, accum_out=dots[:, r:r + 1]).then_inc(row_used.sem, 1)
                        dve.wait_ge(row_used.sem, (tile * 2) * SLOTS + (j + 1) * RING + RING)
                        nc.vector.tensor_copy(dot[:, bass.ds(j * RING, RING)], dots[:]).then_inc(dots_kept.sem, 1)
                        dve.wait_ge(dots_kept.sem, tile * (SLOTS // RING) + j + 1)
                        settle(dve, dve_passed)
                    nc.vector.memset(acc2, 0.0).then_inc(dots_done.sem, 1)
                    dve.wait_ge(gelu_done.sem, tile + 1)
                    tstep(nc.vector.tensor_tensor(wgt[:], gate[:].rearrange("p h k -> p (h k)"), act_g[:], ALU.mult))
                    with dve.Fori(0, SLOTS // RING) as j:
                        for r in range(RING):
                            slot = (tile * 2 + 1) * SLOTS + j * RING + r
                            dve.wait_ge(row_in[r].sem, ((tile * 2 + 1) * (SLOTS // RING) + j + 1) * 16)
                            dve.wait_ge(row_used.sem, slot + RING - 1)
                            s = acc2 if r % 2 else acc_i
                            nc.vector.scalar_tensor_tensor(
                                out=s, in0=rows[:, r, :], scalar=wgt[:, bass.ds(j * RING + r, 1)], in1=s,
                                op0=ALU.mult, op1=ALU.add).then_inc(row_used.sem, 1)
                    dve.wait_ge(row_used.sem, (tile * 2 + 2) * SLOTS + RING)
                    tstep(nc.vector.tensor_tensor(h_i, acc_i, acc2, ALU.add))
                    assert count[0] == TILE_STEPS, count[0]
                dve_step.made += NT * TILE_STEPS
                pr.need(ln2_in, 32)
                norm(step, root, lambda ins: pr.mark(ins, h_ready))
                pr.need(h_ready, 2 * NT)

            dve.wait_ge(h_ready.sem, NT + DEPTH * 2 * NT)

        @block.sync
        def _(sp):
            sp.wait_ge(h_ready.sem, NT + DEPTH * 2 * NT)
            sp.dma_start(out.rearrange("(i p) d -> p i d", p=P), h[:]).then_inc(out_sent.sem, 16)
            sp.wait_ge(out_sent.sem, 16)

        for name, s in names:
            if s.made and s.made != s.per_layer:
                raise AssertionError(f"{name}: {s.made} a layer, not {s.per_layer}")


def constants():
    import numpy as np
    r = np.arange(P)
    ident = np.eye(P)
    causal = np.where(r[None, :] <= r[:, None], 0.0, MASK)
    iota = np.tile(np.arange(64), (P, 1))
    s, t = r[:, None], r[None, :]
    levels = [s == t]
    for lev in range(1, LEVELS):
        m = 2 ** (lev - 1)
        levels.append((s // (2 * m) == t // (2 * m)) & (s % (2 * m) < m) & (t % (2 * m) >= m))
    starts = np.tile((np.arange(T) % P != 0), (P, 1))
    return np.ascontiguousarray(np.concatenate([ident, causal, iota] + levels + [starts], axis=1).astype(np.float32))


def kernel(**inputs):
    import numpy as np
    import concourse.bacc as bacc
    from concourse.bass_utils import run_bass_kernel_spmd as run

    a = {k: np.asarray(val) for k, val in inputs.items()}
    depth = a["w_in"].shape[0]
    arrays = {
        "x": a["x"][0],
        "pT": a["p"][:, 0].transpose(0, 2, 1),
        "emb_g": a["emb_ln_g"], "emb_b": a["emb_ln_b"],
        "w_in": a["w_in"], "fox_fb": a["fox_fb"], "fox_g": a["fox_norm_g"],
        "lbl": a["hg_lb_logits"].reshape(depth, HH, HD).transpose(2, 0, 1),
        "hg_g": a["hg_norm_g"], "w_out": a["w_out"], "ln1_g": a["ln1_g"], "ln1_b": a["ln1_b"],
        "wq": a["peer_wq"],
        "keysT": a["peer_keys"].reshape(depth, 2 * PH, NK, P).transpose(0, 3, 1, 2),
        "u": a["peer_u"], "v": a["peer_v"], "gate_w": a["ple_gate_w"], "ple_w": a["ple_w"],
        "ln2_g": a["ln2_g"], "ln2_b": a["ln2_b"], "consts": constants(),
    }
    nc = bacc.Bacc("TRN2", target_bir_lowering=False, num_devices=1)
    nc.disable_value_cache = True
    feed, args = {}, {}
    for name, val in arrays.items():
        val = np.ascontiguousarray(val)
        feed[f"in_{name}"] = val
        args[name] = nc.dram_tensor(f"in_{name}", val.shape, mybir.dt.from_np(val.dtype), kind="ExternalInput").ap()
    args["out"] = nc.dram_tensor("out_h", (T, D), F32, kind="ExternalOutput").ap()
    build(nc, **args)
    r = run(nc, [feed], core_ids=[0])
    return r.results[0]["out_h"].reshape(1, T, D)
```

```python
from contextlib import ExitStack

import concourse.bass as bass
from concourse import mybir

P = 128
T = 512
D = 1024
NT = T // P
NC = D // P
FH, FD = 8, 64
FW = FH * FD
HH, HD = 4, 128
HW = HH * HD
IN_COLS = 3 * FW + FH + 4 * HW
PH, NK, TOPK = 8, 128, 16
NE = NK * NK
SLOTS = PH * TOPK
PLE = 256
BANKS = 8
PANEL = 512
GROUP = 4
UPANELS = NK // GROUP
CHUNK = 4
TB = P // 4
BLOCKS = T // TB
PAIR = 2
LEVELS = 8
STAIR = [TOPK // (a + 1) for a in range(TOPK)]
CAND = sum(STAIR)
LN_EPS, RMS_EPS, LB_FLOOR, MASK = 1e-5, 1e-6, 1e-30, -1e30
LN_SPLIT = 2.0 ** 60

ALU = mybir.AluOpType
ACT = mybir.ActivationFunctionType
F32 = mybir.dt.float32
BF16 = mybir.dt.bfloat16
F32R = mybir.dt.float32r
U32 = mybir.dt.uint32
AX_X = mybir.AxisListType.X


class Signal:

    def __init__(self, sem, per_layer, before=0):
        self.sem, self.per_layer, self.before, self.made = sem, per_layer, before, 0


def build(nc, x, pT, emb_g, emb_b, w_in, fox_fb, fox_g, lbl, hg_g, w_out, ln1_g, ln1_b,
          wq, keysT, u, v, gate_w, ple_w, ln2_g, ln2_b, consts, out):
    DEPTH = w_in.shape[0]
    ALPHA = (2 * DEPTH) ** 0.25
    SCALE = FD ** -0.5
    act_dram = nc.dram_tensor("act_scratch", (DEPTH, UPANELS, P, GROUP * T), F32).ap()
    gate_dram = nc.dram_tensor("gate_scratch", (DEPTH, BLOCKS, P, NK, TB), F32).ap()

    c0 = 3 * FW + FH
    PANELS = [(w_in, c0 + HW), (w_in, c0), (w_in, 0), (w_in, FW), (w_in, 2 * FW),
              (w_in, c0 + 2 * HW), (w_in, c0 + 3 * HW),
              (w_out, 0), (w_out, PANEL)] + [(wq, PANEL * j) for j in range(4)] + \
             [(None, None)] * UPANELS + [(gate_w, 0), (gate_w, PANEL), (ple_w, None)] + [(None, None)] * UPANELS
    K_WQ, K_U = 9, 13
    K_GATE = K_U + UPANELS
    K_PLE, K_V = K_GATE + 2, K_GATE + 3

    with ExitStack() as ctx:
        def sb(name, shape, dt=F32):
            return ctx.enter_context(nc.sbuf_tensor(name, shape, dt))

        names = []

        def sig(name, per_layer, before=0):
            s = Signal(ctx.enter_context(nc.semaphore(name)), per_layer, before)
            names.append((name, s))
            return s

        ps = ctx.enter_context(nc.psum_tensor("ps", [P, BANKS, 512], F32))

        h = sb("h", [P, NT, D])
        hT = sb("hT", [P, NC, T])
        panel = sb("panel", [P, 2, NC, PANEL])
        wff = sb("wff", [P, NC, FH])
        lng = sb("lng", [P, 2, D])
        ng = sb("ng", [P, 2, 512])
        pTs = sb("pTs", [P, 2, T])
        cst = sb("cst", [P, consts.shape[1]])
        cb = sb("cb", [P, 2 * P], BF16)
        with ExitStack() as shared:
            def half(name, n):
                return shared.enter_context(nc.sbuf_tensor(name, [P, n], F32R))
            wide_hi, wide_lo = half("wide_hi", NC * T), half("wide_lo", NC * T)
            slim_hi, slim_lo = half("slim_hi", GROUP * T), half("slim_lo", GROUP * T)
        arena = sb("arena", [P, 25600])
        work = sb("work", [P, 2048])
        negc = sb("negc", [FH, T])
        ff_bias = sb("ff_bias", [FH, 1])
        stat = sb("stat", [P, NT, 12])
        mv = sb("mv", [P, NT, 2])
        rstd = sb("rstd", [P, NT])

        ident = cst[:, 0:128]
        cmask = cst[:, 128:256]
        iota = cst[:, 256:384]
        level_mask = cst[:, 384:384 + LEVELS * P]
        reset = cst[:, 1408:1408 + T]
        ident_b, cmask_b = cb[:, 0:128], cb[:, 128:256]

        def part(at, *shape):
            n = 1
            for s in shape:
                n *= s
            ap = arena[:, at:at + n]
            if len(shape) == 2:
                return ap.rearrange("p (a b) -> p a b", b=shape[1])
            if len(shape) == 3:
                return ap.rearrange("p (a b c) -> p a b c", b=shape[1], c=shape[2])
            return ap

        fqT = part(0, 4, T)
        fkT = part(2048, 4, T)
        fv = part(4096, NT, FW)
        QE = part(0, LEVELS - 1, T)
        KE = part(3584, LEVELS - 1, T)
        gt = [part(2048 * j, HH, T) for j in range(3)]
        hqT = part(7168, HH, T)
        kT = part(9216, HH, T)
        b = part(11264, HH, T)
        hi = part(13312, NT, HW)
        silu = part(15360, NT, HW)
        qe = part(17408, HH, T)
        kd = part(19456, HH, T)
        mix = part(21504, NT, D)
        pqT = part(0, 2 * PH, T)
        keys_s = part(8192, 2 * PH, NK)
        scores_all = part(12288, NT, 2 * PH * NK)
        score = lng[:].rearrange("p a (b n) -> p (a b) n", n=NK)
        h_hi, h_lo = (w[:].rearrange("p (c t) -> p c t", c=NC) for w in (wide_hi, wide_lo))
        u_hi, u_lo = (w[:].rearrange("p (b c n) -> p b c n", b=2, c=NC) for w in (slim_hi, slim_lo))
        v_hi, v_lo = (w[:].rearrange("p (g d) -> p g d", g=GROUP) for w in (wide_hi, wide_lo))
        w_hi, w_lo = (w[:].rearrange("p (g t) -> p g t", g=GROUP) for w in (slim_hi, slim_lo))
        gmat = arena[:, 12288:20480].rearrange("p (b i t) -> p b i t", b=2, i=NK)
        gact = arena[:, 20480:22528].rearrange("p (g t) -> p g t", g=GROUP)
        tabT = part(22528, 3, T)
        top = part(24064, 2 * PH, TOPK)
        top_i = part(24320, 2 * PH, TOPK)
        top_u = arena[:, 24576:24832].bitcast(U32).rearrange("p (a k) -> p a k", k=TOPK)
        acc = part(12288, NT, D)
        wact = arena[:, 16384:20480].rearrange("p (b g t) -> p b g t", b=2, g=GROUP)
        gin = arena[:, 20480:24576].rearrange("p (b j g t) -> p b j g t", b=2, j=BLOCKS, g=GROUP)
        cand_s = work[:, 0:PH * CAND].rearrange("p (h c) -> p h c", c=CAND)
        cand_i = work[:, 400:400 + PH * CAND].rearrange("p (h c) -> p h c", c=CAND)
        pick = work[:, 800:800 + TOPK * CAND].rearrange("p (k c) -> p k c", c=CAND)
        hot1 = work[:, 0:1024].rearrange("p (b c n) -> p b c n", b=2, c=CHUNK)
        hot2 = work[:, 1024:2048].rearrange("p (b c n) -> p b c n", b=2, c=CHUNK)
        probs = work[:, 0:1024].rearrange("p (a n) -> p a n", a=2)
        probsT = work[:, 1024:2048].rearrange("p (a n) -> p a n", a=2)
        AT = work[:, 0:2048].rearrange("p (a l n) -> p a l n", a=2, n=P)

        ffw = work[0:FH, 0:3 * T].rearrange("p (a t) -> p a t", a=3)

        nmax = sb("nmax", [P, 2])
        psum_p = sb("psum_p", [P, 4])
        rinv = sb("rinv", [P, 2])
        state = sb("state", [P, HH, HD])
        kdT = sb("kdT", [P, 2, P])
        eblast = sb("eblast", [P, HH * NT])
        ssq = sb("ssq", [P, 16])
        lb_in = sb("lb_in", [P, DEPTH, HH])
        lb_all = sb("lb_all", [P, DEPTH, HH])
        lb_t = sb("lb_t", [P, 2, HH])
        lb = sb("lb", [P, 2, HH])
        sel_s = sb("sel_s", [P, PH, TOPK])
        sel_u = sb("sel_u", [P, PH, TOPK], U32)
        sel_p = sb("sel_p", [P, PH, TOPK])
        expert = sb("expert", [P, SLOTS])
        exp_u = sb("exp_u", [P, 2, SLOTS], U32)
        table = sb("table", [P, 3, SLOTS])
        gate = table[:, 2, :].rearrange("p (h k) -> p h k", k=TOPK)
        gate_e = sb("gate_e", [P, PH, TOPK])
        gsum = sb("gsum", [P, 2, PH])
        hot_s = sb("hot_s", [P, 2, 3, CHUNK])

        dve_passed = sig("dve_passed", 0)
        pe_passed = sig("pe_passed", 0)
        const_in = sig("const_in", 0, 16)
        x_in = sig("x_in", 0, 16)
        emb_in = sig("emb_in", 0, 32)
        lb_loaded = sig("lb_loaded", 0, 16)
        ff_in = sig("ff_in", 32)
        gains_in = sig("gains_in", 32)
        ln1_in = sig("ln1_in", 32)
        ln2_in = sig("ln2_in", 32)
        pT_in = sig("pT_in", 16)
        keys_in = sig("keys_in", 16)
        panel_in = [sig(f"panel_in{s}", 16 * len(PANELS) // 2) for s in range(2)]
        h_ready = sig("h_ready", 2 * NT, NT)
        lb_shift = sig("lb_shift", 0, 1)
        lb_exp = sig("lb_exp", 0, 1)
        var_ready = sig("var_ready", 4, 1)
        root_ready = sig("root_ready", 4, 1)
        casts = sig("casts", 0, 2)
        dve_step = sig("dve_step", 269, 15)
        act_step = sig("act_step", 1)
        turned = sig("turned", 3 * NC)
        hT_act = sig("hT_act", 3 * NC // 2)
        hT_dve = sig("hT_dve", 3 * NC // 2)
        projected = sig("projected", 29)
        ff_z = sig("ff_z", 1)
        ff_e = sig("ff_e", 1)
        negc_ready = sig("negc_ready", 1)
        hf_ready = sig("hf_ready", HH)
        hf_exp = sig("hf_exp", HH)
        f_ready = sig("f_ready", 1)
        f_log = sig("f_log", 1)
        b_ready = sig("b_ready", 1)
        b_exp = sig("b_exp", 1)
        d_exp = sig("d_exp", 1)
        hdec_ready = sig("hdec_ready", 1)
        qk_ready = sig("qk_ready", 12)
        v_ready = sig("v_ready", 8)
        hg_sig = sig("hg_sig", NT)
        silu_ready = sig("silu_ready", NT)
        NS = FH * NT
        scored = sig("scored", NS)
        nmax_ready = sig("nmax_ready", NS)
        probs_ready = sig("probs_ready", NS)
        probs_turned = sig("probs_turned", NS)
        probsT_ready = sig("probsT_ready", NS)
        pv_done = sig("pv_done", NS)
        fox_out = sig("fox_out", NS)
        lev_ready = sig("lev_ready", HH)
        lev_exp = sig("lev_exp", HH)
        lev_mul = sig("lev_mul", HH)
        a_done = sig("a_done", 2 * HH * NT)
        at_ready = sig("at_ready", 2 * HH * NT)
        o_done = sig("o_done", HH * NT)
        o_out = sig("o_out", HH * NT)
        kd_turned = sig("kd_turned", HH * (NT - 1))
        kdT_ready = sig("kdT_ready", HH * (NT - 1))
        u_done = sig("u_done", HH * (NT - 1))
        state_ready = sig("state_ready", HH * (NT - 1))
        mix_ready = sig("mix_ready", 2)
        outed = sig("outed", 8)
        pre1 = sig("pre1", 8)
        queried = sig("queried", 16)
        pq_act = sig("pq_act", 8)
        pq_dve = sig("pq_dve", 8)
        key_scored = sig("key_scored", 16)
        score_sb = sig("score_sb", 16)
        gated = sig("gated", 8)
        gate_sig = sig("gate_sig", 8)
        pled = sig("pled", 8)
        ple_mul = sig("ple_mul", 8)
        acc_init = sig("acc_init", 8)
        routed = sig("routed", NT)
        sel_shift = sig("sel_shift", NT)
        sel_exp = sig("sel_exp", NT)
        SEGS = [0, 1, 3, 5, 7, 8]
        NG = T // CHUNK
        table_ready = sig("table_ready", NT)
        table_turned = sig("table_turned", NT, 1)
        tab_ready = sig("tab_ready", NT)
        hot_step = sig("hot_step", NG)
        a_full = sig("a_full", NK)
        gelu_done = sig("gelu_done", NK, GROUP)
        h_split = sig("h_split", 2)
        u_hi_ready = sig("u_hi_ready", NK)
        u_lo_ready = sig("u_lo_ready", NK)
        act_out = [sig(f"act_out{r}", 16 * UPANELS, 16) for r in range(2)]
        hot_ready = sig("hot_ready", NG)
        g_full = sig("g_full", NG, 2)
        g_kept = sig("g_kept", NG, 4)
        g_out = [sig(f"g_out{r}", 16 * BLOCKS // 2, 16) for r in range(2)]
        act_in = [sig(f"act_in{r}", 16 * UPANELS // 2) for r in range(2)]
        gate_in = [sig(f"gate_in{r}", 16 * UPANELS // 2) for r in range(2)]
        w_ready = sig("w_ready", UPANELS)
        v_hi_ready = sig("v_hi_ready", NK)
        v_lo_ready = sig("v_lo_ready", NK, 1)
        w_hi_ready = sig("w_hi_ready", NK)
        w_lo_ready = sig("w_lo_ready", NK)
        y_done = sig("y_done", NK, GROUP)
        y_added = sig("y_added", 8)
        out_sent = sig("out_sent", 0, 16)

        block = ctx.enter_context(nc.Block())

        def settle(eng, passed):
            eng.sem_inc(passed.sem, 1)

        class Program:

            def __init__(self, eng, layer):
                self.eng, self.layer = eng, layer

            def need(self, s, n):
                self.eng.wait_ge(s.sem, self.layer * s.per_layer + (s.before + n))

            def mark(self, ins, s, n=1):
                ins.then_inc(s.sem, n)
                s.made += n
                return s.made

            def link(self, ins, s):
                self.need(s, self.mark(ins, s))

        G_T1 = 0
        G_PROJ = G_T1 + NC
        G_FOX = G_PROJ + 29
        G_HG = G_FOX + 3 * NS
        G_T2 = G_HG + 4 * HH * NT + 2 * HH * (NT - 1) - HH * NT
        G_OUT = G_T2 + NC
        G_T3 = G_OUT + 8
        G_Q = G_T3 + NC
        G_PLE = 0

        def bank(g):
            return ps[:, g % BANKS, :]

        def fox_group(kind, s):
            g = G_FOX
            for st in range(NS + 2):
                for k in range(3):
                    q = st - k
                    if 0 <= q < NS:
                        if (k, q) == (kind, s):
                            return g
                        g += 1

        def hg_group(kind, j):
            g = G_HG
            for jj in range(HH * NT):
                for k in (0, 1, 3, 2, 4):
                    if k >= 3 and jj % NT == NT - 1:
                        continue
                    if (k, jj) == (kind, j):
                        return g
                    g += 1

        @block.sync
        def _(sp):
            sp.dma_start(cst[:], consts).then_inc(const_in.sem, 16)
            sp.dma_start(h[:], x.rearrange("(i p) d -> p i d", p=P)).then_inc(x_in.sem, 16)
            sp.dma_start(lb_in[:], lbl).then_inc(lb_loaded.sem, 16)
            for k, a in enumerate((emb_g, emb_b)):
                sp.dma_start(lng[:, k, :], a.partition_broadcast(P)).then_inc(emb_in.sem, 16)
            with sp.Fori(0, DEPTH) as layer:
                pr = Program(sp, layer)
                at = bass.ds(layer, 1)

                def load_panel(k, n=None):
                    w, col = PANELS[k]
                    if w is None:
                        src = (u if k < K_GATE else v)[at, bass.ds(n, 1)].rearrange("l n p c -> p (l n c)")
                        dst = panel[:, k % 2].rearrange("p c n -> p (c n)")
                    elif col is None:
                        src = w[at].rearrange("l (c p) n -> p (l c) n", p=P)
                        dst = panel[:, k % 2, 0:2 * PLE // P, :].rearrange("p (c a) n -> p c (a n)", c=PLE // P)
                    else:
                        src = w[at, :, col:col + PANEL].rearrange("l (c p) n -> p (l c) n", p=P)
                        dst = panel[:, k % 2]
                    sp.dma_start(dst, src).then_inc(panel_in[k % 2].sem, 16)

                def row(a):
                    return a[at].rearrange("l d -> (l d)").partition_broadcast(P)

                pr.need(v_lo_ready, 0)
                load_panel(0)
                pr.mark(sp.dma_start(wff[:], w_in[at, :, 3 * FW:3 * FW + FH].rearrange("l (c p) n -> p (l c) n", p=P)),
                        ff_in, 16)
                pr.mark(sp.dma_start(ff_bias[:], fox_fb[at].rearrange("l h -> h l")), ff_in, 16)
                load_panel(1)
                for k, a in enumerate((fox_g, hg_g)):
                    pr.mark(sp.dma_start(ng[:, k, :], row(a)), gains_in, 16)
                pr.mark(sp.dma_start(pTs[:], pT[at].rearrange("l (c p) t -> p (l c) t", p=P)), pT_in, 16)
                pr.need(h_ready, 0)
                for k, a in enumerate((ln1_g, ln1_b)):
                    pr.mark(sp.dma_start(lng[:, k, :], row(a)), ln1_in, 16)
                for k in range(2, 9):
                    pr.need(projected, 1 + 4 * (k - 1))
                    load_panel(k)
                for k in range(9, 11):
                    pr.need(outed, 4 * (k - 8))
                    load_panel(k)
                pr.need(h_ready, NT)
                pr.mark(sp.dma_start(keys_s, keysT[at].rearrange("l d a n -> d (l a) n")), keys_in, 16)
                for k in range(11, K_U + 2):
                    pr.need(queried, 4 * (k - 10))
                    load_panel(k, k - K_U)
                with sp.Fori(1, UPANELS // 2) as q:
                    for r in range(2):
                        sp.wait_ge(u_lo_ready.sem, layer * NK + (q * 2 + r - 1) * GROUP)
                        load_panel(K_U + r, q * 2 + r)
                for k in range(K_GATE, K_GATE + 2):
                    pr.need(u_lo_ready, GROUP * (UPANELS - 1 + k - K_GATE))
                    load_panel(k)
                pr.need(routed, NT)
                for k, a in enumerate((ln2_g, ln2_b)):
                    pr.mark(sp.dma_start(lng[:, k, :], row(a)), ln2_in, 16)
                pr.need(gated, 4)
                load_panel(K_PLE)
                pr.need(gated, 8)
                load_panel(K_V, 0)
                pr.need(pled, 8)
                load_panel(K_V + 1, 1)
                with sp.Fori(1, UPANELS // 2) as q:
                    for r in range(2):
                        sp.wait_ge(v_lo_ready.sem, layer * NK + ((q * 2 + r - 1) * GROUP + v_lo_ready.before))
                        load_panel(K_V + r, q * 2 + r)

        @block.tensor
        def _(pe):
            pe.wait_ge(const_in.sem, 16)
            pe.wait_ge(casts.sem, 2)
            pe.sem_inc(y_done.sem, y_done.before)
            pe.sem_inc(g_full.sem, g_full.before)
            pe.sem_inc(table_turned.sem, table_turned.before)
            with pe.Fori(0, DEPTH) as layer:
                pr = Program(pe, layer)
                freed = []

                def take(g, release):
                    assert g == len(freed), (g, len(freed))
                    if g >= BANKS:
                        pr.need(*freed[g - BANKS])
                    freed.append(release)
                    return bank(g)

                def turn(src, g0, n):
                    for c in range(NC):
                        o = take(g0 + c, ((hT_act, hT_dve)[c % 2], (n * NC + c) // 2 + 1))
                        for i in range(NT):
                            mm = nc.tensor.transpose(o[:, i * P:(i + 1) * P], src[:, i, c * P:(c + 1) * P], ident)
                        pr.mark(mm, turned)
                    pr.need(hT_act, (n + 1) * NC // 2)
                    pr.need(hT_dve, (n + 1) * NC // 2)

                def columns(o, w, m):
                    for c in range(NC):
                        mm = nc.tensor.matmul(o, w[:, c, m * P:(m + 1) * P], hT[:, c, :],
                                              start=(c == 0), stop=(c == NC - 1))
                    return mm

                def tokens(o, w, i):
                    for c in range(NC):
                        mm = nc.tensor.matmul(o, hT[:, c, i * P:(i + 1) * P], w[:, c, :],
                                              start=(c == 0), stop=(c == NC - 1))
                    return mm

                def loaded(k):
                    pr.need(panel_in[k % 2], 16 * (k // 2 + 1))
                    return panel[:, k % 2]

                pr.need(h_ready, 0)
                turn(h, G_T1, 0)
                pr.need(ff_in, 32)
                g = G_PROJ
                o = take(g, (ff_z, 1))
                for c in range(NC):
                    mm = nc.tensor.matmul(o[0:FH, :], wff[:, c, :], hT[:, c, :], start=(c == 0), stop=(c == NC - 1))
                pr.mark(mm, projected)
                for k in range(7):
                    w = loaded(k)
                    for m in range(4):
                        g += 1
                        release = [(hf_ready, m + 1), (qk_ready, m + 1), (qk_ready, 5 + m), (qk_ready, 9 + m),
                                   (v_ready, m + 1), (v_ready, 5 + m), (silu_ready, m + 1)][k]
                        o = take(g, release)
                        pr.mark(columns(o, w, m) if k < 4 else tokens(o, w, m), projected)

                pr.need(negc_ready, 1)
                pr.need(qk_ready, 12)
                pr.need(v_ready, 4)
                for st in range(NS + 2):
                    if st < NS:
                        hd, i = st // NT, st % NT
                        n = (i + 1) * P
                        o = take(fox_group(0, st), (probs_ready, st + 1))
                        rows_ = slice(FD * (hd % 2), FD * (hd % 2) + FD)
                        nc.tensor.matmul(o[:, 0:n], fqT[rows_, hd // 2, i * P:(i + 1) * P], fkT[rows_, hd // 2, 0:n],
                                         start=True, stop=False)
                        nc.tensor.matmul(o[:, 0:n], ident[0:FH, hd:hd + 1].to_broadcast([FH, P]), negc[:, 0:n],
                                         start=False, stop=False)
                        pr.mark(nc.tensor.matmul(o[:, n - P:n], ident_b, cmask_b, start=False, stop=True), scored)
                    if 0 <= st - 1 < NS:
                        s = st - 1
                        i = s % NT
                        o = take(fox_group(1, s), (probsT_ready, s + 1))
                        pr.need(probs_ready, s + 1)
                        for j in range(i + 1):
                            mm = nc.tensor.transpose(o[:, j * P:(j + 1) * P], probs[:, s % 2, j * P:(j + 1) * P], ident)
                        pr.mark(mm, probs_turned)
                    if 0 <= st - 2:
                        s = st - 2
                        hd, i = s // NT, s % NT
                        o = take(fox_group(2, s), (fox_out, s + 1))
                        pr.need(probsT_ready, s + 1)
                        for j in range(i + 1):
                            mm = nc.tensor.matmul(o[:, 0:FD], probsT[:, s % 2, j * P:(j + 1) * P],
                                                  fv[:, j, hd * FD:(hd + 1) * FD], start=(j == 0), stop=(j == i))
                        pr.mark(mm, pv_done)

                pr.need(hdec_ready, 1)
                pr.need(v_ready, 8)
                for j in range(HH * NT):
                    hd, i = j // NT, j % NT
                    toks = slice(i * P, (i + 1) * P)
                    if i == 0:
                        pr.need(lev_mul, hd + 1)
                    for half in range(2):
                        o = take(hg_group(half, j), (at_ready, 2 * j + half + 1))
                        for k in range(4):
                            lev = 4 * half + k
                            kk = kT[:, hd, toks] if lev == 0 else KE[:, lev - 1, toks]
                            qq = hqT[:, hd, toks] if lev == 0 else QE[:, lev - 1, toks]
                            mm = nc.tensor.matmul(o[:, k * P:(k + 1) * P], kk, qq, start=True, stop=True)
                        pr.mark(mm, a_done)
                    up = hd * (NT - 1) + i
                    if i < NT - 1:
                        o = take(hg_group(3, j), (kdT_ready, up + 1))
                        pr.mark(nc.tensor.transpose(o[:, 0:P], kd[:, hd, toks], ident), kd_turned)
                    o = take(hg_group(2, j), (o_out, j + 1))
                    vv = hi[:, i, hd * HD:(hd + 1) * HD]
                    if i > 0:
                        pr.need(state_ready, up)
                        nc.tensor.matmul(o[:, 0:HD], qe[:, hd, toks], state[:, hd, :], start=True, stop=False)
                    pr.need(at_ready, 2 * j + 2)
                    for lev in range(LEVELS):
                        mm = nc.tensor.matmul(o[:, 0:HD], AT[:, j % 2, lev, :], vv,
                                              start=(lev == 0 and i == 0), stop=(lev == LEVELS - 1))
                    pr.mark(mm, o_done)
                    if i < NT - 1:
                        o = take(hg_group(4, j), (state_ready, up + 1))
                        pr.need(kdT_ready, up + 1)
                        pr.mark(nc.tensor.matmul(o[:, 0:HD], kdT[:, up % 2, :], vv, start=True, stop=True), u_done)

                pr.need(mix_ready, 2)
                turn(mix, G_T2, 1)
                for half in range(2):
                    w = loaded(7 + half)
                    for i in range(NT):
                        o = take(G_OUT + 4 * half + i, (pre1, 4 * half + i + 1))
                        pr.mark(tokens(o, w, i), outed)

                pr.need(h_ready, NT)
                turn(h, G_T3, 2)
                for k in range(4):
                    w = loaded(9 + k)
                    for m in range(4):
                        g = 4 * k + m
                        o = take(G_Q + g, ((pq_act, pq_dve)[g % 2], g // 2 + 1))
                        pr.mark(columns(o, w, m), queried)

                pr.need(keys_in, 16)
                pr.need(pq_act, 8)
                pr.need(pq_dve, 8)

                for i in range(NT):
                    for k in range(4):
                        if 4 * i + k >= BANKS:
                            pr.need(score_sb, 4 * i + k - BANKS + 1)
                        for a in range(4):
                            mm = nc.tensor.matmul(bank(4 * i + k)[:, a * NK:(a + 1) * NK],
                                                  pqT[:, 4 * k + a, i * P:(i + 1) * P],
                                                  keys_s[:, 4 * k + a, :], start=True, stop=True)
                        pr.mark(mm, key_scored)

                def first_products(q, r, g):
                    tile = q * (2 * GROUP) + (r * GROUP + g + 1)
                    pe.wait_ge(u_lo_ready.sem, layer * NK + tile)
                    pe.wait_ge(gelu_done.sem, layer * NK + tile)
                    for c in range(NC):
                        for k, (uu, hh) in enumerate(((u_lo, h_hi), (u_hi, h_lo), (u_hi, h_hi))):
                            mm = nc.tensor.matmul(bank(g), uu[:, g % 2, c, :], hh[:, c, :], start=(c + k == 0),
                                                  stop=(c == NC - 1 and k == 2))
                    mm.then_inc(a_full.sem, 1)

                def turn_table(i):
                    pr.need(table_ready, i + 1)
                    if i > 0:
                        pr.need(tab_ready, i)
                    for k in range(3):
                        mm = nc.tensor.transpose(bank(4)[:, k * P:(k + 1) * P], table[:, k, :], ident)
                    pr.mark(mm, table_turned)

                pr.need(score_sb, 4 * NT)
                pr.need(h_split, 2)
                settle(pe, pe_passed)
                for seg in range(len(SEGS) - 1):
                    with pe.Fori(SEGS[seg], SEGS[seg + 1]) as q:
                        for r in range(2):
                            for g in range(GROUP):
                                first_products(q, r, g)
                    if seg > 0:
                        turn_table(seg - 1)
                pr.need(tab_ready, NT)
                settle(pe, pe_passed)
                with pe.Fori(SEGS[-1], UPANELS // 2) as q:
                    for r in range(2):
                        for g in range(GROUP):
                            first_products(q, r, g)
                            for k in range(2 * g, 2 * g + 2):
                                chunk = layer * NG + (q - SEGS[-1]) * 16 + (r * 8 + k)
                                pe.wait_ge(hot_ready.sem, chunk + 1)
                                pe.wait_ge(g_kept.sem, chunk + 1)
                                for c in range(CHUNK):
                                    mm = nc.tensor.matmul(bank(4 + k % 4)[:, c * NK:(c + 1) * NK],
                                                          hot1[:, k % 2, c, :], hot2[:, k % 2, c, :],
                                                          start=True, stop=True)
                                mm.then_inc(g_full.sem, 1)

                pr.need(gelu_done, NK)
                pr.need(g_kept, NG)
                pr.need(pT_in, 16)
                freed.clear()
                for half in range(2):
                    w = loaded(K_GATE + half)
                    for i in range(NT):
                        o = take(G_PLE + 4 * half + i, (gate_sig, 4 * half + i + 1))
                        pr.mark(tokens(o, w, i), gated)
                loaded(K_PLE)
                wp = panel[:, K_PLE % 2, 0:4, :].rearrange("p (c a) n -> p c (a n)", c=2)
                for half in range(2):
                    for i in range(NT):
                        o = take(G_PLE + 8 + 4 * half + i, (ple_mul, 4 * half + i + 1))
                        for c in range(2):
                            mm = nc.tensor.matmul(o, pTs[:, c, i * P:(i + 1) * P],
                                                  wp[:, c, half * 512:(half + 1) * 512], start=(c == 0), stop=(c == 1))
                        pr.mark(mm, pled)

                def second_products(q, r, start=False, stop=False):
                    for g in range(GROUP):
                        tile = layer * NK + q * (2 * GROUP) + (r * GROUP + g + 1)
                        pe.wait_ge(v_lo_ready.sem, tile + v_lo_ready.before)
                        pe.wait_ge(w_lo_ready.sem, tile)
                        for k in range(BANKS):
                            i, half = k // 2, k % 2
                            for n, (ww, vv) in enumerate(((w_lo, v_hi), (w_hi, v_lo), (w_hi, v_hi))):
                                mm = nc.tensor.matmul(bank(k), ww[:, g, i * P:(i + 1) * P],
                                                      vv[:, g, half * 512:(half + 1) * 512],
                                                      start=(start and g + n == 0),
                                                      stop=(stop and g == GROUP - 1 and n == 2))
                        mm.then_inc(y_done.sem, 1)

                pr.need(ple_mul, 8)
                second_products(0, 0, start=True)
                second_products(0, 1)
                with pe.Fori(1, UPANELS // 2 - 1) as q:
                    for r in range(2):
                        second_products(q, r)
                second_products(UPANELS // 2 - 1, 0)
                second_products(UPANELS // 2 - 1, 1, stop=True)

        @block.scalar
        def _(act):
            act.sem_inc(gelu_done.sem, gelu_done.before)
            act.sem_inc(g_kept.sem, g_kept.before)
            for r in range(2):
                act.sem_inc(act_out[r].sem, 16)
                act.sem_inc(g_out[r].sem, 16)
            act.wait_ge(lb_shift.sem, 1)
            nc.scalar.activation(lb_in[:], lb_in[:], ACT.Exp).then_inc(lb_exp.sem, 1)
            act.wait_ge(var_ready.sem, 1)
            nc.scalar.activation(rstd[:], rstd[:], ACT.Sqrt).then_inc(root_ready.sem, 1)
            with act.Fori(0, DEPTH) as layer:
                pr = Program(act, layer)

                def turn(g0, n):
                    for c in range(0, NC, 2):
                        pr.need(turned, n * NC + c + 1)
                        pr.mark(nc.scalar.copy(hT[:, c, :], bank(g0 + c)), hT_act)

                def root(n, var):
                    pr.need(var_ready, n)
                    pr.mark(nc.scalar.activation(var, var, ACT.Sqrt), root_ready)

                turn(G_T1, 0)
                pr.need(ff_z, 1)
                pr.link(nc.scalar.activation(ffw[:, 2, :], ffw[:, 1, :], ACT.Exp), act_step)
                pr.mark(nc.scalar.activation(ffw[:, 1, :], ffw[:, 2, :], ACT.Ln, bias=1.0), ff_e)
                for m in range(HH):
                    pr.need(hf_ready, m + 1)
                    pr.mark(nc.scalar.activation(gt[0][:, m, :], gt[0][:, m, :], ACT.Exp), hf_exp)
                for m in range(4):
                    pr.need(projected, 6 + m)
                    pr.mark(nc.scalar.copy(hqT[:, m, :], bank(G_PROJ + 5 + m)), qk_ready)
                pr.need(f_ready, 1)
                nc.scalar.activation(gt[1], gt[1], ACT.Ln)
                pr.mark(nc.scalar.activation(gt[2], gt[2], ACT.Ln), f_log)
                pr.need(b_ready, 1)
                pr.mark(nc.scalar.activation(qe, b, ACT.Exp), b_exp)
                for hd in range(HH):
                    for i in range(NT):
                        last = nc.scalar.activation(kd[:, hd, i * P:(i + 1) * P], b[:, hd, i * P:(i + 1) * P], ACT.Exp,
                                                    scale=-1.0, bias=b[:, hd, (i + 1) * P - 1:(i + 1) * P])
                pr.mark(last, d_exp)
                pr.need(hdec_ready, 1)
                for k, dst in enumerate((fqT, fkT)):
                    for m in range(4):
                        pr.need(projected, 10 + 4 * k + m)
                        pr.mark(nc.scalar.copy(dst[:, m, :], bank(G_PROJ + 9 + 4 * k + m)), qk_ready)
                for i in range(NT):
                    pr.need(projected, 26 + i)
                    pr.mark(nc.scalar.activation(silu[:, i, :], bank(G_PROJ + 25 + i), ACT.Sigmoid), hg_sig)
                for s in range(NS):
                    n = (s % NT + 1) * P
                    pr.need(nmax_ready, s + 1)
                    if s >= 2:
                        pr.need(probs_turned, s - 1)
                        pr.need(fox_out, s - 1)
                    pr.mark(nc.scalar.activation(probs[:, s % 2, 0:n], bank(fox_group(0, s))[:, 0:n], ACT.Exp,
                                                 scale=SCALE, bias=nmax[:, s % 2:s % 2 + 1],
                                                 accum_out=psum_p[:, s % 2:s % 2 + 1]), probs_ready)
                root(1, ssq[:, 0:NT])
                for hd in range(HH):
                    pr.need(lev_ready, hd + 1)
                    pr.mark(nc.scalar.activation(KE, KE, ACT.Exp), lev_exp)
                    for i in range(NT - 1):
                        up = hd * (NT - 1) + i
                        pr.need(kd_turned, up + 1)
                        if up >= 2:
                            pr.need(u_done, up - 1)
                        pr.mark(nc.scalar.copy(kdT[:, up % 2, :], bank(hg_group(3, hd * NT + i))[:, 0:P]), kdT_ready)
                root(2, ssq[:])
                turn(G_T2, 1)
                root(3, rstd[:])
                turn(G_T3, 2)
                for g in range(0, 16, 2):
                    pr.need(queried, g + 1)
                    pr.mark(nc.scalar.copy(pqT[:, g, :], bank(G_Q + g)), pq_act)

                for g in range(4 * NT):
                    pr.need(key_scored, g + 1)
                    pr.mark(nc.scalar.copy(scores_all[:, g // 4, (g % 4) * 512:(g % 4 + 1) * 512], bank(g)), score_sb)
                pr.mark(nc.scalar.copy(h_hi, hT[:]), h_split)

                def split_u(q, r, g):
                    tile = q * (2 * GROUP) + (r * GROUP + g)
                    if g == 0:
                        act.wait_ge(panel_in[(K_U + r) % 2].sem,
                                    layer * (8 * len(PANELS)) + q * 16 + 16 * ((K_U + r) // 2 + 1))
                    raw = panel[:, (K_U + r) % 2].rearrange("p c n -> p (c n)")
                    nc.scalar.copy(u_hi[:, g % 2].rearrange("p c n -> p (c n)"),
                                   raw[:, g * D:(g + 1) * D]).then_inc(u_hi_ready.sem, 1)

                def activations(q, r, g, ahead=True):
                    tile = q * (2 * GROUP) + (r * GROUP + g + 1)
                    act.wait_ge(a_full.sem, layer * NK + tile)
                    if ahead:
                        if g < 2:
                            split_u(q, r, g + 2)
                        else:
                            split_u(q + r, 1 - r, g - 2)
                    if g % PAIR == 0:
                        act.wait_ge(act_out[g // PAIR].sem,
                                    layer * act_out[0].per_layer + q * 32 + (16 * r + 16))
                    nc.scalar.activation(gact[:, g, :], bank(g), ACT.Gelu).then_inc(gelu_done.sem, 1)
                    if g % PAIR == PAIR - 1:
                        act.wait_ge(gelu_done.sem, layer * NK + tile + gelu_done.before)
                        g0 = g - PAIR + 1
                        act.dma_start(act_dram[bass.ds(layer, 1), bass.ds(q * 2 + r, 1), :, g0 * T:(g + 1) * T]
                                      .rearrange("l n p c -> p (l n c)"),
                                      gact[:, g0:g + 1].rearrange("p g t -> p (g t)")
                                      ).then_inc(act_out[g // PAIR].sem, 16)

                def table_by_token(i):
                    pr.need(table_turned, i + 1)
                    pr.mark(nc.scalar.copy(tabT[:, :, i * P:(i + 1) * P],
                                           bank(4)[:, 0:3 * P].rearrange("p (k t) -> p k t", k=3)), tab_ready)

                def exponentials(i):
                    pr.need(sel_shift, i + 1)
                    pr.mark(nc.scalar.activation(gate_e[:], gate_e[:], ACT.Exp), sel_exp)

                split_u(0, 0, 0)
                split_u(0, 0, 1)
                for seg in range(len(SEGS) - 1):
                    with act.Fori(SEGS[seg], SEGS[seg + 1]) as q:
                        for r in range(2):
                            for g in range(GROUP):
                                activations(q, r, g)
                    if seg < NT:
                        exponentials(seg)
                    if seg > 0:
                        table_by_token(seg - 1)

                def gate_blocks(q, last=False):
                    for r in range(2):
                        block_ = (q - SEGS[-1]) * 2 + r
                        for g in range(GROUP):
                            activations(q, r, g, not (last and r == 1 and g >= 2))
                            if g == 0:
                                act.wait_ge(g_out[r].sem, layer * g_out[r].per_layer + (q - SEGS[-1]) * 16 + 16)
                            for k in range(2 * g, 2 * g + 2):
                                chunk = layer * NG + (q - SEGS[-1]) * 16 + (r * 8 + k)
                                act.wait_ge(g_full.sem, chunk + (1 + g_full.before))
                                nc.scalar.copy(gmat[:, r, :, k * CHUNK:(k + 1) * CHUNK],
                                               bank(4 + k % 4).rearrange("p (c n) -> p n c", c=CHUNK)
                                               ).then_inc(g_kept.sem, 1)
                        act.wait_ge(g_kept.sem, layer * NG + (q - SEGS[-1]) * 16 + ((r + 1) * 8 + g_kept.before))
                        act.dma_start(gate_dram[bass.ds(layer, 1), bass.ds(block_, 1)]
                                      .rearrange("l n p a t -> p (l n a t)"),
                                      gmat[:, r].rearrange("p a t -> p (a t)")).then_inc(g_out[r].sem, 16)

                with act.Fori(SEGS[-1], UPANELS // 2 - 1) as q:
                    gate_blocks(q)
                gate_blocks(UPANELS // 2 - 1, last=True)
                for r in range(2):
                    pr.need(act_out[r], act_out[r].per_layer)
                    pr.need(g_out[r], g_out[r].per_layer)

                def fetch(n, r):
                    act.dma_start(wact[:, r].rearrange("p g t -> p (g t)"),
                                  act_dram[bass.ds(layer, 1), bass.ds(n, 1)].rearrange("l n p c -> p (l n c)")
                                  ).then_inc(act_in[r].sem, 16)
                    act.dma_start(gin[:, r].rearrange("p j g t -> p j (g t)"),
                                  gate_dram[bass.ds(layer, 1), :, :, bass.ds(n * GROUP, GROUP), :]
                                  .rearrange("l j p g t -> p (l j) (g t)")).then_inc(gate_in[r].sem, 16)

                for r in range(2):
                    fetch(r, r)
                for g in range(8):
                    half, i = g // 4, g % 4
                    pr.need(gated, g + 1)
                    pr.mark(nc.scalar.activation(acc[:, i, half * 512:(half + 1) * 512], bank(G_PLE + g),
                                                 ACT.Sigmoid), gate_sig)

                def split_v(q, r):
                    act.wait_ge(panel_in[(K_V + r) % 2].sem,
                                layer * (8 * len(PANELS)) + q * 16 + 16 * ((K_V + r) // 2 + 1))
                    raw = panel[:, (K_V + r) % 2].rearrange("p c n -> p (c n)")
                    for g in range(GROUP):
                        act.wait_ge(y_done.sem, layer * NK + q * (2 * GROUP) + (r * GROUP + g + 1))
                        nc.scalar.copy(v_hi[:, g], raw[:, g * D:(g + 1) * D]).then_inc(v_hi_ready.sem, 1)
                        if g == 0:
                            act.wait_ge(w_ready.sem, layer * UPANELS + q * 2 + (r + 1))
                        nc.scalar.copy(w_hi[:, g], wact[:, r, g]).then_inc(w_hi_ready.sem, 1)

                with act.Fori(0, UPANELS // 2 - 1) as q:
                    for r in range(2):
                        split_v(q, r)
                        act.wait_ge(w_lo_ready.sem, layer * NK + q * (2 * GROUP) + (r + 1) * GROUP)
                        fetch(q * 2 + (2 + r), r)
                for r in range(2):
                    split_v(UPANELS // 2 - 1, r)
                root(4, rstd[:])

        @block.gpsimd
        def _(pool):
            pool.sem_inc(v_lo_ready.sem, v_lo_ready.before)
            with pool.Fori(0, DEPTH) as layer:
                for hi_ready, lo_ready, k0, ring, hi_, lo_ in (
                        (u_hi_ready, u_lo_ready, K_U, 2, slim_hi, slim_lo),
                        (v_hi_ready, v_lo_ready, K_V, GROUP, wide_hi, wide_lo)):
                    with pool.Fori(0, UPANELS // 2) as q:
                        for r in range(2):
                            raw = panel[:, (k0 + r) % 2].rearrange("p c n -> p (c n)")
                            for g in range(GROUP):
                                pool.wait_ge(hi_ready.sem, layer * NK + q * (2 * GROUP) + (r * GROUP + g + 1))
                                at = slice(g % ring * D, (g % ring + 1) * D)
                                nc.gpsimd.tensor_tensor(lo_[:, at], raw[:, g * D:(g + 1) * D],
                                                        hi_[:, at].bitcast(F32), ALU.subtract
                                                        ).then_inc(lo_ready.sem, 1)

        @block.vector
        def _(dve):
            before = [0]

            def first(ins):
                ins.then_inc(dve_step.sem, 1)
                before[0] += 1
                dve.wait_ge(dve_step.sem, before[0])

            def norm(src, step, root, signal):
                for i in range(NT):
                    for k in range(2):
                        last = nc.vector.bn_stats(stat[:, i, 6 * k:6 * k + 6], src[:, i, k * 512:(k + 1) * 512])
                step(last)
                for i in range(NT):
                    last = nc.vector.bn_aggr(mv[:, i, :], stat[:, i, :])
                step(last)
                root(nc.vector.tensor_scalar(rstd[:], mv[:, :, 1], LN_EPS, None, ALU.add))
                step(nc.vector.reciprocal(rstd[:], rstd[:]))
                for i in range(NT):
                    last = nc.vector.tensor_scalar(h[:, i, :], src[:, i, :], mv[:, i, 0:1], rstd[:, i:i + 1],
                                                   ALU.subtract, ALU.mult)
                step(last)
                for i in range(NT):
                    last = nc.vector.tensor_tensor(h[:, i, :], h[:, i, :], lng[:, 0, :], ALU.mult)
                step(last)
                for i in range(NT):
                    signal(nc.vector.tensor_tensor(h[:, i, :], h[:, i, :], lng[:, 1, :], ALU.add))

            dve.wait_ge(const_in.sem, 16)
            nc.vector.tensor_copy(ident_b, ident).then_inc(casts.sem, 1)
            nc.vector.tensor_copy(cmask_b, cmask).then_inc(casts.sem, 1)
            dve.wait_ge(lb_loaded.sem, 16)
            first(nc.vector.tensor_copy(lb_t[:, 0, :], lb_in[:, 0, :]))
            for k in range(1, DEPTH):
                first(nc.vector.tensor_tensor(lb_t[:, 0, :], lb_t[:, 0, :], lb_in[:, k, :], ALU.max))
            for k in range(DEPTH):
                last = nc.vector.tensor_tensor(lb_in[:, k, :], lb_in[:, k, :], lb_t[:, 0, :], ALU.subtract)
            last.then_inc(lb_shift.sem, 1)
            dve.wait_ge(lb_exp.sem, 1)
            first(nc.vector.tensor_copy(lb_t[:, 0, :], lb_in[:, 0, :]))
            for k in range(1, DEPTH):
                first(nc.vector.tensor_tensor(lb_t[:, 0, :], lb_t[:, 0, :], lb_in[:, k, :], ALU.add))
            first(nc.vector.reciprocal(lb_t[:, 1, :], lb_t[:, 0, :]))
            for k in range(DEPTH):
                last = nc.vector.tensor_tensor(lb_in[:, k, :], lb_in[:, k, :], lb_t[:, 1, :], ALU.mult)
            first(last)
            first(nc.vector.tensor_copy(lb_all[:, 0, :], lb_in[:, 0, :]))
            for k in range(1, DEPTH):
                first(nc.vector.tensor_tensor(lb_all[:, k, :], lb_all[:, k - 1, :], lb_in[:, k, :], ALU.add))
            first(nc.vector.tensor_copy(lb_t[:, 0, :], lb_in[:, 0, :]))
            for k in range(DEPTH):
                last = nc.vector.tensor_tensor(lb_all[:, k, :], lb_all[:, k, :], lb_t[:, 0, :], ALU.subtract)
            first(last)
            dve.wait_ge(x_in.sem, 16)
            dve.wait_ge(emb_in.sem, 32)
            def root0(ins):
                ins.then_inc(var_ready.sem, 1)
                dve.wait_ge(root_ready.sem, 1)

            norm(h, first, root0, lambda ins: ins.then_inc(h_ready.sem, 1))
            assert before[0] == dve_step.before, before[0]

            with dve.Fori(0, DEPTH) as layer:
                pr = Program(dve, layer)

                def step(ins):
                    n = pr.mark(ins, dve_step)
                    pr.need(dve_step, n)
                    settle(dve, dve_passed)

                def root(ins):
                    pr.need(root_ready, pr.mark(ins, var_ready))

                def turn(g0, n):
                    for c in range(1, NC, 2):
                        pr.need(turned, n * NC + c + 1)
                        pr.mark(nc.vector.tensor_copy(hT[:, c, :], bank(g0 + c)), hT_dve)

                lb_now = lb_all[:, bass.ds(layer, 1), :].rearrange("p a h -> p (a h)")
                nc.vector.tensor_scalar(lb[:, 0, :], lb_now, LB_FLOOR, None, ALU.max)
                step(nc.vector.tensor_scalar(lb[:, 1, :], lb_now, -1.0, 1.0, ALU.mult, ALU.add))
                turn(G_T1, 0)
                pr.need(projected, 1)
                pr.need(ff_in, 32)
                step(nc.vector.tensor_scalar(ffw[:, 0, :], bank(G_PROJ)[0:FH, :], ff_bias[:], None, ALU.add))
                pr.mark(nc.vector.scalar_tensor_tensor(out=ffw[:, 1, :], in0=ffw[:, 0, :], scalar=-1.0, in1=ffw[:, 0, :],
                                                       op0=ALU.mult, op1=ALU.min), ff_z)
                for m in range(HH):
                    pr.need(projected, 2 + m)
                    pr.mark(nc.vector.tensor_scalar(gt[0][:, m, :], bank(G_PROJ + 1 + m), 80.0, None, ALU.min),
                            hf_ready)
                pr.need(ff_e, 1)
                step(nc.vector.scalar_tensor_tensor(out=ffw[:, 2, :], in0=ffw[:, 0, :], scalar=0.0, in1=ffw[:, 1, :],
                                                    op0=ALU.min, op1=ALU.subtract))
                step(nc.vector.memset(ffw[:, 1, :], 1.0))
                step(nc.vector.tensor_tensor_scan(out=ffw[:, 0, :], data0=ffw[:, 1, :], data1=ffw[:, 2, :],
                                                  initial=0.0, op0=ALU.mult, op1=ALU.add))
                pr.mark(nc.vector.tensor_scalar(negc[:], ffw[:, 0, :], -1.0 / SCALE, None, ALU.mult), negc_ready)
                pr.need(hf_exp, HH)
                step(nc.vector.tensor_scalar(kT, gt[0], 1.0, None, ALU.add))
                step(nc.vector.reciprocal(kT, kT))
                for m in range(HH):
                    last = nc.vector.tensor_scalar(kT[:, m, :], kT[:, m, :], lb[:, 1, m:m + 1], None, ALU.mult)
                step(last)
                step(nc.vector.tensor_tensor(gt[0], gt[0], kT, ALU.mult))
                for m in range(HH):
                    last = nc.vector.tensor_scalar(gt[0][:, m, :], gt[0][:, m, :], lb[:, 0, m:m + 1], None, ALU.add)
                step(last)
                nc.vector.tensor_scalar(gt[1], gt[0], 1.0 / LN_SPLIT, None, ALU.max)
                pr.mark(nc.vector.tensor_scalar(gt[2], gt[0], LN_SPLIT, 1.0, ALU.mult, ALU.min), f_ready)
                pr.need(f_log, 1)
                step(nc.vector.tensor_tensor(gt[1], gt[1], gt[2], ALU.add))
                for m in range(HH):
                    last = nc.vector.tensor_tensor_scan(out=b[:, m, :], data0=reset, data1=gt[1][:, m, :],
                                                        initial=0.0, op0=ALU.mult, op1=ALU.add)
                pr.mark(last, b_ready)
                pr.need(b_exp, 1)
                step(nc.vector.tensor_copy(eblast[:].rearrange("p (h i) -> p h i", h=HH),
                                           qe.rearrange("p h (i t) -> p h i t", t=P)[:, :, :, P - 1]))
                pr.need(qk_ready, 4)
                nc.vector.tensor_tensor(qe, qe, hqT, ALU.mult)
                pr.need(d_exp, 1)
                pr.mark(nc.vector.tensor_tensor(kd, kd, kT, ALU.mult), hdec_ready)
                pr.need(hdec_ready, 1)
                for k, dst in enumerate((fv, hi)):
                    for i in range(NT):
                        pr.need(projected, 18 + 4 * k + i)
                        pr.mark(nc.vector.tensor_copy(dst[:, i, :], bank(G_PROJ + 17 + 4 * k + i)), v_ready)
                for i in range(NT):
                    pr.need(hg_sig, i + 1)
                    pr.mark(nc.vector.tensor_tensor(silu[:, i, :], silu[:, i, :], bank(G_PROJ + 25 + i), ALU.mult),
                            silu_ready)

                for st in range(NS + 2):
                    if st < NS:
                        n = (st % NT + 1) * P
                        pr.need(scored, st + 1)
                        if st >= 2:
                            pr.need(probs_ready, st - 1)
                        if st >= 1:
                            pr.need(nmax_ready, st)
                        step(nc.vector.tensor_reduce(rinv[:, 1:2], bank(fox_group(0, st))[:, 0:n], AX_X, ALU.max))
                        pr.mark(nc.vector.tensor_scalar(nmax[:, st % 2:st % 2 + 1], rinv[:, 1:2], -SCALE, None,
                                                        ALU.mult), nmax_ready)
                    if 0 <= st - 1 < NS:
                        s = st - 1
                        n = (s % NT + 1) * P
                        pr.need(probs_turned, s + 1)
                        if s >= 2:
                            pr.need(pv_done, s - 1)
                        pr.mark(nc.vector.tensor_copy(probsT[:, s % 2, 0:n], bank(fox_group(1, s))[:, 0:n]),
                                probsT_ready)
                    if 0 <= st - 2:
                        s = st - 2
                        hd, i = s // NT, s % NT
                        pr.need(probs_ready, s + 1)
                        if s >= 1:
                            pr.need(fox_out, s)
                        step(nc.vector.reciprocal(rinv[:, 0:1], psum_p[:, s % 2:s % 2 + 1]))
                        pr.need(pv_done, s + 1)
                        pr.mark(nc.vector.tensor_scalar(mix[:, i, hd * FD:(hd + 1) * FD],
                                                        bank(fox_group(2, s))[:, 0:FD], rinv[:, 0:1], None, ALU.mult),
                                fox_out)

                sq = gt[0]
                pr.need(pv_done, NS)
                pr.need(fox_out, NS)
                step(nc.vector.tensor_tensor(sq, mix[:, :, 0:FW], mix[:, :, 0:FW], ALU.mult))
                step(nc.vector.tensor_reduce(ssq[:, 0:NT], sq, AX_X, ALU.add))
                root(nc.vector.tensor_scalar(ssq[:, 0:NT], ssq[:, 0:NT], 1.0 / FW, RMS_EPS, ALU.mult, ALU.add))
                step(nc.vector.reciprocal(ssq[:, 0:NT], ssq[:, 0:NT]))
                pr.need(gains_in, 32)
                for i in range(NT):
                    last = nc.vector.scalar_tensor_tensor(out=mix[:, i, 0:FW], in0=mix[:, i, 0:FW],
                                                          scalar=ssq[:, i:i + 1], in1=ng[:, 0, :],
                                                          op0=ALU.mult, op1=ALU.mult)
                pr.mark(last, mix_ready)

                for hd in range(HH):
                    if hd > 0:
                        pr.need(a_done, 2 * NT * hd)
                    for lev in range(1, LEVELS):
                        m = 2 ** (lev - 1)
                        bb = b[:, hd, :].rearrange("p (g a m) -> p g a m", a=2, m=m)
                        dd = KE[:, lev - 1, :].rearrange("p (g a m) -> p g a m", a=2, m=m)
                        mid = bb[:, :, 0, m - 1:m].to_broadcast([P, T // (2 * m), m])
                        nc.vector.tensor_tensor(dd[:, :, 0, :], mid, bb[:, :, 0, :], ALU.subtract)
                        last = nc.vector.tensor_tensor(dd[:, :, 1, :], bb[:, :, 1, :], mid, ALU.subtract)
                    pr.mark(last, lev_ready)
                    pr.need(lev_exp, hd + 1)

                    def over_levels(ap):
                        return ap.rearrange("p (o t) -> p o t", o=1).to_broadcast([P, LEVELS - 1, T])

                    step(nc.vector.tensor_tensor(QE, KE, over_levels(hqT[:, hd, :]), ALU.mult))
                    pr.mark(nc.vector.tensor_tensor(KE, KE, over_levels(kT[:, hd, :]), ALU.mult), lev_mul)
                    for i in range(NT):
                        j = hd * NT + i
                        if j >= 2:
                            pr.need(o_done, j - 1)
                        for half in range(2):
                            pr.need(a_done, 2 * j + half + 1)
                            pr.mark(nc.vector.tensor_tensor(
                                AT[:, j % 2, 4 * half:4 * half + 4, :].rearrange("p l n -> p (l n)"),
                                bank(hg_group(half, j)), level_mask[:, half * 512:(half + 1) * 512], ALU.mult),
                                at_ready)
                        pr.need(o_done, j + 1)
                        pr.mark(nc.vector.tensor_copy(mix[:, i, FW + hd * HD:FW + (hd + 1) * HD],
                                                      bank(hg_group(2, j))[:, 0:HD]), o_out)
                        if i < NT - 1:
                            up = hd * (NT - 1) + i
                            pr.need(u_done, up + 1)
                            upd = bank(hg_group(4, j))[:, 0:HD]
                            if i == 0:
                                ins = nc.vector.tensor_copy(state[:, hd, :], upd)
                            else:
                                pr.need(state_ready, up)
                                ins = nc.vector.scalar_tensor_tensor(out=state[:, hd, :], in0=state[:, hd, :],
                                                                     scalar=eblast[:, j:j + 1], in1=upd,
                                                                     op0=ALU.mult, op1=ALU.add)
                            pr.mark(ins, state_ready)
                pr.need(o_out, HH * NT)
                pr.need(mix_ready, 1)
                o_hg = mix[:, :, FW:2 * FW]
                step(nc.vector.tensor_tensor(sq, o_hg, o_hg, ALU.mult))
                step(nc.vector.tensor_reduce(ssq[:], sq.rearrange("p i (h n) -> p (i h) n", n=HD), AX_X, ALU.add))
                root(nc.vector.tensor_scalar(ssq[:], ssq[:], 1.0 / HD, RMS_EPS, ALU.mult, ALU.add))
                step(nc.vector.reciprocal(ssq[:], ssq[:]))
                for i in range(NT):
                    for hd in range(HH):
                        cols = slice(FW + hd * HD, FW + (hd + 1) * HD)
                        last = nc.vector.scalar_tensor_tensor(
                            out=mix[:, i, cols], in0=mix[:, i, cols], scalar=ssq[:, i * HH + hd:i * HH + hd + 1],
                            in1=ng[:, 1, hd * HD:(hd + 1) * HD], op0=ALU.mult, op1=ALU.mult)
                step(last)
                pr.mark(nc.vector.tensor_tensor(o_hg, o_hg, silu, ALU.mult), mix_ready)

                turn(G_T2, 1)
                for g in range(8):
                    half, i = g // 4, g % 4
                    pr.need(outed, g + 1)
                    hh = h[:, i, half * 512:(half + 1) * 512]
                    pr.mark(nc.vector.scalar_tensor_tensor(out=hh, in0=hh, scalar=ALPHA, in1=bank(G_OUT + g),
                                                           op0=ALU.mult, op1=ALU.add), pre1)
                pr.need(pre1, 8)
                pr.need(ln1_in, 32)
                norm(h, step, root, lambda ins: pr.mark(ins, h_ready))
                pr.need(h_ready, NT)

                turn(G_T3, 2)
                for g in range(1, 16, 2):
                    pr.need(queried, g + 1)
                    pr.mark(nc.vector.tensor_copy(pqT[:, g, :], bank(G_Q + g)), pq_dve)
                pr.need(h_split, 1)
                pr.mark(nc.vector.tensor_tensor(h_lo, hT[:], h_hi.bitcast(F32), ALU.subtract), h_split)
                with dve.Fori(0, NT) as i:
                    tile = layer * NT + i
                    TILE_STEPS = 43
                    at_entry = dve_step.made
                    count = [0]

                    def tstep(ins):
                        ins.then_inc(dve_step.sem, 1)
                        count[0] += 1
                        dve.wait_ge(dve_step.sem, layer * dve_step.per_layer + i * TILE_STEPS +
                                    (dve_step.before + at_entry + count[0]))
                        settle(dve, dve_passed)

                    def top16(values, keep, keep_u, n):
                        for a in range(n):
                            last = nc.vector.max(keep[:, a, 0:8], values[:, a, :])
                        tstep(last)
                        for a in range(n):
                            last = nc.vector.max_index(keep_u[:, a, 0:8], keep[:, a, 0:8], values[:, a, :])
                        tstep(last)
                        for a in range(n):
                            last = nc.vector.match_replace(values[:, a, :], keep[:, a, 0:8], values[:, a, :], -3e38)
                        tstep(last)
                        for a in range(n):
                            last = nc.vector.max(keep[:, a, 8:16], values[:, a, :])
                        tstep(last)
                        for a in range(n):
                            last = nc.vector.max_index(keep_u[:, a, 8:16], keep[:, a, 8:16], values[:, a, :])
                        tstep(last)

                    dve.wait_ge(score_sb.sem, layer * score_sb.per_layer + score_sb.per_layer)
                    settle(dve, dve_passed)
                    tstep(nc.vector.tensor_copy(score.rearrange("p a n -> p (a n)"),
                                                scores_all[:, bass.ds(i, 1), :].rearrange("p o n -> p (o n)")))
                    top16(score, top, top_u, 2 * PH)
                    tstep(nc.vector.tensor_copy(top_i, top_u))
                    ti = top_i.rearrange("p (h a) k -> p h a k", a=2)
                    ts = top.rearrange("p (h a) k -> p h a k", a=2)
                    tstep(nc.vector.tensor_scalar(ti[:, :, 0, :], ti[:, :, 0, :], float(NK), None, ALU.mult))
                    off = 0
                    for a in range(8):
                        nb = STAIR[a]
                        for src, dst in ((ts, cand_s), (ti, cand_i)):
                            nc.vector.tensor_tensor(dst[:, :, off:off + nb], src[:, :, 1, 0:nb],
                                                    src[:, :, 0, a:a + 1].to_broadcast([P, PH, nb]), ALU.add)
                        off += nb
                    for src, dst in ((ts, cand_s), (ti, cand_i)):
                        last = nc.vector.tensor_tensor(dst[:, :, off:CAND], src[:, :, 0, 8:TOPK],
                                                       src[:, :, 1, 0:1].to_broadcast([P, PH, 8]), ALU.add)
                    tstep(last)
                    top16(cand_s, sel_s, sel_u, PH)
                    nc.vector.tensor_copy(sel_p[:], sel_u[:]).then_inc(routed.sem, 1)
                    dve.wait_ge(routed.sem, tile + 1)
                    nc.vector.tensor_tensor(gate_e[:], sel_s[:], sel_s[:, :, 0:1].to_broadcast([P, PH, TOPK]),
                                            ALU.subtract).then_inc(sel_shift.sem, 1)
                    for a in range(PH):
                        tstep(nc.vector.tensor_tensor(
                            pick, iota[:, 0:CAND].rearrange("p (o c) -> p o c", o=1).to_broadcast([P, TOPK, CAND]),
                            sel_p[:, a, :].rearrange("p (k o) -> p k o", o=1).to_broadcast([P, TOPK, CAND]),
                            ALU.is_equal))
                        tstep(nc.vector.tensor_tensor(
                            pick, pick, cand_i[:, a:a + 1, :].to_broadcast([P, TOPK, CAND]), ALU.mult))
                        tstep(nc.vector.tensor_reduce(expert[:, a * TOPK:(a + 1) * TOPK], pick, AX_X, ALU.add))
                    tstep(nc.vector.tensor_copy(exp_u[:, 0, :], expert[:]))
                    tstep(nc.vector.tensor_scalar(exp_u[:, 1, :], exp_u[:, 0, :], NK - 1, None, ALU.bitwise_and))
                    tstep(nc.vector.tensor_scalar(exp_u[:, 0, :], exp_u[:, 0, :], 7, None,
                                                  ALU.logical_shift_right))
                    dve.wait_ge(table_turned.sem, tile + 1)
                    nc.vector.tensor_copy(table[:, 0:2, :], exp_u[:])
                    dve.wait_ge(sel_exp.sem, tile + 1)
                    tstep(nc.vector.tensor_reduce(gsum[:, 0, :], gate_e[:], AX_X, ALU.add))
                    tstep(nc.vector.reciprocal(gsum[:, 1, :], gsum[:, 0, :]))
                    nc.vector.tensor_tensor(gate, gate_e[:], gsum[:, 1, :].rearrange("p (h o) -> p h o", o=1)
                                            .to_broadcast([P, PH, TOPK]), ALU.mult).then_inc(table_ready.sem, 1)
                    dve.wait_ge(table_ready.sem, tile + 1)
                    settle(dve, dve_passed)
                    assert count[0] == TILE_STEPS, count[0]
                dve_step.made += NT * TILE_STEPS

                pr.need(tab_ready, NT)
                settle(dve, dve_passed)
                with dve.Fori(0, NG // 2) as q:
                    for r in range(2):
                        chunk = layer * NG + q * 2 + r
                        dve.wait_ge(g_full.sem, chunk + 1)
                        nc.vector.tensor_copy(hot_s[:, r], tabT[:, 0:3, bass.ds((q * 2 + r) * CHUNK, CHUNK)]
                                              ).then_inc(hot_step.sem, 1)
                        dve.wait_ge(hot_step.sem, chunk + 1)
                        for c in range(CHUNK):
                            nc.vector.tensor_scalar(hot1[:, r, c, :], iota, hot_s[:, r, 0, c:c + 1], None,
                                                    ALU.is_equal)
                            last = nc.vector.tensor_scalar(hot2[:, r, c, :], iota, hot_s[:, r, 1, c:c + 1],
                                                           hot_s[:, r, 2, c:c + 1], ALU.is_equal, ALU.mult)
                        last.then_inc(hot_ready.sem, 1)

                for g in range(8):
                    half, i = g // 4, g % 4
                    aa = acc[:, i, half * 512:(half + 1) * 512]
                    pr.need(gate_sig, g + 1)
                    pr.need(pled, g + 1)
                    pr.mark(nc.vector.tensor_tensor(aa, aa, bank(G_PLE + 8 + g), ALU.mult), ple_mul)
                    pr.need(ple_mul, g + 1)
                    pr.mark(nc.vector.scalar_tensor_tensor(out=aa, in0=h[:, i, half * 512:(half + 1) * 512],
                                                           scalar=ALPHA, in1=aa, op0=ALU.mult, op1=ALU.add), acc_init)
                pr.need(acc_init, 8)


                def weights(q, r):
                    dve.wait_ge(act_in[r].sem, layer * act_in[r].per_layer + (q * 16 + 16))
                    dve.wait_ge(gate_in[r].sem, layer * gate_in[r].per_layer + (q * 16 + 16))
                    ww = wact[:, r].rearrange("p g (j t) -> p g j t", t=TB)
                    nc.vector.tensor_tensor(ww, ww, gin[:, r].rearrange("p j g t -> p g j t"),
                                            ALU.mult).then_inc(w_ready.sem, 1)

                def low_weights(q, r):
                    for g in range(GROUP):
                        dve.wait_ge(w_hi_ready.sem, layer * NK + q * (2 * GROUP) + (r * GROUP + g + 1))
                        nc.vector.tensor_tensor(w_lo[:, g], wact[:, r, g], w_hi[:, g].bitcast(F32),
                                                ALU.subtract).then_inc(w_lo_ready.sem, 1)

                weights(0, 0)
                with dve.Fori(0, UPANELS // 2 - 1) as q:
                    weights(q, 1)
                    low_weights(q, 0)
                    weights(q + 1, 0)
                    low_weights(q, 1)
                weights(UPANELS // 2 - 1, 1)
                low_weights(UPANELS // 2 - 1, 0)
                low_weights(UPANELS // 2 - 1, 1)
                pr.need(y_done, NK)
                for k in range(BANKS):
                    i, half = k // 2, k % 2
                    aa = acc[:, i, half * 512:(half + 1) * 512]
                    pr.mark(nc.vector.tensor_tensor(aa, aa, bank(k), ALU.add), y_added)
                pr.need(y_added, BANKS)
                pr.need(ln2_in, 32)
                norm(acc, step, root, lambda ins: pr.mark(ins, h_ready))
                pr.need(h_ready, 2 * NT)

            dve.wait_ge(h_ready.sem, NT + DEPTH * 2 * NT)

        @block.sync
        def _(sp):
            sp.wait_ge(h_ready.sem, NT + DEPTH * 2 * NT)
            sp.dma_start(out.rearrange("(i p) d -> p i d", p=P), h[:]).then_inc(out_sent.sem, 16)
            sp.wait_ge(out_sent.sem, 16)

        for name, s in names:
            if s.made and s.made != s.per_layer:
                raise AssertionError(f"{name}: {s.made} a layer, not {s.per_layer}")


def constants():
    import numpy as np
    r = np.arange(P)
    ident = np.eye(P)
    causal = np.where(r[None, :] <= r[:, None], 0.0, MASK)
    iota = np.tile(np.arange(P), (P, 1))
    s, t = r[:, None], r[None, :]
    levels = [s == t]
    for lev in range(1, LEVELS):
        m = 2 ** (lev - 1)
        levels.append((s // (2 * m) == t // (2 * m)) & (s % (2 * m) < m) & (t % (2 * m) >= m))
    starts = np.tile((np.arange(T) % P != 0), (P, 1))
    return np.ascontiguousarray(np.concatenate([ident, causal, iota] + levels + [starts], axis=1).astype(np.float32))


def kernel(**inputs):
    import numpy as np
    import concourse.bacc as bacc
    from concourse.bass_utils import run_bass_kernel_spmd as run

    a = {k: np.asarray(val) for k, val in inputs.items()}
    depth = a["w_in"].shape[0]
    arrays = {
        "x": a["x"][0],
        "pT": a["p"][:, 0].transpose(0, 2, 1),
        "emb_g": a["emb_ln_g"], "emb_b": a["emb_ln_b"],
        "w_in": a["w_in"], "fox_fb": a["fox_fb"], "fox_g": a["fox_norm_g"],
        "lbl": a["hg_lb_logits"].reshape(depth, HH, HD).transpose(2, 0, 1),
        "hg_g": a["hg_norm_g"], "w_out": a["w_out"], "ln1_g": a["ln1_g"], "ln1_b": a["ln1_b"],
        "wq": a["peer_wq"],
        "keysT": a["peer_keys"].reshape(depth, 2 * PH, NK, P).transpose(0, 3, 1, 2),
        "u": a["peer_u"].reshape(depth, NK, UPANELS, GROUP, NC, P).transpose(0, 2, 5, 3, 4, 1)
        .reshape(depth, UPANELS, P, GROUP * NC * NK),
        "v": a["peer_v"].reshape(depth, NK, UPANELS, GROUP, D).transpose(0, 2, 1, 3, 4)
        .reshape(depth, UPANELS, NK, GROUP * D),
        "gate_w": a["ple_gate_w"], "ple_w": a["ple_w"],
        "ln2_g": a["ln2_g"], "ln2_b": a["ln2_b"], "consts": constants(),
    }
    nc = bacc.Bacc("TRN2", target_bir_lowering=False, num_devices=1)
    nc.disable_value_cache = True
    feed, args = {}, {}
    for name, val in arrays.items():
        val = np.ascontiguousarray(val)
        feed[f"in_{name}"] = val
        args[name] = nc.dram_tensor(f"in_{name}", val.shape, mybir.dt.from_np(val.dtype), kind="ExternalInput").ap()
    args["out"] = nc.dram_tensor("out_h", (T, D), F32, kind="ExternalOutput").ap()
    build(nc, **args)
    r = run(nc, [feed], core_ids=[0])
    return r.results[0]["out_h"].reshape(1, T, D)
```

```python
from contextlib import ExitStack

import concourse.bass as bass
from concourse import mybir

P = 128
T = 512
D = 1024
NT = T // P
NC = D // P
FH, FD = 8, 64
FW = FH * FD
HH, HD = 4, 128
HW = HH * HD
IN_COLS = 3 * FW + FH + 4 * HW
PH, NK, TOPK = 8, 128, 16
NE = NK * NK
SLOTS = PH * TOPK
PLE = 256
BANKS = 8
PANEL = 512
KC = NC // 2
RING = 4
GROUP = 4
UPANELS = NK // GROUP
CHUNK = 4
TB = P // 4
BLOCKS = T // TB
PAIR = 2
LEVELS = 8
STAIR = [TOPK // (a + 1) for a in range(TOPK)]
CAND = sum(STAIR)
LN_EPS, RMS_EPS, LB_FLOOR, MASK = 1e-5, 1e-6, 1e-30, -1e30
LN_SPLIT = 2.0 ** 60

ALU = mybir.AluOpType
ACT = mybir.ActivationFunctionType
F32 = mybir.dt.float32
BF16 = mybir.dt.bfloat16
F32R = mybir.dt.float32r
U32 = mybir.dt.uint32
AX_X = mybir.AxisListType.X


class Signal:

    def __init__(self, sem, per_layer, before=0):
        self.sem, self.per_layer, self.before, self.made = sem, per_layer, before, 0


def build(nc, x, pT, emb_g, emb_b, w_in, fox_fb, fox_g, lbl, hg_g, w_out, ln1_g, ln1_b,
          wq, keysT, u, v, gate_w, ple_w, ln2_g, ln2_b, consts, out):
    DEPTH = w_in.shape[0]
    ALPHA = (2 * DEPTH) ** 0.25
    SCALE = FD ** -0.5
    act_dram = nc.dram_tensor("act_scratch", (DEPTH, UPANELS, P, GROUP * T), F32).ap()
    gate_dram = nc.dram_tensor("gate_scratch", (DEPTH, BLOCKS, P, NK, TB), F32).ap()

    c0 = 3 * FW + FH
    MIXER_PANELS = [(w_in, c0 + HW), (w_in, c0), (w_in, 0), (w_in, FW), (w_in, 2 * FW),
                    (w_in, c0 + 2 * HW), (w_in, c0 + 3 * HW), (w_out, 0), (w_out, PANEL)] + \
                   [(wq, PANEL * j) for j in range(4)]
    GATE_PANELS = [(gate_w, 0), (gate_w, PANEL)]
    K_U = 1 + 2 * len(MIXER_PANELS)
    K_GATE = K_U + 2 * UPANELS
    K_PLE, K_V = K_GATE + 2 * len(GATE_PANELS), K_GATE + 2 * len(GATE_PANELS) + 1
    LOADS = K_V + 2 * UPANELS
    S_GATE = 2 + KC * (K_U - 1)
    SPLITS = S_GATE + KC * 2 * len(GATE_PANELS)

    with ExitStack() as ctx:
        def sb(name, shape, dt=F32):
            return ctx.enter_context(nc.sbuf_tensor(name, shape, dt))

        names = []

        def sig(name, per_layer, before=0):
            s = Signal(ctx.enter_context(nc.semaphore(name)), per_layer, before)
            names.append((name, s))
            return s

        ps = ctx.enter_context(nc.psum_tensor("ps", [P, BANKS, 512], F32))

        h = sb("h", [P, NT, D])
        hT_hi = sb("hT_hi", [P, NC, T], F32R)
        hT_lo = sb("hT_lo", [P, NC, T], F32R)
        panel = sb("panel", [P, 2, KC * PANEL])
        lng = sb("lng", [P, 2, D])
        ng = sb("ng", [P, 2, 512])
        pTs = sb("pTs", [P, 2, T])
        cst = sb("cst", [P, consts.shape[1]])
        cb = sb("cb", [P, 2 * P], BF16)
        def half(name, n):
            return shared.enter_context(nc.sbuf_tensor(name, [P, n], F32R))

        with ExitStack() as shared:
            wide_hi, wide_lo = half("wide_hi", NC * T), half("wide_lo", NC * T)
            slim_hi, slim_lo = half("slim_hi", GROUP * T), half("slim_lo", GROUP * T)
            half("between", 21504 - 2 * NC * T - 2 * GROUP * T)
            ring_hi, ring_lo = half("ring_hi", RING * PANEL), half("ring_lo", RING * PANEL)
        with ExitStack() as shared:
            half("below", 2 * NC * T // 2)
            hot1, hot2_hi, hot2_lo = (half(n, 2 * CHUNK * NK)[:].rearrange("p (b c n) -> p b c n", b=2, c=CHUNK)
                                      for n in ("hot1", "hot2_hi", "hot2_lo"))
        arena = sb("arena", [P, 25600])
        work = sb("work", [P, 2048])
        negc = sb("negc", [FH, T])
        ff_bias = sb("ff_bias", [FH, 1])
        stat = sb("stat", [P, NT, 12])
        mv = sb("mv", [P, NT, 2])
        rstd = sb("rstd", [P, NT])

        ident = cst[:, 0:128]
        cmask = cst[:, 128:256]
        iota = cst[:, 256:384]
        level_mask = cst[:, 384:384 + LEVELS * P]
        reset = cst[:, 1408:1408 + T]
        zeros = reset[:, 0:1].to_broadcast([P, PANEL])
        ident_b, cmask_b = cb[:, 0:128], cb[:, 128:256]

        def part(at, *shape):
            n = 1
            for s in shape:
                n *= s
            ap = arena[:, at:at + n]
            if len(shape) == 2:
                return ap.rearrange("p (a b) -> p a b", b=shape[1])
            if len(shape) == 3:
                return ap.rearrange("p (a b c) -> p a b c", b=shape[1], c=shape[2])
            return ap

        fqT = part(0, 4, T)
        fkT = part(2048, 4, T)
        fv = part(4096, NT, FW)
        QE = part(0, LEVELS - 1, T)
        KE = part(3584, LEVELS - 1, T)
        gt = [part(2048 * j, HH, T) for j in range(3)]
        hqT = part(7168, HH, T)
        kT = part(9216, HH, T)
        b = part(11264, HH, T)
        hi = part(13312, NT, HW)
        silu = part(15360, NT, HW)
        qe = part(17408, HH, T)
        kd = part(19456, HH, T)
        mix = part(21504, NT, D)
        pqT = part(0, 2 * PH, T)
        keys_s = part(8192, 2 * PH, NK)
        scores_all = part(12288, NT, 2 * PH * NK)
        score = lng[:].rearrange("p a (b n) -> p (a b) n", n=NK)
        u_hi, u_lo = (w[:].rearrange("p (b c n) -> p b c n", b=2, c=NC) for w in (slim_hi, slim_lo))
        v_hi, v_lo = (w[:].rearrange("p (g d) -> p g d", g=GROUP) for w in (wide_hi, wide_lo))
        w_hi, w_lo = (w[:].rearrange("p (g t) -> p g t", g=GROUP) for w in (slim_hi, slim_lo))
        gmat = arena[:, 12288:20480].rearrange("p (b i t) -> p b i t", b=2, i=NK)
        gact = arena[:, 0:2048].rearrange("p (g t) -> p g t", g=GROUP)
        tabT = part(2048, 4, T)
        top = part(4096, 2 * PH, TOPK)
        top_i = part(4352, 2 * PH, TOPK)
        top_u = arena[:, 4608:4864].bitcast(U32).rearrange("p (a k) -> p a k", k=TOPK)
        acc = part(12288, NT, D)
        wact = arena[:, 16384:20480].rearrange("p (b g t) -> p b g t", b=2, g=GROUP)
        gin = arena[:, 20480:24576].rearrange("p (b j g t) -> p b j g t", b=2, j=BLOCKS, g=GROUP)
        cand_s = work[:, 0:PH * CAND].rearrange("p (h c) -> p h c", c=CAND)
        cand_i = work[:, 400:400 + PH * CAND].rearrange("p (h c) -> p h c", c=CAND)
        pick = work[:, 800:800 + TOPK * CAND].rearrange("p (k c) -> p k c", c=CAND)
        probs = work[:, 0:1024].rearrange("p (a n) -> p a n", a=2)
        probsT = work[:, 1024:2048].rearrange("p (a n) -> p a n", a=2)
        AT = work[:, 0:2048].rearrange("p (a l n) -> p a l n", a=2, n=P)

        ffw = work[0:FH, 0:3 * T].rearrange("p (a t) -> p a t", a=3)

        nmax = sb("nmax", [P, 2])
        psum_p = sb("psum_p", [P, 4])
        rinv = sb("rinv", [P, 2])
        state = sb("state", [P, HH, HD])
        kdT = sb("kdT", [P, 2, P])
        eblast = sb("eblast", [P, HH * NT])
        ssq = sb("ssq", [P, 16])
        lb_in = sb("lb_in", [P, DEPTH, HH])
        lb_all = sb("lb_all", [P, DEPTH, HH])
        lb_t = sb("lb_t", [P, 2, HH])
        lb = sb("lb", [P, 2, HH])
        sel_s = sb("sel_s", [P, PH, TOPK])
        sel_u = sb("sel_u", [P, PH, TOPK], U32)
        sel_p = sb("sel_p", [P, PH, TOPK])
        expert = sb("expert", [P, SLOTS])
        exp_u = sb("exp_u", [P, 2, SLOTS], U32)
        table = sb("table", [P, 3, SLOTS])
        gate = table[:, 2, :].rearrange("p (h k) -> p h k", k=TOPK)
        gate_e = sb("gate_e", [P, PH, TOPK])
        gsum = sb("gsum", [P, 2, PH])
        hot_s = sb("hot_s", [P, 2, 4, CHUNK])

        dve_passed = sig("dve_passed", 0)
        pe_passed = sig("pe_passed", 0)
        pool_passed = sig("pool_passed", 0)
        const_in = sig("const_in", 0, 16)
        x_in = sig("x_in", 0, 16)
        emb_in = sig("emb_in", 0, 32)
        lb_loaded = sig("lb_loaded", 0, 16)
        ff_in = sig("ff_in", 16)
        gains_in = sig("gains_in", 32)
        ln1_in = sig("ln1_in", 32)
        ln2_in = sig("ln2_in", 32)
        pT_in = sig("pT_in", 16)
        keys_in = sig("keys_in", 16)
        panel_in = [sig(f"panel_in{s}", 16 * LOADS // 2) for s in range(2)]
        h_ready = sig("h_ready", 2 * NT, NT)
        lb_shift = sig("lb_shift", 0, 1)
        lb_exp = sig("lb_exp", 0, 1)
        var_ready = sig("var_ready", 4, 1)
        root_ready = sig("root_ready", 4, 1)
        casts = sig("casts", 0, 2)
        dve_step = sig("dve_step", 271, 15)
        act_step = sig("act_step", 1)
        turned = sig("turned", 3 * NC)
        hT_hi_ready = sig("hT_hi_ready", 3 * NC)
        hT_lo_ready = sig("hT_lo_ready", 3 * NC)
        ring_hi_ready = sig("ring_hi_ready", SPLITS)
        ring_lo_ready = sig("ring_lo_ready", SPLITS)
        ring_used = sig("ring_used", SPLITS, RING)
        products = sig("products", 3 * (len(MIXER_PANELS) + len(GATE_PANELS)))
        ff_z = sig("ff_z", 1)
        ff_e = sig("ff_e", 1)
        negc_ready = sig("negc_ready", 1)
        hf_ready = sig("hf_ready", HH)
        hf_exp = sig("hf_exp", HH)
        f_ready = sig("f_ready", 1)
        f_log = sig("f_log", 1)
        b_ready = sig("b_ready", 1)
        b_exp = sig("b_exp", 1)
        d_exp = sig("d_exp", 1)
        hdec_ready = sig("hdec_ready", 1)
        qk_ready = sig("qk_ready", 12)
        v_ready = sig("v_ready", 8)
        hg_sig = sig("hg_sig", NT)
        silu_ready = sig("silu_ready", NT)
        NS = FH * NT
        scored = sig("scored", NS)
        nmax_ready = sig("nmax_ready", NS)
        probs_ready = sig("probs_ready", NS)
        probs_turned = sig("probs_turned", NS)
        probsT_ready = sig("probsT_ready", NS)
        pv_done = sig("pv_done", NS)
        fox_out = sig("fox_out", NS)
        lev_ready = sig("lev_ready", HH)
        lev_exp = sig("lev_exp", HH)
        lev_mul = sig("lev_mul", HH)
        a_done = sig("a_done", 2 * HH * NT)
        at_ready = sig("at_ready", 2 * HH * NT)
        o_done = sig("o_done", HH * NT)
        o_out = sig("o_out", HH * NT)
        kd_turned = sig("kd_turned", HH * (NT - 1))
        kdT_ready = sig("kdT_ready", HH * (NT - 1))
        u_done = sig("u_done", HH * (NT - 1))
        state_ready = sig("state_ready", HH * (NT - 1))
        mix_ready = sig("mix_ready", 2)
        pre1 = sig("pre1", 8)
        pq_act = sig("pq_act", 8)
        pq_dve = sig("pq_dve", 8)
        key_scored = sig("key_scored", 16)
        score_sb = sig("score_sb", 16)
        gate_sig = sig("gate_sig", 8)
        pled = sig("pled", 8)
        ple_mul = sig("ple_mul", 8)
        acc_init = sig("acc_init", 8)
        routed = sig("routed", NT)
        sel_shift = sig("sel_shift", NT)
        sel_exp = sig("sel_exp", NT)
        SEGS = [0, 1, 3, 5, 7, 8]
        NG = T // CHUNK
        table_ready = sig("table_ready", NT)
        table_turned = sig("table_turned", NT, 1)
        tab_ready = sig("tab_ready", NT)
        hot_step = sig("hot_step", NG)
        a_full = sig("a_full", NK)
        gelu_done = sig("gelu_done", NK, GROUP)
        u_hi_ready = sig("u_hi_ready", NK)
        u_lo_ready = sig("u_lo_ready", NK)
        act_out = [sig(f"act_out{r}", 16 * UPANELS, 16) for r in range(2)]
        hot_ready = sig("hot_ready", NG)
        g_full = sig("g_full", NG, 2)
        g_kept = sig("g_kept", NG, 4)
        g_out = [sig(f"g_out{r}", 16 * BLOCKS // 2, 16) for r in range(2)]
        act_in = [sig(f"act_in{r}", 16 * UPANELS // 2) for r in range(2)]
        gate_in = [sig(f"gate_in{r}", 16 * UPANELS // 2) for r in range(2)]
        w_ready = sig("w_ready", UPANELS)
        v_hi_ready = sig("v_hi_ready", NK)
        v_lo_ready = sig("v_lo_ready", NK, 1)
        w_hi_ready = sig("w_hi_ready", NK)
        w_lo_ready = sig("w_lo_ready", NK)
        y_done = sig("y_done", NK, GROUP)
        y_added = sig("y_added", 8)
        out_sent = sig("out_sent", 0, 16)

        block = ctx.enter_context(nc.Block())

        def settle(eng, passed):
            eng.sem_inc(passed.sem, 1)

        class Program:

            def __init__(self, eng, layer):
                self.eng, self.layer = eng, layer

            def need(self, s, n):
                self.eng.wait_ge(s.sem, self.layer * s.per_layer + (s.before + n))

            def mark(self, ins, s, n=1):
                ins.then_inc(s.sem, n)
                s.made += n
                return s.made

            def link(self, ins, s):
                self.need(s, self.mark(ins, s))

        def product(pr, n):
            if n % 4 < 3:
                pr.need(products, n // 4 * 3 + n % 4 + 1)
            else:
                pr.need(ring_used, 2 + 2 * KC * (n // 4 + 1))

        G_T1 = 0
        G_PROJ = G_T1 + NC
        G_FOX = G_PROJ + 29
        G_HG = G_FOX + 3 * NS
        G_T2 = G_HG + 4 * HH * NT + 2 * HH * (NT - 1) - HH * NT
        G_OUT = G_T2 + NC
        G_T3 = G_OUT + 8
        G_Q = G_T3 + NC
        G_PLE = 0

        def bank(g):
            return ps[:, g % BANKS, :]

        def fox_group(kind, s):
            g = G_FOX
            for st in range(NS + 2):
                for k in range(3):
                    q = st - k
                    if 0 <= q < NS:
                        if (k, q) == (kind, s):
                            return g
                        g += 1

        def hg_group(kind, j):
            g = G_HG
            for jj in range(HH * NT):
                for k in (0, 1, 3, 2, 4):
                    if k >= 3 and jj % NT == NT - 1:
                        continue
                    if (k, jj) == (kind, j):
                        return g
                    g += 1

        @block.sync
        def _(sp):
            sp.dma_start(h[:], x.rearrange("(i p) d -> p i d", p=P)).then_inc(x_in.sem, 16)
            sp.dma_start(lb_in[:], lbl).then_inc(lb_loaded.sem, 16)
            for k, a in enumerate((emb_g, emb_b)):
                sp.dma_start(lng[:, k, :], a.partition_broadcast(P)).then_inc(emb_in.sem, 16)
            sp.dma_start(cst[:], consts).then_inc(const_in.sem, 16)
            with sp.Fori(0, DEPTH) as layer:
                pr = Program(sp, layer)
                at = bass.ds(layer, 1)

                def load_panel(k, n=None):
                    dst = panel[:, k % 2]
                    if k == 0:
                        src = w_in[at, :, 3 * FW:3 * FW + P].rearrange("l (c p) n -> p (l c) n", p=P)
                        dst = dst[:, 0:NC * P].rearrange("p (c n) -> p c n", n=P)
                    elif k == K_PLE:
                        src = ple_w[at].rearrange("l (c p) n -> p (l c) n", p=P)
                        dst = dst.rearrange("p (c n) -> p c n", n=D)
                    elif n is not None:
                        src = (u if k < K_GATE else v)[at, bass.ds(n, 1)].rearrange("l n p c -> p (l n c)")
                    else:
                        j, rows = ((k - 1) // 2, (k - 1) % 2) if k < K_U else ((k - K_GATE) // 2, (k - K_GATE) % 2)
                        w, col = (MIXER_PANELS if k < K_U else GATE_PANELS)[j]
                        src = w[at, rows * KC * P:(rows + 1) * KC * P, col:col + PANEL].rearrange(
                            "l (c p) n -> p (l c) n", p=P)
                        dst = dst.rearrange("p (c n) -> p c n", n=PANEL)
                    sp.dma_start(dst, src).then_inc(panel_in[k % 2].sem, 16)

                def row(a):
                    return a[at].rearrange("l d -> (l d)").partition_broadcast(P)

                pr.need(v_lo_ready, 0)
                load_panel(0)
                pr.mark(sp.dma_start(ff_bias[:], fox_fb[at].rearrange("l h -> h l")), ff_in, 16)
                load_panel(1)
                for k, a in enumerate((fox_g, hg_g)):
                    pr.mark(sp.dma_start(ng[:, k, :], row(a)), gains_in, 16)
                pr.mark(sp.dma_start(pTs[:], pT[at].rearrange("l (c p) t -> p (l c) t", p=P)), pT_in, 16)
                pr.need(h_ready, 0)
                for k, a in enumerate((ln1_g, ln1_b)):
                    pr.mark(sp.dma_start(lng[:, k, :], row(a)), ln1_in, 16)
                for k in range(2, K_U):
                    pr.need(ring_lo_ready, 2 + KC * (k - 2))
                    load_panel(k)
                pr.need(h_ready, NT)
                pr.mark(sp.dma_start(keys_s, keysT[at].rearrange("l d a n -> d (l a) n")), keys_in, 16)
                for r in range(2):
                    pr.need(ring_lo_ready, S_GATE - KC * (1 - r))
                    load_panel(K_U + r, r)
                with sp.Fori(1, UPANELS) as q:
                    for r in range(2):
                        sp.wait_ge(u_lo_ready.sem, layer * NK + (q * 2 + r - 1) * PAIR)
                        load_panel(K_U + r, q * 2 + r)
                for k in range(K_GATE, K_GATE + 2):
                    pr.need(u_lo_ready, PAIR * (2 * UPANELS - 1 + k - K_GATE))
                    load_panel(k)
                pr.need(routed, NT)
                for k, a in enumerate((ln2_g, ln2_b)):
                    pr.mark(sp.dma_start(lng[:, k, :], row(a)), ln2_in, 16)
                for k in range(K_GATE + 2, K_V + 1):
                    pr.need(ring_lo_ready, S_GATE + KC * (k - K_GATE - 1))
                    load_panel(k, 0 if k == K_V else None)
                pr.need(pled, 8)
                load_panel(K_V + 1, 1)
                with sp.Fori(1, UPANELS) as q:
                    for r in range(2):
                        sp.wait_ge(v_lo_ready.sem, layer * NK + ((q * 2 + r - 1) * PAIR + v_lo_ready.before))
                        load_panel(K_V + r, q * 2 + r)

        @block.tensor
        def _(pe):
            pe.wait_ge(const_in.sem, 16)
            pe.wait_ge(casts.sem, 2)
            pe.sem_inc(y_done.sem, y_done.before)
            pe.sem_inc(g_full.sem, g_full.before)
            pe.sem_inc(table_turned.sem, table_turned.before)
            with pe.Fori(0, DEPTH) as layer:
                pr = Program(pe, layer)
                freed = []

                def take(g, release):
                    assert g == len(freed), (g, len(freed))
                    if g >= BANKS:
                        pr.need(*freed[g - BANKS])
                    freed.append(release)
                    return bank(g)

                def turn(src, g0, n):
                    for c in range(NC):
                        o = take(g0 + c, (hT_lo_ready, n * NC + c + 1))
                        for i in range(NT):
                            mm = nc.tensor.transpose(o[:, i * P:(i + 1) * P], src[:, i, c * P:(c + 1) * P], ident)
                        pr.mark(mm, turned)
                    pr.need(hT_lo_ready, (n + 1) * NC)

                used = [0]

                def next_chunk():
                    pr.need(ring_lo_ready, used[0] + 1)
                    at = (used[0] % RING) * PANEL
                    return [w[:, at:at + PANEL] for w in (ring_hi, ring_lo)]

                def matmul3(o, lhs, rhs, start, stop):
                    for n, (a, b_) in enumerate(((1, 0), (0, 1), (0, 0))):
                        mm = nc.tensor.matmul(o, lhs[a], rhs[b_], start=(start and n == 0), stop=(stop and n == 2))
                    return mm

                def project(o4, by_token):
                    for c in range(NC):
                        w = next_chunk()
                        for m in range(4):
                            if by_token:
                                mm = matmul3(o4[m], [x_[:, c, m * P:(m + 1) * P] for x_ in (hT_hi, hT_lo)], w,
                                             c == 0, c == NC - 1)
                            else:
                                mm = matmul3(o4[m], [x_[:, m * P:(m + 1) * P] for x_ in w],
                                             [x_[:, c, :] for x_ in (hT_hi, hT_lo)], c == 0, c == NC - 1)
                            if m == 3:
                                pr.mark(mm, ring_used)
                            elif c == NC - 1:
                                pr.mark(mm, products)
                        used[0] += 1

                pr.need(h_ready, 0)
                turn(h, G_T1, 0)
                g = G_PROJ
                o = take(g, (ff_z, 1))
                for part_ in range(2):
                    w = next_chunk()
                    for c in range(4):
                        mm = matmul3(o, [x_[:, c * P:(c + 1) * P] for x_ in w],
                                     [x_[:, 4 * part_ + c, :] for x_ in (hT_hi, hT_lo)],
                                     part_ + c == 0, part_ == 1 and c == 3)
                    used[0] += 1
                    pr.mark(mm, ring_used)
                for k in range(7):
                    o4 = []
                    for m in range(4):
                        g += 1
                        o4.append(take(g, [(hf_ready, m + 1), (qk_ready, m + 1), (qk_ready, 5 + m), (qk_ready, 9 + m),
                                           (v_ready, m + 1), (v_ready, 5 + m), (silu_ready, m + 1)][k]))
                    project(o4, k >= 4)

                pr.need(negc_ready, 1)
                pr.need(qk_ready, 12)
                pr.need(v_ready, 4)
                for st in range(NS + 2):
                    if st < NS:
                        hd, i = st // NT, st % NT
                        n = (i + 1) * P
                        o = take(fox_group(0, st), (probs_ready, st + 1))
                        rows_ = slice(FD * (hd % 2), FD * (hd % 2) + FD)
                        nc.tensor.matmul(o[:, 0:n], fqT[rows_, hd // 2, i * P:(i + 1) * P], fkT[rows_, hd // 2, 0:n],
                                         start=True, stop=False)
                        nc.tensor.matmul(o[:, 0:n], ident[0:FH, hd:hd + 1].to_broadcast([FH, P]), negc[:, 0:n],
                                         start=False, stop=False)
                        pr.mark(nc.tensor.matmul(o[:, n - P:n], ident_b, cmask_b, start=False, stop=True), scored)
                    if 0 <= st - 1 < NS:
                        s = st - 1
                        i = s % NT
                        o = take(fox_group(1, s), (probsT_ready, s + 1))
                        pr.need(probs_ready, s + 1)
                        for j in range(i + 1):
                            mm = nc.tensor.transpose(o[:, j * P:(j + 1) * P], probs[:, s % 2, j * P:(j + 1) * P], ident)
                        pr.mark(mm, probs_turned)
                    if 0 <= st - 2:
                        s = st - 2
                        hd, i = s // NT, s % NT
                        o = take(fox_group(2, s), (fox_out, s + 1))
                        pr.need(probsT_ready, s + 1)
                        for j in range(i + 1):
                            mm = nc.tensor.matmul(o[:, 0:FD], probsT[:, s % 2, j * P:(j + 1) * P],
                                                  fv[:, j, hd * FD:(hd + 1) * FD], start=(j == 0), stop=(j == i))
                        pr.mark(mm, pv_done)

                pr.need(hdec_ready, 1)
                pr.need(v_ready, 8)
                for j in range(HH * NT):
                    hd, i = j // NT, j % NT
                    toks = slice(i * P, (i + 1) * P)
                    if i == 0:
                        pr.need(lev_mul, hd + 1)
                    for half in range(2):
                        o = take(hg_group(half, j), (at_ready, 2 * j + half + 1))
                        for k in range(4):
                            lev = 4 * half + k
                            kk = kT[:, hd, toks] if lev == 0 else KE[:, lev - 1, toks]
                            qq = hqT[:, hd, toks] if lev == 0 else QE[:, lev - 1, toks]
                            mm = nc.tensor.matmul(o[:, k * P:(k + 1) * P], kk, qq, start=True, stop=True)
                        pr.mark(mm, a_done)
                    up = hd * (NT - 1) + i
                    if i < NT - 1:
                        o = take(hg_group(3, j), (kdT_ready, up + 1))
                        pr.mark(nc.tensor.transpose(o[:, 0:P], kd[:, hd, toks], ident), kd_turned)
                    o = take(hg_group(2, j), (o_out, j + 1))
                    vv = hi[:, i, hd * HD:(hd + 1) * HD]
                    if i > 0:
                        pr.need(state_ready, up)
                        nc.tensor.matmul(o[:, 0:HD], qe[:, hd, toks], state[:, hd, :], start=True, stop=False)
                    pr.need(at_ready, 2 * j + 2)
                    for lev in range(LEVELS):
                        mm = nc.tensor.matmul(o[:, 0:HD], AT[:, j % 2, lev, :], vv,
                                              start=(lev == 0 and i == 0), stop=(lev == LEVELS - 1))
                    pr.mark(mm, o_done)
                    if i < NT - 1:
                        o = take(hg_group(4, j), (state_ready, up + 1))
                        pr.need(kdT_ready, up + 1)
                        pr.mark(nc.tensor.matmul(o[:, 0:HD], kdT[:, up % 2, :], vv, start=True, stop=True), u_done)

                pr.need(mix_ready, 2)
                turn(mix, G_T2, 1)
                for half in range(2):
                    project([take(G_OUT + 4 * half + i, (pre1, 4 * half + i + 1)) for i in range(NT)], True)

                pr.need(h_ready, NT)
                turn(h, G_T3, 2)
                for k in range(4):
                    project([take(G_Q + g, ((pq_act, pq_dve)[g % 2], g // 2 + 1)) for g in range(4 * k, 4 * k + 4)],
                            False)

                pr.need(keys_in, 16)
                pr.need(pq_act, 8)
                pr.need(pq_dve, 8)

                for i in range(NT):
                    for k in range(4):
                        if 4 * i + k >= BANKS:
                            pr.need(score_sb, 4 * i + k - BANKS + 1)
                        for a in range(4):
                            mm = nc.tensor.matmul(bank(4 * i + k)[:, a * NK:(a + 1) * NK],
                                                  pqT[:, 4 * k + a, i * P:(i + 1) * P],
                                                  keys_s[:, 4 * k + a, :], start=True, stop=True)
                        pr.mark(mm, key_scored)

                def first_products(q, r, g):
                    tile = q * (2 * GROUP) + (r * GROUP + g + 1)
                    pe.wait_ge(u_lo_ready.sem, layer * NK + tile)
                    pe.wait_ge(gelu_done.sem, layer * NK + tile)
                    for c in range(NC):
                        mm = matmul3(bank(g), [x_[:, g % 2, c, :] for x_ in (u_hi, u_lo)],
                                     [x_[:, c, :] for x_ in (hT_hi, hT_lo)], c == 0, c == NC - 1)
                    mm.then_inc(a_full.sem, 1)

                def turn_table(i):
                    pr.need(table_ready, i + 1)
                    if i > 0:
                        pr.need(tab_ready, i)
                    for k in range(3):
                        mm = nc.tensor.transpose(bank(4)[:, k * P:(k + 1) * P], table[:, k, :], ident)
                    pr.mark(mm, table_turned)

                pr.need(score_sb, 4 * NT)
                settle(pe, pe_passed)
                for seg in range(len(SEGS) - 1):
                    with pe.Fori(SEGS[seg], SEGS[seg + 1]) as q:
                        for r in range(2):
                            for g in range(GROUP):
                                first_products(q, r, g)
                    if seg > 0:
                        turn_table(seg - 1)
                pr.need(tab_ready, NT)
                settle(pe, pe_passed)
                with pe.Fori(SEGS[-1], UPANELS // 2) as q:
                    for r in range(2):
                        for g in range(GROUP):
                            first_products(q, r, g)
                            for k in range(2 * g, 2 * g + 2):
                                chunk = layer * NG + (q - SEGS[-1]) * 16 + (r * 8 + k)
                                pe.wait_ge(hot_ready.sem, chunk + 1)
                                pe.wait_ge(g_kept.sem, chunk + 1)
                                for c in range(CHUNK):
                                    o = bank(4 + k % 4)[:, c * NK:(c + 1) * NK]
                                    nc.tensor.matmul(o, hot1[:, k % 2, c, :], hot2_lo[:, k % 2, c, :],
                                                     start=True, stop=False)
                                    mm = nc.tensor.matmul(o, hot1[:, k % 2, c, :], hot2_hi[:, k % 2, c, :],
                                                          start=False, stop=True)
                                mm.then_inc(g_full.sem, 1)

                pr.need(gelu_done, NK)
                pr.need(g_kept, NG)
                pr.need(pT_in, 16)
                freed.clear()
                for half in range(2):
                    project([take(G_PLE + 4 * half + i, (gate_sig, 4 * half + i + 1)) for i in range(NT)], True)
                pr.need(panel_in[K_PLE % 2], 16 * (K_PLE // 2 + 1))
                wp = panel[:, K_PLE % 2].rearrange("p (c n) -> p c n", n=D)
                for half in range(2):
                    for i in range(NT):
                        o = take(G_PLE + 8 + 4 * half + i, (ple_mul, 4 * half + i + 1))
                        for c in range(2):
                            mm = nc.tensor.matmul(o, pTs[:, c, i * P:(i + 1) * P],
                                                  wp[:, c, half * 512:(half + 1) * 512], start=(c == 0), stop=(c == 1))
                        pr.mark(mm, pled)

                def second_products(q, r, start=False, stop=False):
                    for g in range(GROUP):
                        tile = layer * NK + q * (2 * GROUP) + (r * GROUP + g + 1)
                        pe.wait_ge(v_lo_ready.sem, tile + v_lo_ready.before)
                        pe.wait_ge(w_lo_ready.sem, tile)
                        for k in range(BANKS):
                            i, half = k // 2, k % 2
                            mm = matmul3(bank(k), [x_[:, g, i * P:(i + 1) * P] for x_ in (w_hi, w_lo)],
                                         [x_[:, g, half * 512:(half + 1) * 512] for x_ in (v_hi, v_lo)],
                                         start and g == 0, stop and g == GROUP - 1)
                        mm.then_inc(y_done.sem, 1)

                pr.need(ple_mul, 8)
                second_products(0, 0, start=True)
                second_products(0, 1)
                with pe.Fori(1, UPANELS // 2 - 1) as q:
                    for r in range(2):
                        second_products(q, r)
                second_products(UPANELS // 2 - 1, 0)
                second_products(UPANELS // 2 - 1, 1, stop=True)

        @block.scalar
        def _(act):
            act.sem_inc(gelu_done.sem, gelu_done.before)
            act.sem_inc(g_kept.sem, g_kept.before)
            for r in range(2):
                act.sem_inc(act_out[r].sem, 16)
                act.sem_inc(g_out[r].sem, 16)
            act.wait_ge(lb_shift.sem, 1)
            nc.scalar.activation(lb_in[:], lb_in[:], ACT.Exp).then_inc(lb_exp.sem, 1)
            act.wait_ge(var_ready.sem, 1)
            nc.scalar.activation(rstd[:], rstd[:], ACT.Sqrt).then_inc(root_ready.sem, 1)
            with act.Fori(0, DEPTH) as layer:
                pr = Program(act, layer)

                def turn(g0, n):
                    for c in range(NC):
                        pr.need(turned, n * NC + c + 1)
                        pr.mark(nc.scalar.copy(hT_hi[:, c, :], bank(g0 + c)), hT_hi_ready)

                def root(n, var):
                    pr.need(var_ready, n)
                    pr.mark(nc.scalar.activation(var, var, ACT.Sqrt), root_ready)

                turn(G_T1, 0)
                pr.need(ff_z, 1)
                pr.link(nc.scalar.activation(ffw[:, 2, :], ffw[:, 1, :], ACT.Exp), act_step)
                pr.mark(nc.scalar.activation(ffw[:, 1, :], ffw[:, 2, :], ACT.Ln, bias=1.0), ff_e)
                for m in range(HH):
                    pr.need(hf_ready, m + 1)
                    pr.mark(nc.scalar.activation(gt[0][:, m, :], gt[0][:, m, :], ACT.Exp), hf_exp)
                for m in range(4):
                    product(pr, 4 + m)
                    pr.mark(nc.scalar.copy(hqT[:, m, :], bank(G_PROJ + 5 + m)), qk_ready)
                pr.need(f_ready, 1)
                nc.scalar.activation(gt[1], gt[1], ACT.Ln)
                pr.mark(nc.scalar.activation(gt[2], gt[2], ACT.Ln), f_log)
                pr.need(b_ready, 1)
                pr.mark(nc.scalar.activation(qe, b, ACT.Exp), b_exp)
                for hd in range(HH):
                    for i in range(NT):
                        last = nc.scalar.activation(kd[:, hd, i * P:(i + 1) * P], b[:, hd, i * P:(i + 1) * P], ACT.Exp,
                                                    scale=-1.0, bias=b[:, hd, (i + 1) * P - 1:(i + 1) * P])
                pr.mark(last, d_exp)
                pr.need(hdec_ready, 1)
                for k, dst in enumerate((fqT, fkT)):
                    for m in range(4):
                        product(pr, 8 + 4 * k + m)
                        pr.mark(nc.scalar.copy(dst[:, m, :], bank(G_PROJ + 9 + 4 * k + m)), qk_ready)
                for i in range(NT):
                    product(pr, 24 + i)
                    pr.mark(nc.scalar.activation(silu[:, i, :], bank(G_PROJ + 25 + i), ACT.Sigmoid), hg_sig)
                for s in range(NS):
                    n = (s % NT + 1) * P
                    pr.need(nmax_ready, s + 1)
                    if s >= 2:
                        pr.need(probs_turned, s - 1)
                        pr.need(fox_out, s - 1)
                    pr.mark(nc.scalar.activation(probs[:, s % 2, 0:n], bank(fox_group(0, s))[:, 0:n], ACT.Exp,
                                                 scale=SCALE, bias=nmax[:, s % 2:s % 2 + 1],
                                                 accum_out=psum_p[:, s % 2:s % 2 + 1]), probs_ready)
                root(1, ssq[:, 0:NT])
                for hd in range(HH):
                    pr.need(lev_ready, hd + 1)
                    pr.mark(nc.scalar.activation(KE, KE, ACT.Exp), lev_exp)
                    for i in range(NT - 1):
                        up = hd * (NT - 1) + i
                        pr.need(kd_turned, up + 1)
                        if up >= 2:
                            pr.need(u_done, up - 1)
                        pr.mark(nc.scalar.copy(kdT[:, up % 2, :], bank(hg_group(3, hd * NT + i))[:, 0:P]), kdT_ready)
                root(2, ssq[:])
                turn(G_T2, 1)
                root(3, rstd[:])
                turn(G_T3, 2)
                for g in range(0, 16, 2):
                    product(pr, 36 + g)
                    pr.mark(nc.scalar.copy(pqT[:, g, :], bank(G_Q + g)), pq_act)

                for g in range(4 * NT):
                    pr.need(key_scored, g + 1)
                    pr.mark(nc.scalar.copy(scores_all[:, g // 4, (g % 4) * 512:(g % 4 + 1) * 512], bank(g)), score_sb)
                def split_u(q, r, g):
                    tile = q * (2 * GROUP) + (r * GROUP + g)
                    slot = (K_U + g // PAIR) % 2
                    if g % PAIR == 0:
                        act.wait_ge(panel_in[slot].sem, layer * panel_in[slot].per_layer +
                                    (q * 32 + 16 * r + 16 * ((K_U + g // PAIR) // 2 + 1)))
                    nc.scalar.copy(u_hi[:, g % 2].rearrange("p c n -> p (c n)"),
                                   panel[:, slot, g % PAIR * D:(g % PAIR + 1) * D]).then_inc(u_hi_ready.sem, 1)

                def activations(q, r, g, ahead=True):
                    tile = q * (2 * GROUP) + (r * GROUP + g + 1)
                    act.wait_ge(a_full.sem, layer * NK + tile)
                    if ahead:
                        if g < 2:
                            split_u(q, r, g + 2)
                        else:
                            split_u(q + r, 1 - r, g - 2)
                    if g % PAIR == 0:
                        act.wait_ge(act_out[g // PAIR].sem,
                                    layer * act_out[0].per_layer + q * 32 + (16 * r + 16))
                    nc.scalar.activation(gact[:, g, :], bank(g), ACT.Gelu).then_inc(gelu_done.sem, 1)
                    if g % PAIR == PAIR - 1:
                        act.wait_ge(gelu_done.sem, layer * NK + tile + gelu_done.before)
                        g0 = g - PAIR + 1
                        act.dma_start(act_dram[bass.ds(layer, 1), bass.ds(q * 2 + r, 1), :, g0 * T:(g + 1) * T]
                                      .rearrange("l n p c -> p (l n c)"),
                                      gact[:, g0:g + 1].rearrange("p g t -> p (g t)")
                                      ).then_inc(act_out[g // PAIR].sem, 16)

                def table_by_token(i):
                    pr.need(table_turned, i + 1)
                    pr.mark(nc.scalar.copy(tabT[:, 0:3, i * P:(i + 1) * P],
                                           bank(4)[:, 0:3 * P].rearrange("p (k t) -> p k t", k=3)), tab_ready)

                def exponentials(i):
                    pr.need(sel_shift, i + 1)
                    pr.mark(nc.scalar.activation(gate_e[:], gate_e[:], ACT.Exp), sel_exp)

                split_u(0, 0, 0)
                split_u(0, 0, 1)
                for seg in range(len(SEGS) - 1):
                    with act.Fori(SEGS[seg], SEGS[seg + 1]) as q:
                        for r in range(2):
                            for g in range(GROUP):
                                activations(q, r, g)
                    if seg < NT:
                        exponentials(seg)
                    if seg > 0:
                        table_by_token(seg - 1)

                def gate_blocks(q, last=False):
                    for r in range(2):
                        block_ = (q - SEGS[-1]) * 2 + r
                        for g in range(GROUP):
                            activations(q, r, g, not (last and r == 1 and g >= 2))
                            if g == 0:
                                act.wait_ge(g_out[r].sem, layer * g_out[r].per_layer + (q - SEGS[-1]) * 16 + 16)
                            for k in range(2 * g, 2 * g + 2):
                                chunk = layer * NG + (q - SEGS[-1]) * 16 + (r * 8 + k)
                                act.wait_ge(g_full.sem, chunk + (1 + g_full.before))
                                nc.scalar.copy(gmat[:, r, :, k * CHUNK:(k + 1) * CHUNK],
                                               bank(4 + k % 4).rearrange("p (c n) -> p n c", c=CHUNK)
                                               ).then_inc(g_kept.sem, 1)
                        act.wait_ge(g_kept.sem, layer * NG + (q - SEGS[-1]) * 16 + ((r + 1) * 8 + g_kept.before))
                        act.dma_start(gate_dram[bass.ds(layer, 1), bass.ds(block_, 1)]
                                      .rearrange("l n p a t -> p (l n a t)"),
                                      gmat[:, r].rearrange("p a t -> p (a t)")).then_inc(g_out[r].sem, 16)

                with act.Fori(SEGS[-1], UPANELS // 2 - 1) as q:
                    gate_blocks(q)
                gate_blocks(UPANELS // 2 - 1, last=True)
                for r in range(2):
                    pr.need(act_out[r], act_out[r].per_layer)
                    pr.need(g_out[r], g_out[r].per_layer)

                def fetch(n, r):
                    act.dma_start(wact[:, r].rearrange("p g t -> p (g t)"),
                                  act_dram[bass.ds(layer, 1), bass.ds(n, 1)].rearrange("l n p c -> p (l n c)")
                                  ).then_inc(act_in[r].sem, 16)
                    act.dma_start(gin[:, r].rearrange("p j g t -> p j (g t)"),
                                  gate_dram[bass.ds(layer, 1), :, :, bass.ds(n * GROUP, GROUP), :]
                                  .rearrange("l j p g t -> p (l j) (g t)")).then_inc(gate_in[r].sem, 16)

                for g in range(8):
                    half, i = g // 4, g % 4
                    product(pr, 52 + g)
                    pr.mark(nc.scalar.activation(acc[:, i, half * 512:(half + 1) * 512], bank(G_PLE + g),
                                                 ACT.Sigmoid), gate_sig)
                for r in range(2):
                    fetch(r, r)

                def split_v(q, r):
                    for g in range(GROUP):
                        slot = (K_V + g // PAIR) % 2
                        if g % PAIR == 0:
                            act.wait_ge(panel_in[slot].sem, layer * panel_in[slot].per_layer +
                                        (q * 32 + 16 * r + 16 * ((K_V + g // PAIR) // 2 + 1)))
                        act.wait_ge(y_done.sem, layer * NK + q * (2 * GROUP) + (r * GROUP + g + 1))
                        nc.scalar.copy(v_hi[:, g], panel[:, slot, g % PAIR * D:(g % PAIR + 1) * D]
                                       ).then_inc(v_hi_ready.sem, 1)
                        if g == 0:
                            act.wait_ge(w_ready.sem, layer * UPANELS + q * 2 + (r + 1))
                        nc.scalar.copy(w_hi[:, g], wact[:, r, g]).then_inc(w_hi_ready.sem, 1)

                with act.Fori(0, UPANELS // 2 - 1) as q:
                    for r in range(2):
                        split_v(q, r)
                        act.wait_ge(w_lo_ready.sem, layer * NK + q * (2 * GROUP) + (r + 1) * GROUP)
                        fetch(q * 2 + (2 + r), r)
                for r in range(2):
                    split_v(UPANELS // 2 - 1, r)
                root(4, rstd[:])

        @block.gpsimd
        def _(pool):
            pool.wait_ge(const_in.sem, 16)
            pool.sem_inc(v_lo_ready.sem, v_lo_ready.before)
            pool.sem_inc(ring_used.sem, ring_used.before)
            with pool.Fori(0, DEPTH) as layer:
                pr = Program(pool, layer)

                def split(src, n, e):
                    at = slice(e % RING * PANEL, e % RING * PANEL + PANEL)
                    pool.wait_ge(ring_used.sem, layer * SPLITS + n)
                    nc.gpsimd.tensor_tensor(ring_hi[:, at], src, zeros, ALU.subtract).then_inc(ring_hi_ready.sem, 1)
                    pool.wait_ge(ring_hi_ready.sem, layer * SPLITS + n)
                    nc.gpsimd.tensor_tensor(ring_lo[:, at], src, ring_hi[:, at].bitcast(F32),
                                            ALU.subtract).then_inc(ring_lo_ready.sem, 1)

                def split_panels(first, end, k0, n0):
                    with pool.Fori(first, end) as j:
                        for r in range(2):
                            slot = panel_in[(k0 + r) % 2]
                            pool.wait_ge(slot.sem, layer * slot.per_layer + j * 16 + 16 * ((k0 + r) // 2 + 1))
                            settle(pool, pool_passed)
                            for c in range(KC):
                                split(panel[:, (k0 + r) % 2, c * PANEL:(c + 1) * PANEL],
                                      j * (2 * KC) + (n0 + r * KC + c + 1), n0 + r * KC + c)

                pr.need(h_ready, 0)
                pr.need(panel_in[0], 16)
                settle(pool, pool_passed)
                for e in range(2):
                    split(panel[:, 0, e * PANEL:(e + 1) * PANEL], e + 1, e)
                split_panels(0, 7, 1, 2)
                pr.need(turned, 2 * NC)
                settle(pool, pool_passed)
                split_panels(7, len(MIXER_PANELS), 1, 2)

                def low_parts(k0, hi_ready, lo_ready, ring, hi_, lo_):
                    with pool.Fori(0, UPANELS // 2) as q:
                        for r in range(2):
                            for g in range(GROUP):
                                raw = panel[:, (k0 + g // PAIR) % 2, g % PAIR * D:(g % PAIR + 1) * D]
                                pool.wait_ge(hi_ready.sem, layer * NK + q * (2 * GROUP) + (r * GROUP + g + 1))
                                at = slice(g % ring * D, (g % ring + 1) * D)
                                nc.gpsimd.tensor_tensor(lo_[:, at], raw, hi_[:, at].bitcast(F32), ALU.subtract
                                                        ).then_inc(lo_ready.sem, 1)

                low_parts(K_U, u_hi_ready, u_lo_ready, PAIR, slim_hi, slim_lo)
                split_panels(0, len(GATE_PANELS), K_GATE, S_GATE)
                low_parts(K_V, v_hi_ready, v_lo_ready, GROUP, wide_hi, wide_lo)

        @block.vector
        def _(dve):
            before = [0]

            def first(ins):
                ins.then_inc(dve_step.sem, 1)
                before[0] += 1
                dve.wait_ge(dve_step.sem, before[0])

            def norm(src, step, root, signal):
                for i in range(NT):
                    for k in range(2):
                        last = nc.vector.bn_stats(stat[:, i, 6 * k:6 * k + 6], src[:, i, k * 512:(k + 1) * 512])
                step(last)
                for i in range(NT):
                    last = nc.vector.bn_aggr(mv[:, i, :], stat[:, i, :])
                step(last)
                root(nc.vector.tensor_scalar(rstd[:], mv[:, :, 1], LN_EPS, None, ALU.add))
                step(nc.vector.reciprocal(rstd[:], rstd[:]))
                for i in range(NT):
                    last = nc.vector.tensor_scalar(h[:, i, :], src[:, i, :], mv[:, i, 0:1], rstd[:, i:i + 1],
                                                   ALU.subtract, ALU.mult)
                step(last)
                for i in range(NT):
                    last = nc.vector.tensor_tensor(h[:, i, :], h[:, i, :], lng[:, 0, :], ALU.mult)
                step(last)
                for i in range(NT):
                    signal(nc.vector.tensor_tensor(h[:, i, :], h[:, i, :], lng[:, 1, :], ALU.add))

            dve.wait_ge(lb_loaded.sem, 16)
            first(nc.vector.tensor_copy(lb_t[:, 0, :], lb_in[:, 0, :]))
            for k in range(1, DEPTH):
                first(nc.vector.tensor_tensor(lb_t[:, 0, :], lb_t[:, 0, :], lb_in[:, k, :], ALU.max))
            for k in range(DEPTH):
                last = nc.vector.tensor_tensor(lb_in[:, k, :], lb_in[:, k, :], lb_t[:, 0, :], ALU.subtract)
            last.then_inc(lb_shift.sem, 1)
            dve.wait_ge(lb_exp.sem, 1)
            first(nc.vector.tensor_copy(lb_t[:, 0, :], lb_in[:, 0, :]))
            for k in range(1, DEPTH):
                first(nc.vector.tensor_tensor(lb_t[:, 0, :], lb_t[:, 0, :], lb_in[:, k, :], ALU.add))
            first(nc.vector.reciprocal(lb_t[:, 1, :], lb_t[:, 0, :]))
            for k in range(DEPTH):
                last = nc.vector.tensor_tensor(lb_in[:, k, :], lb_in[:, k, :], lb_t[:, 1, :], ALU.mult)
            first(last)
            first(nc.vector.tensor_copy(lb_all[:, 0, :], lb_in[:, 0, :]))
            for k in range(1, DEPTH):
                first(nc.vector.tensor_tensor(lb_all[:, k, :], lb_all[:, k - 1, :], lb_in[:, k, :], ALU.add))
            first(nc.vector.tensor_copy(lb_t[:, 0, :], lb_in[:, 0, :]))
            for k in range(DEPTH):
                last = nc.vector.tensor_tensor(lb_all[:, k, :], lb_all[:, k, :], lb_t[:, 0, :], ALU.subtract)
            first(last)
            dve.wait_ge(x_in.sem, 16)
            dve.wait_ge(emb_in.sem, 32)
            def root0(ins):
                ins.then_inc(var_ready.sem, 1)
                dve.wait_ge(root_ready.sem, 1)

            norm(h, first, root0, lambda ins: ins.then_inc(h_ready.sem, 1))
            assert before[0] == dve_step.before, before[0]
            dve.wait_ge(const_in.sem, 16)
            nc.vector.tensor_copy(ident_b, ident).then_inc(casts.sem, 1)
            nc.vector.tensor_copy(cmask_b, cmask).then_inc(casts.sem, 1)

            with dve.Fori(0, DEPTH) as layer:
                pr = Program(dve, layer)

                def step(ins):
                    n = pr.mark(ins, dve_step)
                    pr.need(dve_step, n)
                    settle(dve, dve_passed)

                def root(ins):
                    pr.need(root_ready, pr.mark(ins, var_ready))

                def turn(g0, n):
                    for c in range(NC):
                        pr.need(hT_hi_ready, n * NC + c + 1)
                        pr.mark(nc.vector.tensor_tensor(hT_lo[:, c, :], bank(g0 + c), hT_hi[:, c, :].bitcast(F32),
                                                        ALU.subtract), hT_lo_ready)

                lb_now = lb_all[:, bass.ds(layer, 1), :].rearrange("p a h -> p (a h)")
                nc.vector.tensor_scalar(lb[:, 0, :], lb_now, LB_FLOOR, None, ALU.max)
                step(nc.vector.tensor_scalar(lb[:, 1, :], lb_now, -1.0, 1.0, ALU.mult, ALU.add))
                turn(G_T1, 0)
                pr.need(ring_used, 2)
                pr.need(ff_in, 16)
                step(nc.vector.tensor_scalar(ffw[:, 0, :], bank(G_PROJ)[0:FH, :], ff_bias[:], None, ALU.add))
                pr.mark(nc.vector.scalar_tensor_tensor(out=ffw[:, 1, :], in0=ffw[:, 0, :], scalar=-1.0, in1=ffw[:, 0, :],
                                                       op0=ALU.mult, op1=ALU.min), ff_z)
                for m in range(HH):
                    product(pr, m)
                    pr.mark(nc.vector.tensor_scalar(gt[0][:, m, :], bank(G_PROJ + 1 + m), 80.0, None, ALU.min),
                            hf_ready)
                pr.need(ff_e, 1)
                step(nc.vector.scalar_tensor_tensor(out=ffw[:, 2, :], in0=ffw[:, 0, :], scalar=0.0, in1=ffw[:, 1, :],
                                                    op0=ALU.min, op1=ALU.subtract))
                step(nc.vector.memset(ffw[:, 1, :], 1.0))
                step(nc.vector.tensor_tensor_scan(out=ffw[:, 0, :], data0=ffw[:, 1, :], data1=ffw[:, 2, :],
                                                  initial=0.0, op0=ALU.mult, op1=ALU.add))
                pr.mark(nc.vector.tensor_scalar(negc[:], ffw[:, 0, :], -1.0 / SCALE, None, ALU.mult), negc_ready)
                pr.need(hf_exp, HH)
                step(nc.vector.tensor_scalar(kT, gt[0], 1.0, None, ALU.add))
                step(nc.vector.reciprocal(kT, kT))
                for m in range(HH):
                    last = nc.vector.tensor_scalar(kT[:, m, :], kT[:, m, :], lb[:, 1, m:m + 1], None, ALU.mult)
                step(last)
                step(nc.vector.tensor_tensor(gt[0], gt[0], kT, ALU.mult))
                for m in range(HH):
                    last = nc.vector.tensor_scalar(gt[0][:, m, :], gt[0][:, m, :], lb[:, 0, m:m + 1], None, ALU.add)
                step(last)
                nc.vector.tensor_scalar(gt[1], gt[0], 1.0 / LN_SPLIT, None, ALU.max)
                pr.mark(nc.vector.tensor_scalar(gt[2], gt[0], LN_SPLIT, 1.0, ALU.mult, ALU.min), f_ready)
                pr.need(f_log, 1)
                step(nc.vector.tensor_tensor(gt[1], gt[1], gt[2], ALU.add))
                for m in range(HH):
                    last = nc.vector.tensor_tensor_scan(out=b[:, m, :], data0=reset, data1=gt[1][:, m, :],
                                                        initial=0.0, op0=ALU.mult, op1=ALU.add)
                pr.mark(last, b_ready)
                pr.need(b_exp, 1)
                step(nc.vector.tensor_copy(eblast[:].rearrange("p (h i) -> p h i", h=HH),
                                           qe.rearrange("p h (i t) -> p h i t", t=P)[:, :, :, P - 1]))
                pr.need(qk_ready, 4)
                nc.vector.tensor_tensor(qe, qe, hqT, ALU.mult)
                pr.need(d_exp, 1)
                pr.mark(nc.vector.tensor_tensor(kd, kd, kT, ALU.mult), hdec_ready)
                pr.need(hdec_ready, 1)
                for k, dst in enumerate((fv, hi)):
                    for i in range(NT):
                        product(pr, 16 + 4 * k + i)
                        pr.mark(nc.vector.tensor_copy(dst[:, i, :], bank(G_PROJ + 17 + 4 * k + i)), v_ready)
                for i in range(NT):
                    pr.need(hg_sig, i + 1)
                    pr.mark(nc.vector.tensor_tensor(silu[:, i, :], silu[:, i, :], bank(G_PROJ + 25 + i), ALU.mult),
                            silu_ready)

                for st in range(NS + 2):
                    if st < NS:
                        n = (st % NT + 1) * P
                        pr.need(scored, st + 1)
                        if st >= 2:
                            pr.need(probs_ready, st - 1)
                        if st >= 1:
                            pr.need(nmax_ready, st)
                        step(nc.vector.tensor_reduce(rinv[:, 1:2], bank(fox_group(0, st))[:, 0:n], AX_X, ALU.max))
                        pr.mark(nc.vector.tensor_scalar(nmax[:, st % 2:st % 2 + 1], rinv[:, 1:2], -SCALE, None,
                                                        ALU.mult), nmax_ready)
                    if 0 <= st - 1 < NS:
                        s = st - 1
                        n = (s % NT + 1) * P
                        pr.need(probs_turned, s + 1)
                        if s >= 2:
                            pr.need(pv_done, s - 1)
                        pr.mark(nc.vector.tensor_copy(probsT[:, s % 2, 0:n], bank(fox_group(1, s))[:, 0:n]),
                                probsT_ready)
                    if 0 <= st - 2:
                        s = st - 2
                        hd, i = s // NT, s % NT
                        pr.need(probs_ready, s + 1)
                        if s >= 1:
                            pr.need(fox_out, s)
                        step(nc.vector.reciprocal(rinv[:, 0:1], psum_p[:, s % 2:s % 2 + 1]))
                        pr.need(pv_done, s + 1)
                        pr.mark(nc.vector.tensor_scalar(mix[:, i, hd * FD:(hd + 1) * FD],
                                                        bank(fox_group(2, s))[:, 0:FD], rinv[:, 0:1], None, ALU.mult),
                                fox_out)

                sq = gt[0]
                pr.need(pv_done, NS)
                pr.need(fox_out, NS)
                step(nc.vector.tensor_tensor(sq, mix[:, :, 0:FW], mix[:, :, 0:FW], ALU.mult))
                step(nc.vector.tensor_reduce(ssq[:, 0:NT], sq, AX_X, ALU.add))
                root(nc.vector.tensor_scalar(ssq[:, 0:NT], ssq[:, 0:NT], 1.0 / FW, RMS_EPS, ALU.mult, ALU.add))
                step(nc.vector.reciprocal(ssq[:, 0:NT], ssq[:, 0:NT]))
                pr.need(gains_in, 32)
                for i in range(NT):
                    last = nc.vector.scalar_tensor_tensor(out=mix[:, i, 0:FW], in0=mix[:, i, 0:FW],
                                                          scalar=ssq[:, i:i + 1], in1=ng[:, 0, :],
                                                          op0=ALU.mult, op1=ALU.mult)
                pr.mark(last, mix_ready)

                for hd in range(HH):
                    if hd > 0:
                        pr.need(a_done, 2 * NT * hd)
                    for lev in range(1, LEVELS):
                        m = 2 ** (lev - 1)
                        bb = b[:, hd, :].rearrange("p (g a m) -> p g a m", a=2, m=m)
                        dd = KE[:, lev - 1, :].rearrange("p (g a m) -> p g a m", a=2, m=m)
                        mid = bb[:, :, 0, m - 1:m].to_broadcast([P, T // (2 * m), m])
                        nc.vector.tensor_tensor(dd[:, :, 0, :], mid, bb[:, :, 0, :], ALU.subtract)
                        last = nc.vector.tensor_tensor(dd[:, :, 1, :], bb[:, :, 1, :], mid, ALU.subtract)
                    pr.mark(last, lev_ready)
                    pr.need(lev_exp, hd + 1)

                    def over_levels(ap):
                        return ap.rearrange("p (o t) -> p o t", o=1).to_broadcast([P, LEVELS - 1, T])

                    step(nc.vector.tensor_tensor(QE, KE, over_levels(hqT[:, hd, :]), ALU.mult))
                    pr.mark(nc.vector.tensor_tensor(KE, KE, over_levels(kT[:, hd, :]), ALU.mult), lev_mul)
                    for i in range(NT):
                        j = hd * NT + i
                        if j >= 2:
                            pr.need(o_done, j - 1)
                        for half in range(2):
                            pr.need(a_done, 2 * j + half + 1)
                            pr.mark(nc.vector.tensor_tensor(
                                AT[:, j % 2, 4 * half:4 * half + 4, :].rearrange("p l n -> p (l n)"),
                                bank(hg_group(half, j)), level_mask[:, half * 512:(half + 1) * 512], ALU.mult),
                                at_ready)
                        pr.need(o_done, j + 1)
                        pr.mark(nc.vector.tensor_copy(mix[:, i, FW + hd * HD:FW + (hd + 1) * HD],
                                                      bank(hg_group(2, j))[:, 0:HD]), o_out)
                        if i < NT - 1:
                            up = hd * (NT - 1) + i
                            pr.need(u_done, up + 1)
                            upd = bank(hg_group(4, j))[:, 0:HD]
                            if i == 0:
                                ins = nc.vector.tensor_copy(state[:, hd, :], upd)
                            else:
                                pr.need(state_ready, up)
                                ins = nc.vector.scalar_tensor_tensor(out=state[:, hd, :], in0=state[:, hd, :],
                                                                     scalar=eblast[:, j:j + 1], in1=upd,
                                                                     op0=ALU.mult, op1=ALU.add)
                            pr.mark(ins, state_ready)
                pr.need(o_out, HH * NT)
                pr.need(mix_ready, 1)
                o_hg = mix[:, :, FW:2 * FW]
                step(nc.vector.tensor_tensor(sq, o_hg, o_hg, ALU.mult))
                step(nc.vector.tensor_reduce(ssq[:], sq.rearrange("p i (h n) -> p (i h) n", n=HD), AX_X, ALU.add))
                root(nc.vector.tensor_scalar(ssq[:], ssq[:], 1.0 / HD, RMS_EPS, ALU.mult, ALU.add))
                step(nc.vector.reciprocal(ssq[:], ssq[:]))
                for i in range(NT):
                    for hd in range(HH):
                        cols = slice(FW + hd * HD, FW + (hd + 1) * HD)
                        last = nc.vector.scalar_tensor_tensor(
                            out=mix[:, i, cols], in0=mix[:, i, cols], scalar=ssq[:, i * HH + hd:i * HH + hd + 1],
                            in1=ng[:, 1, hd * HD:(hd + 1) * HD], op0=ALU.mult, op1=ALU.mult)
                step(last)
                pr.mark(nc.vector.tensor_tensor(o_hg, o_hg, silu, ALU.mult), mix_ready)

                turn(G_T2, 1)
                for g in range(8):
                    half, i = g // 4, g % 4
                    product(pr, 28 + g)
                    hh = h[:, i, half * 512:(half + 1) * 512]
                    pr.mark(nc.vector.scalar_tensor_tensor(out=hh, in0=hh, scalar=ALPHA, in1=bank(G_OUT + g),
                                                           op0=ALU.mult, op1=ALU.add), pre1)
                pr.need(pre1, 8)
                pr.need(ln1_in, 32)
                norm(h, step, root, lambda ins: pr.mark(ins, h_ready))
                pr.need(h_ready, NT)

                turn(G_T3, 2)
                for g in range(1, 16, 2):
                    product(pr, 36 + g)
                    pr.mark(nc.vector.tensor_copy(pqT[:, g, :], bank(G_Q + g)), pq_dve)
                with dve.Fori(0, NT) as i:
                    tile = layer * NT + i
                    TILE_STEPS = 43
                    at_entry = dve_step.made
                    count = [0]

                    def tstep(ins):
                        ins.then_inc(dve_step.sem, 1)
                        count[0] += 1
                        dve.wait_ge(dve_step.sem, layer * dve_step.per_layer + i * TILE_STEPS +
                                    (dve_step.before + at_entry + count[0]))
                        settle(dve, dve_passed)

                    def top16(values, keep, keep_u, n):
                        for a in range(n):
                            last = nc.vector.max(keep[:, a, 0:8], values[:, a, :])
                        tstep(last)
                        for a in range(n):
                            last = nc.vector.max_index(keep_u[:, a, 0:8], keep[:, a, 0:8], values[:, a, :])
                        tstep(last)
                        for a in range(n):
                            last = nc.vector.match_replace(values[:, a, :], keep[:, a, 0:8], values[:, a, :], -3e38)
                        tstep(last)
                        for a in range(n):
                            last = nc.vector.max(keep[:, a, 8:16], values[:, a, :])
                        tstep(last)
                        for a in range(n):
                            last = nc.vector.max_index(keep_u[:, a, 8:16], keep[:, a, 8:16], values[:, a, :])
                        tstep(last)

                    dve.wait_ge(score_sb.sem, layer * score_sb.per_layer + score_sb.per_layer)
                    settle(dve, dve_passed)
                    tstep(nc.vector.tensor_copy(score.rearrange("p a n -> p (a n)"),
                                                scores_all[:, bass.ds(i, 1), :].rearrange("p o n -> p (o n)")))
                    top16(score, top, top_u, 2 * PH)
                    tstep(nc.vector.tensor_copy(top_i, top_u))
                    ti = top_i.rearrange("p (h a) k -> p h a k", a=2)
                    ts = top.rearrange("p (h a) k -> p h a k", a=2)
                    tstep(nc.vector.tensor_scalar(ti[:, :, 0, :], ti[:, :, 0, :], float(NK), None, ALU.mult))
                    off = 0
                    for a in range(8):
                        nb = STAIR[a]
                        for src, dst in ((ts, cand_s), (ti, cand_i)):
                            nc.vector.tensor_tensor(dst[:, :, off:off + nb], src[:, :, 1, 0:nb],
                                                    src[:, :, 0, a:a + 1].to_broadcast([P, PH, nb]), ALU.add)
                        off += nb
                    for src, dst in ((ts, cand_s), (ti, cand_i)):
                        last = nc.vector.tensor_tensor(dst[:, :, off:CAND], src[:, :, 0, 8:TOPK],
                                                       src[:, :, 1, 0:1].to_broadcast([P, PH, 8]), ALU.add)
                    tstep(last)
                    top16(cand_s, sel_s, sel_u, PH)
                    nc.vector.tensor_copy(sel_p[:], sel_u[:]).then_inc(routed.sem, 1)
                    dve.wait_ge(routed.sem, tile + 1)
                    nc.vector.tensor_tensor(gate_e[:], sel_s[:], sel_s[:, :, 0:1].to_broadcast([P, PH, TOPK]),
                                            ALU.subtract).then_inc(sel_shift.sem, 1)
                    for a in range(PH):
                        tstep(nc.vector.tensor_tensor(
                            pick, iota[:, 0:CAND].rearrange("p (o c) -> p o c", o=1).to_broadcast([P, TOPK, CAND]),
                            sel_p[:, a, :].rearrange("p (k o) -> p k o", o=1).to_broadcast([P, TOPK, CAND]),
                            ALU.is_equal))
                        tstep(nc.vector.tensor_tensor(
                            pick, pick, cand_i[:, a:a + 1, :].to_broadcast([P, TOPK, CAND]), ALU.mult))
                        tstep(nc.vector.tensor_reduce(expert[:, a * TOPK:(a + 1) * TOPK], pick, AX_X, ALU.add))
                    tstep(nc.vector.tensor_copy(exp_u[:, 0, :], expert[:]))
                    tstep(nc.vector.tensor_scalar(exp_u[:, 1, :], exp_u[:, 0, :], NK - 1, None, ALU.bitwise_and))
                    tstep(nc.vector.tensor_scalar(exp_u[:, 0, :], exp_u[:, 0, :], 7, None,
                                                  ALU.logical_shift_right))
                    dve.wait_ge(table_turned.sem, tile + 1)
                    nc.vector.tensor_copy(table[:, 0:2, :], exp_u[:])
                    dve.wait_ge(sel_exp.sem, tile + 1)
                    tstep(nc.vector.tensor_reduce(gsum[:, 0, :], gate_e[:], AX_X, ALU.add))
                    tstep(nc.vector.reciprocal(gsum[:, 1, :], gsum[:, 0, :]))
                    nc.vector.tensor_tensor(gate, gate_e[:], gsum[:, 1, :].rearrange("p (h o) -> p h o", o=1)
                                            .to_broadcast([P, PH, TOPK]), ALU.mult).then_inc(table_ready.sem, 1)
                    dve.wait_ge(table_ready.sem, tile + 1)
                    settle(dve, dve_passed)
                    assert count[0] == TILE_STEPS, count[0]
                dve_step.made += NT * TILE_STEPS

                pr.need(tab_ready, NT)
                settle(dve, dve_passed)
                step(nc.vector.tensor_copy(tabT[:, 3, :].bitcast(F32R), tabT[:, 2, :]))
                step(nc.vector.tensor_tensor(tabT[:, 2, :], tabT[:, 2, :], tabT[:, 3, :], ALU.subtract))
                with dve.Fori(0, NG // 2) as q:
                    for r in range(2):
                        chunk = layer * NG + q * 2 + r
                        dve.wait_ge(g_full.sem, chunk + 1)
                        nc.vector.tensor_copy(hot_s[:, r], tabT[:, :, bass.ds((q * 2 + r) * CHUNK, CHUNK)]
                                              ).then_inc(hot_step.sem, 1)
                        dve.wait_ge(hot_step.sem, chunk + 1)
                        for c in range(CHUNK):
                            nc.vector.tensor_scalar(hot1[:, r, c, :], iota, hot_s[:, r, 0, c:c + 1], None,
                                                    ALU.is_equal)
                            for k, hot2 in ((2, hot2_lo), (3, hot2_hi)):
                                last = nc.vector.tensor_scalar(hot2[:, r, c, :], iota, hot_s[:, r, 1, c:c + 1],
                                                               hot_s[:, r, k, c:c + 1], ALU.is_equal, ALU.mult)
                        last.then_inc(hot_ready.sem, 1)

                for g in range(8):
                    half, i = g // 4, g % 4
                    aa = acc[:, i, half * 512:(half + 1) * 512]
                    pr.need(gate_sig, g + 1)
                    pr.need(pled, g + 1)
                    pr.mark(nc.vector.tensor_tensor(aa, aa, bank(G_PLE + 8 + g), ALU.mult), ple_mul)
                    pr.need(ple_mul, g + 1)
                    pr.mark(nc.vector.scalar_tensor_tensor(out=aa, in0=h[:, i, half * 512:(half + 1) * 512],
                                                           scalar=ALPHA, in1=aa, op0=ALU.mult, op1=ALU.add), acc_init)
                pr.need(acc_init, 8)


                def weights(q, r):
                    dve.wait_ge(act_in[r].sem, layer * act_in[r].per_layer + (q * 16 + 16))
                    dve.wait_ge(gate_in[r].sem, layer * gate_in[r].per_layer + (q * 16 + 16))
                    ww = wact[:, r].rearrange("p g (j t) -> p g j t", t=TB)
                    nc.vector.tensor_tensor(ww, ww, gin[:, r].rearrange("p j g t -> p g j t"),
                                            ALU.mult).then_inc(w_ready.sem, 1)

                def low_weights(q, r):
                    for g in range(GROUP):
                        dve.wait_ge(w_hi_ready.sem, layer * NK + q * (2 * GROUP) + (r * GROUP + g + 1))
                        nc.vector.tensor_tensor(w_lo[:, g], wact[:, r, g], w_hi[:, g].bitcast(F32),
                                                ALU.subtract).then_inc(w_lo_ready.sem, 1)

                weights(0, 0)
                with dve.Fori(0, UPANELS // 2 - 1) as q:
                    weights(q, 1)
                    low_weights(q, 0)
                    weights(q + 1, 0)
                    low_weights(q, 1)
                weights(UPANELS // 2 - 1, 1)
                low_weights(UPANELS // 2 - 1, 0)
                low_weights(UPANELS // 2 - 1, 1)
                pr.need(y_done, NK)
                for k in range(BANKS):
                    i, half = k // 2, k % 2
                    aa = acc[:, i, half * 512:(half + 1) * 512]
                    pr.mark(nc.vector.tensor_tensor(aa, aa, bank(k), ALU.add), y_added)
                pr.need(y_added, BANKS)
                pr.need(ln2_in, 32)
                norm(acc, step, root, lambda ins: pr.mark(ins, h_ready))
                pr.need(h_ready, 2 * NT)

            dve.wait_ge(h_ready.sem, NT + DEPTH * 2 * NT)

        @block.sync
        def _(sp):
            sp.wait_ge(h_ready.sem, NT + DEPTH * 2 * NT)
            sp.dma_start(out.rearrange("(i p) d -> p i d", p=P), h[:]).then_inc(out_sent.sem, 16)
            sp.wait_ge(out_sent.sem, 16)

        for name, s in names:
            if s.made and s.made != s.per_layer:
                raise AssertionError(f"{name}: {s.made} a layer, not {s.per_layer}")


def constants():
    import numpy as np
    r = np.arange(P)
    ident = np.eye(P)
    causal = np.where(r[None, :] <= r[:, None], 0.0, MASK)
    iota = np.tile(np.arange(P), (P, 1))
    s, t = r[:, None], r[None, :]
    levels = [s == t]
    for lev in range(1, LEVELS):
        m = 2 ** (lev - 1)
        levels.append((s // (2 * m) == t // (2 * m)) & (s % (2 * m) < m) & (t % (2 * m) >= m))
    starts = np.tile((np.arange(T) % P != 0), (P, 1))
    return np.ascontiguousarray(np.concatenate([ident, causal, iota] + levels + [starts], axis=1).astype(np.float32))


def kernel(**inputs):
    import numpy as np
    import concourse.bacc as bacc
    from concourse.bass_utils import run_bass_kernel_spmd as run

    a = {k: np.asarray(val) for k, val in inputs.items()}
    depth = a["w_in"].shape[0]
    arrays = {
        "x": a["x"][0],
        "pT": a["p"][:, 0].transpose(0, 2, 1),
        "emb_g": a["emb_ln_g"], "emb_b": a["emb_ln_b"],
        "w_in": a["w_in"], "fox_fb": a["fox_fb"], "fox_g": a["fox_norm_g"],
        "lbl": a["hg_lb_logits"].reshape(depth, HH, HD).transpose(2, 0, 1),
        "hg_g": a["hg_norm_g"], "w_out": a["w_out"], "ln1_g": a["ln1_g"], "ln1_b": a["ln1_b"],
        "wq": a["peer_wq"],
        "keysT": a["peer_keys"].reshape(depth, 2 * PH, NK, P).transpose(0, 3, 1, 2),
        "u": a["peer_u"].reshape(depth, NK, 2 * UPANELS, PAIR, NC, P).transpose(0, 2, 5, 3, 4, 1)
        .reshape(depth, 2 * UPANELS, P, PAIR * NC * NK),
        "v": a["peer_v"].reshape(depth, NK, 2 * UPANELS, PAIR, D).transpose(0, 2, 1, 3, 4)
        .reshape(depth, 2 * UPANELS, NK, PAIR * D),
        "gate_w": a["ple_gate_w"], "ple_w": a["ple_w"],
        "ln2_g": a["ln2_g"], "ln2_b": a["ln2_b"], "consts": constants(),
    }
    nc = bacc.Bacc("TRN2", target_bir_lowering=False, num_devices=1)
    nc.disable_value_cache = True
    feed, args = {}, {}
    for name, val in arrays.items():
        val = np.ascontiguousarray(val)
        feed[f"in_{name}"] = val
        args[name] = nc.dram_tensor(f"in_{name}", val.shape, mybir.dt.from_np(val.dtype), kind="ExternalInput").ap()
    args["out"] = nc.dram_tensor("out_h", (T, D), F32, kind="ExternalOutput").ap()
    build(nc, **args)
    r = run(nc, [feed], core_ids=[0])
    return r.results[0]["out_h"].reshape(1, T, D)
```
